# Optimizing a Trainium2 kernel written in Bass

```python
import math
import jax, jax.numpy as jnp
from jax import lax
import numpy as np

D_MODEL = 1024
BATCH = 1
SEQ = 1024
DEPTH = 2
DEC_BATCH = 8
DEC_SEQ = 8
PAST_LEN = 1024
PAGE_SIZE = 128

HEAD_DIM = 64
N_EVEN = (DEPTH + 1) // 2
N_ODD = DEPTH // 2
NSA_HEADS = 8
NSA_KV = 2
NSA_REP = NSA_HEADS // NSA_KV
CMP_STRIDE = 16
CMP_BLOCK = 2 * CMP_STRIDE
CMP_HIDDEN = 2 * HEAD_DIM
SEL_BLOCK = 64
N_SELECT = 16
WINDOW = 512
Q_BLOCK = 128
ROPE_DIM = HEAD_DIM // 4
ROPE_THETA = 500000.0
RWKV_HEADS = 8
RWKV_WIDTH = RWKV_HEADS * HEAD_DIM
LORA_W = 64
LORA_A = 64
LORA_G = 128
RWKV_GN_EPS = 64e-5
GLA_HEADS = 4
GLA_DK = D_MODEL // 2 // GLA_HEADS
GLA_DV = D_MODEL // GLA_HEADS
GLA_RANK = 16
GLA_TAU = 16.0
GLA_CHUNK = 64
D_FF = ((8 * D_MODEL // 3 + 255) // 256) * 256
NSA_Q = NSA_HEADS * HEAD_DIM
NSA_KVW = 3 * 2 * NSA_KV * HEAD_DIM
NSA_IN = NSA_Q + NSA_KVW + 3 * NSA_HEADS
RWKV_IN = 3 * RWKV_WIDTH + LORA_W + LORA_A + LORA_G
EVEN_IN = NSA_IN + RWKV_IN
MIX_WIDTH = NSA_Q + RWKV_WIDTH
GLA_KW = GLA_HEADS * GLA_DK
GLA_VW = GLA_HEADS * GLA_DV
ODD_IN = 2 * GLA_KW + GLA_VW + GLA_RANK + GLA_VW

kernel_name = 'hybrid_nsa_rwkv7_gla_decode_step'

def rmsnorm(x, g, eps=1e-6):
    xf = x.astype(jnp.float32)
    y = xf * lax.rsqrt(jnp.mean(xf * xf, axis=-1, keepdims=True) + eps)
    return (y * g.astype(jnp.float32)).astype(x.dtype)

def rope(x, pos):
    half = ROPE_DIM // 2
    inv = ROPE_THETA ** (-jnp.arange(half, dtype=jnp.float32) / half)
    ang = pos.astype(jnp.float32)[:, None] * inv[None, :]
    shp = (pos.shape[0],) + (1,) * (x.ndim - 3) + (half,)
    cos, sin = jnp.cos(ang).reshape(shp), jnp.sin(ang).reshape(shp)
    xr = x[..., :ROPE_DIM].astype(jnp.float32)
    x1, x2 = xr[..., :half], xr[..., half:]
    rot = jnp.concatenate([x1 * cos - x2 * sin, x2 * cos + x1 * sin], axis=-1)
    return jnp.concatenate([rot.astype(x.dtype), x[..., ROPE_DIM:]], axis=-1)

def masked_softmax(s, mask):
    p = jax.nn.softmax(jnp.where(mask, s, -1e30), axis=-1)
    return jnp.where(mask, p, 0.0)

def swiglu(x, wg, wu, wd):
    return (jax.nn.silu(x @ wg) * (x @ wu)) @ wd

def nsa_project(h, pos, qn, kn):
    B, T = h.shape[:2]
    q = h[..., :NSA_Q].reshape(B, T, NSA_HEADS, HEAD_DIM)
    kv = h[..., NSA_Q:NSA_Q + NSA_KVW].reshape(B, T, 3, 2, NSA_KV, HEAD_DIM)
    gates = jax.nn.sigmoid(h[..., NSA_Q + NSA_KVW:NSA_IN].astype(jnp.float32)).reshape(B, T, NSA_HEADS, 3)
    q = rope(rmsnorm(q, qn), pos)
    k = rope(rmsnorm(kv[:, :, :, 0], kn[:, None, :]), pos)
    kv = jnp.stack([k, kv[:, :, :, 1]], axis=3)
    rows = kv[:, :, :2].reshape(B, T, 4, NSA_KV, HEAD_DIM)
    win = kv[:, :, 2]
    return q, gates, rows, win

def compress(k, w1, w2, pe):
    B, L = k.shape[:2]
    n_chunks = L // CMP_STRIDE
    c = k[:, :n_chunks * CMP_STRIDE].reshape(B, n_chunks, CMP_STRIDE, NSA_KV, HEAD_DIM)
    h = (jnp.einsum('bnlgd,ldh->bngh', c[:, :-1], w1[:CMP_STRIDE])
         + jnp.einsum('bnlgd,ldh->bngh', c[:, 1:], w1[CMP_STRIDE:])
         + jnp.einsum('ld,ldh->h', pe, w1))
    return jnp.einsum('bngh,hd->bngd', jax.nn.gelu(h), w2)

def nsa_keys(rows, cw1, cw2, cpe):
    B, L = rows.shape[:2]
    kc = compress(rows[:, :, 0], cw1[0], cw2[0], cpe[0])
    vc = compress(rows[:, :, 1], cw1[1], cw2[1], cpe[1])
    n_cmp = kc.shape[1]
    cmp_start = jnp.arange(n_cmp, dtype=jnp.int32) * CMP_STRIDE
    cmp_end = cmp_start + CMP_BLOCK - 1
    n_sel = -(-L // SEL_BLOCK)
    sel_start = jnp.arange(n_sel, dtype=jnp.int32) * SEL_BLOCK
    sel_map = ((cmp_start[:, None] <= sel_start[None, :] + SEL_BLOCK - 1)
               & (cmp_end[:, None] >= sel_start[None, :])).astype(jnp.float32)
    slc = jnp.pad(rows[:, :, 2:4], ((0, 0), (0, n_sel * SEL_BLOCK - L), (0, 0), (0, 0), (0, 0)))
    slc = slc.reshape(B, n_sel, SEL_BLOCK, 2, NSA_KV, HEAD_DIM).transpose(3, 0, 4, 1, 2, 5)
    return kc, vc, cmp_end, sel_map, slc[0], slc[1]

def nsa_block(q, gates, q_pos, kc, vc, cmp_end, sel_map, ksb, vsb, win, w_pos):
    f32 = jnp.float32
    B, QB = q.shape[:2]
    qg = q.reshape(B, QB, NSA_KV, NSA_REP, HEAD_DIM).astype(f32) * (HEAD_DIM ** -0.5)
    tq = q_pos[:, None]
    s = jnp.einsum('bqgrd,bngd->bqgrn', qg, kc.astype(f32))
    p = masked_softmax(s, (cmp_end[None, :] <= tq)[None, :, None, None, :])
    o_cmp = jnp.einsum('bqgrn,bngd->bqgrd', p, vc.astype(f32))
    imp = jnp.einsum('bqgrn,nj->bqgj', p, sel_map)
    n_sel = sel_map.shape[1]
    blk = jnp.arange(n_sel, dtype=jnp.int32)[None, :]
    cur = tq // SEL_BLOCK
    forced = (blk == 0) | (blk == cur) | (blk == cur - 1)
    valid = blk * SEL_BLOCK <= tq
    imp = jnp.where(valid[None, :, None, :], jnp.where(forced[None, :, None, :], 1e30, imp), -1e30)
    n_top = min(N_SELECT, n_sel)
    _, idx = lax.top_k(imp, n_top)
    bi = jnp.arange(B)[:, None, None, None]
    gi = jnp.arange(NSA_KV)[None, None, :, None]
    nk = n_top * SEL_BLOCK
    k_sel = ksb[bi, gi, idx].reshape(B, QB, NSA_KV, nk, HEAD_DIM).astype(f32)
    v_sel = vsb[bi, gi, idx].reshape(B, QB, NSA_KV, nk, HEAD_DIM).astype(f32)
    k_pos = (idx[..., None] * SEL_BLOCK + jnp.arange(SEL_BLOCK, dtype=jnp.int32)).reshape(B, QB, NSA_KV, nk)
    s = jnp.einsum('bqgrd,bqgkd->bqgrk', qg, k_sel)
    p = masked_softmax(s, (k_pos <= q_pos[None, :, None, None])[:, :, :, None, :])
    o_slc = jnp.einsum('bqgrk,bqgkd->bqgrd', p, v_sel)
    s = jnp.einsum('bqgrd,bkgd->bqgrk', qg, win[:, :, 0].astype(f32))
    wp = w_pos[None, :]
    m = (wp <= tq) & (wp > tq - WINDOW) & (wp >= 0)
    p = masked_softmax(s, m[None, :, None, None, :])
    o_win = jnp.einsum('bqgrk,bkgd->bqgrd', p, win[:, :, 1].astype(f32))
    g = gates.reshape(B, QB, NSA_KV, NSA_REP, 3)
    o = g[..., 0:1] * o_cmp + g[..., 1:2] * o_slc + g[..., 2:3] * o_win
    return o.reshape(B, QB, NSA_Q)

def nsa_prompt(q, gates, rows, win, cw1, cw2, cpe):
    B, T = q.shape[:2]
    kc, vc, cmp_end, sel_map, ksb, vsb = nsa_keys(rows, cw1, cw2, cpe)
    win_pad = jnp.pad(win, ((0, 0), (WINDOW, 0), (0, 0), (0, 0), (0, 0)))
    nb = T // Q_BLOCK
    qb = q.reshape(B, nb, Q_BLOCK, NSA_HEADS, HEAD_DIM).swapaxes(0, 1)
    gb = gates.reshape(B, nb, Q_BLOCK, NSA_HEADS, 3).swapaxes(0, 1)

    def body(args):
        i, q_i, g_i = args
        s0 = i * Q_BLOCK
        w_i = lax.dynamic_slice_in_dim(win_pad, s0, WINDOW + Q_BLOCK, axis=1)
        q_pos = s0 + jnp.arange(Q_BLOCK, dtype=jnp.int32)
        w_pos = s0 - WINDOW + jnp.arange(WINDOW + Q_BLOCK, dtype=jnp.int32)
        return nsa_block(q_i, g_i, q_pos, kc, vc, cmp_end, sel_map, ksb, vsb, w_i, w_pos)

    o = lax.map(body, (jnp.arange(nb, dtype=jnp.int32), qb, gb))
    return o.swapaxes(0, 1).reshape(B, T, NSA_Q)

def rwkv_scan(r, w, k, v, kk, a, S0):
    def step(S, inp):
        r_t, w_t, k_t, v_t, kk_t, a_t = inp
        sa = jnp.einsum('bhvk,bhk->bhv', S, -kk_t)
        S = (S * w_t[:, :, None, :] + sa[..., None] * (kk_t * a_t)[:, :, None, :]
             + v_t[..., None] * k_t[:, :, None, :])
        return S, jnp.einsum('bhvk,bhk->bhv', S, r_t)
    xs = tuple(jnp.moveaxis(t, 1, 0) for t in (r, w, k, v, kk, a))
    S, ys = lax.scan(step, S0, xs)
    return jnp.moveaxis(ys, 0, 1), S

def rwkv_mix(p, prev, S0, mu, w0, wB, a0, aB, gB, k_k, k_a, r_k, ln_w, ln_b):
    f32 = jnp.float32
    B, T = p.shape[:2]
    W = RWKV_WIDTH
    p = p.astype(f32)
    p_prev = jnp.concatenate([prev.astype(f32)[:, None], p[:, :-1]], axis=1)
    ps = p + mu * (p_prev - p)
    r, k, v = ps[..., :W], ps[..., W:2 * W], ps[..., 2 * W:3 * W]
    o = 3 * W
    xw, xa, xg = ps[..., o:o + LORA_W], ps[..., o + LORA_W:o + LORA_W + LORA_A], ps[..., o + LORA_W + LORA_A:]
    z = w0 + jnp.tanh(xw) @ wB
    w = jnp.exp(-jnp.exp(-jax.nn.softplus(-z) - 0.5))
    a = jax.nn.sigmoid(a0 + xa @ aB)
    g = jax.nn.sigmoid(xg) @ gB
    heads = lambda t: t.reshape(B, T, RWKV_HEADS, HEAD_DIM)
    kk = heads(k * k_k)
    kk = kk * lax.rsqrt(jnp.maximum(jnp.sum(kk * kk, axis=-1, keepdims=True), 1e-24))
    k = heads(k * (1.0 + (a - 1.0) * k_a))
    r, v, w, a = heads(r), heads(v), heads(w), heads(a)
    y, S = rwkv_scan(r, w, k, v, kk, a, S0.astype(f32))
    mean = jnp.mean(y, axis=-1, keepdims=True)
    var = jnp.mean(jnp.square(y - mean), axis=-1, keepdims=True)
    y = ((y - mean) * lax.rsqrt(var + RWKV_GN_EPS)).reshape(B, T, W) * ln_w + ln_b
    y = y + (jnp.sum(r * k * r_k, axis=-1, keepdims=True) * v).reshape(B, T, W)
    return y * g, S, p[:, -1]

def gla_chunked(q, k, v, logg, S0):
    B, T, H, DK = q.shape
    DV = v.shape[-1]
    C = GLA_CHUNK if T % GLA_CHUNK == 0 else T
    N = T // C
    to_chunks = lambda x: x.reshape(B, N, C, H, x.shape[-1]).transpose(1, 0, 3, 2, 4)
    causal = jnp.tril(jnp.ones((C, C), dtype=bool))[:, :, None]

    def step(S, inp):
        qc, kc, vc, gc = inp
        b = jnp.cumsum(gc, axis=2)
        diff = b[:, :, :, None, :] - b[:, :, None, :, :]
        decay = jnp.exp(jnp.where(causal, diff, -jnp.inf))
        A = jnp.einsum('bhtd,bhsd,bhtsd->bhts', qc, kc, decay)
        o = jnp.einsum('bhts,bhsv->bhtv', A, vc) + jnp.einsum('bhtk,bhkv->bhtv', qc * jnp.exp(b), S)
        b_last = b[:, :, -1:, :]
        S = jnp.exp(b_last[:, :, 0, :])[..., None] * S + jnp.einsum('bhsk,bhsv->bhkv', kc * jnp.exp(b_last - b), vc)
        return S, o

    S, o = lax.scan(step, S0, (to_chunks(q), to_chunks(k), to_chunks(v), to_chunks(logg)))
    return o.transpose(1, 0, 3, 2, 4).reshape(B, T, H, DV), S

def gla_mix(h, S0, gate_up, gate_b, gn):
    f32 = jnp.float32
    B, T = h.shape[:2]
    h = h.astype(f32)
    q = h[..., :GLA_KW].reshape(B, T, GLA_HEADS, GLA_DK) * (GLA_DK ** -0.5)
    k = h[..., GLA_KW:2 * GLA_KW].reshape(B, T, GLA_HEADS, GLA_DK)
    o = 2 * GLA_KW
    v = h[..., o:o + GLA_VW].reshape(B, T, GLA_HEADS, GLA_DV)
    gd = h[..., o + GLA_VW:o + GLA_VW + GLA_RANK]
    r = h[..., o + GLA_VW + GLA_RANK:]
    logg = (jax.nn.log_sigmoid(gd @ gate_up + gate_b) / GLA_TAU).reshape(B, T, GLA_HEADS, GLA_DK)
    out, S = gla_chunked(q, k, v, logg, S0.astype(f32))
    out = rmsnorm(out, gn).reshape(B, T, GLA_VW) * jax.nn.silu(r)
    return out, S

def setup_inputs(seed: int = 0) -> dict:
    key = jax.random.key(seed)
    ks = iter(jax.random.split(key, 64))
    f32 = jnp.float32
    nrm = lambda shape, scale: jax.random.normal(next(ks), shape, f32) * scale
    gain = lambda shape: 1.0 + nrm(shape, 0.02)
    n_pages = PAST_LEN // PAGE_SIZE
    n_pool = (DEC_BATCH * n_pages * 5) // 4
    wb = min(WINDOW, PAST_LEN)
    perm = jax.random.permutation(next(ks), n_pool)
    page_table = perm[:DEC_BATCH * n_pages].reshape(DEC_BATCH, n_pages).astype(jnp.int32)
    return {
        'x_prompt': nrm((BATCH, SEQ, D_MODEL), 1.0),
        'x_sample': nrm((DEC_BATCH, DEC_SEQ, D_MODEL), 1.0),
        'cache_nsa_kv': nrm((N_EVEN, n_pool, PAGE_SIZE, 4, NSA_KV, HEAD_DIM), 1.0),
        'cache_nsa_win': nrm((N_EVEN, DEC_BATCH, wb, 2, NSA_KV, HEAD_DIM), 1.0),
        'state_rwkv': nrm((N_EVEN, DEC_BATCH, RWKV_HEADS, HEAD_DIM, HEAD_DIM), 0.2),
        'state_rwkv_shift': nrm((N_EVEN, DEC_BATCH, RWKV_IN), 1.0),
        'state_gla': nrm((N_ODD, DEC_BATCH, GLA_HEADS, GLA_DK, GLA_DV), 0.2),
        'page_table': page_table,
        'norm_mix': gain((DEPTH, D_MODEL)),
        'norm_ffn': gain((DEPTH, D_MODEL)),
        'w_in_even': nrm((N_EVEN, D_MODEL, EVEN_IN), D_MODEL ** -0.5),
        'nsa_qnorm': gain((N_EVEN, HEAD_DIM)),
        'nsa_knorm': gain((N_EVEN, 3, HEAD_DIM)),
        'cmp_w1': nrm((N_EVEN, 2, CMP_BLOCK, HEAD_DIM, CMP_HIDDEN), (CMP_BLOCK * HEAD_DIM) ** -0.5),
        'cmp_w2': nrm((N_EVEN, 2, CMP_HIDDEN, HEAD_DIM), CMP_HIDDEN ** -0.5),
        'cmp_pe': nrm((N_EVEN, 2, CMP_BLOCK, HEAD_DIM), 0.1),
        'rwkv_mu': jax.random.uniform(next(ks), (N_EVEN, RWKV_IN), f32),
        'rwkv_w0': nrm((N_EVEN, RWKV_WIDTH), 0.5),
        'rwkv_wB': nrm((N_EVEN, LORA_W, RWKV_WIDTH), LORA_W ** -0.5),
        'rwkv_a0': nrm((N_EVEN, RWKV_WIDTH), 0.5),
        'rwkv_aB': nrm((N_EVEN, LORA_A, RWKV_WIDTH), LORA_A ** -0.5),
        'rwkv_gB': nrm((N_EVEN, LORA_G, RWKV_WIDTH), LORA_G ** -0.5),
        'rwkv_kk': 0.85 + nrm((N_EVEN, RWKV_WIDTH), 0.05),
        'rwkv_ka': 1.0 + nrm((N_EVEN, RWKV_WIDTH), 0.05),
        'rwkv_rk': nrm((N_EVEN, RWKV_HEADS, HEAD_DIM), 0.1),
        'rwkv_ln_w': gain((N_EVEN, RWKV_WIDTH)),
        'rwkv_ln_b': nrm((N_EVEN, RWKV_WIDTH), 0.02),
        'w_out_even': nrm((N_EVEN, MIX_WIDTH, D_MODEL), MIX_WIDTH ** -0.5),
        'w_in_odd': nrm((N_ODD, D_MODEL, ODD_IN), D_MODEL ** -0.5),
        'gla_gate_up': nrm((N_ODD, GLA_RANK, GLA_KW), GLA_RANK ** -0.5),
        'gla_gate_b': 1.0 + nrm((N_ODD, GLA_KW), 0.5),
        'gla_norm': gain((N_ODD, GLA_DV)),
        'w_out_odd': nrm((N_ODD, GLA_VW, D_MODEL), GLA_VW ** -0.5),
        'ffn_gate': nrm((DEPTH, D_MODEL, D_FF), D_MODEL ** -0.5),
        'ffn_up': nrm((DEPTH, D_MODEL, D_FF), D_MODEL ** -0.5),
        'ffn_down': nrm((DEPTH, D_FF, D_MODEL), D_FF ** -0.5),
    }

def reference(x_prompt, x_sample, cache_nsa_kv, cache_nsa_win, state_rwkv, state_rwkv_shift, state_gla,
              page_table, norm_mix, norm_ffn, w_in_even, nsa_qnorm, nsa_knorm, cmp_w1, cmp_w2, cmp_pe,
              rwkv_mu, rwkv_w0, rwkv_wB, rwkv_a0, rwkv_aB, rwkv_gB, rwkv_kk, rwkv_ka, rwkv_rk,
              rwkv_ln_w, rwkv_ln_b, w_out_even, w_in_odd, gla_gate_up, gla_gate_b, gla_norm, w_out_odd,
              ffn_gate, ffn_up, ffn_down):
    dt = x_prompt.dtype
    B, T = x_prompt.shape[:2]
    DB, S = x_sample.shape[:2]
    P = page_table.shape[1] * PAGE_SIZE
    WB = cache_nsa_win.shape[2]
    WP = min(WINDOW, T)
    pos_p = jnp.arange(T, dtype=jnp.int32)
    pos_s = P + jnp.arange(S, dtype=jnp.int32)
    win_pos_s = P - WB + jnp.arange(WB + S, dtype=jnp.int32)
    y_p, y_s = x_prompt, x_sample
    kv_p, kv_s, win_p, win_s, rw_p, rw_s, sh_p, sh_s, gl_p, gl_s = ([] for _ in range(10))
    for layer in range(DEPTH):
        li = layer // 2
        if layer % 2 == 0:
            h_p = rmsnorm(y_p, norm_mix[layer]) @ w_in_even[li]
            h_s = rmsnorm(y_s, norm_mix[layer]) @ w_in_even[li]
            q, g, rows, win = nsa_project(h_p[..., :NSA_IN], pos_p, nsa_qnorm[li], nsa_knorm[li])
            o_nsa_p = nsa_prompt(q, g, rows, win, cmp_w1[li], cmp_w2[li], cmp_pe[li])
            kv_p.append(rows.astype(dt))
            win_p.append(win[:, T - WP:].astype(dt))
            q, g, rows, win = nsa_project(h_s[..., :NSA_IN], pos_s, nsa_qnorm[li], nsa_knorm[li])
            past = cache_nsa_kv[li][page_table].reshape(DB, P, 4, NSA_KV, HEAD_DIM)
            rows_all = jnp.concatenate([past, rows.astype(past.dtype)], axis=1)
            win_all = jnp.concatenate([cache_nsa_win[li], win.astype(cache_nsa_win.dtype)], axis=1)
            kc, vc, cmp_end, sel_map, ksb, vsb = nsa_keys(rows_all, cmp_w1[li], cmp_w2[li], cmp_pe[li])
            o_nsa_s = nsa_block(q, g, pos_s, kc, vc, cmp_end, sel_map, ksb, vsb, win_all, win_pos_s)
            kv_s.append(rows.astype(dt))
            win_s.append(win_all[:, S:].astype(dt))
            rw_par = (rwkv_mu[li], rwkv_w0[li], rwkv_wB[li], rwkv_a0[li], rwkv_aB[li], rwkv_gB[li],
                      rwkv_kk[li], rwkv_ka[li], rwkv_rk[li], rwkv_ln_w[li], rwkv_ln_b[li])
            o_rw_p, st, last = rwkv_mix(h_p[..., NSA_IN:], jnp.zeros((B, RWKV_IN), dt),
                                        jnp.zeros((B, RWKV_HEADS, HEAD_DIM, HEAD_DIM), dt), *rw_par)
            rw_p.append(st.astype(dt))
            sh_p.append(last.astype(dt))
            o_rw_s, st, last = rwkv_mix(h_s[..., NSA_IN:], state_rwkv_shift[li], state_rwkv[li], *rw_par)
            rw_s.append(st.astype(dt))
            sh_s.append(last.astype(dt))
            mix_p = jnp.concatenate([o_nsa_p.astype(dt), o_rw_p.astype(dt)], axis=-1) @ w_out_even[li]
            mix_s = jnp.concatenate([o_nsa_s.astype(dt), o_rw_s.astype(dt)], axis=-1) @ w_out_even[li]
        else:
            h_p = rmsnorm(y_p, norm_mix[layer]) @ w_in_odd[li]
            h_s = rmsnorm(y_s, norm_mix[layer]) @ w_in_odd[li]
            o_p, st = gla_mix(h_p, jnp.zeros((B, GLA_HEADS, GLA_DK, GLA_DV), dt),
                              gla_gate_up[li], gla_gate_b[li], gla_norm[li])
            gl_p.append(st.astype(dt))
            o_s, st = gla_mix(h_s, state_gla[li], gla_gate_up[li], gla_gate_b[li], gla_norm[li])
            gl_s.append(st.astype(dt))
            mix_p = o_p.astype(dt) @ w_out_odd[li]
            mix_s = o_s.astype(dt) @ w_out_odd[li]
        y_p = y_p + mix_p
        y_s = y_s + mix_s
        y_p = y_p + swiglu(rmsnorm(y_p, norm_ffn[layer]), ffn_gate[layer], ffn_up[layer], ffn_down[layer])
        y_s = y_s + swiglu(rmsnorm(y_s, norm_ffn[layer]), ffn_gate[layer], ffn_up[layer], ffn_down[layer])
    return (y_p, y_s, jnp.stack(kv_p), jnp.stack(kv_s), jnp.stack(win_p), jnp.stack(win_s),
            jnp.stack(rw_p), jnp.stack(rw_s), jnp.stack(sh_p), jnp.stack(sh_s),
            jnp.stack(gl_p), jnp.stack(gl_s))


_drawn_inputs = setup_inputs


def setup_inputs(seed=0):
    import zlib

    import numpy as np

    out = dict(_drawn_inputs(seed))
    spreads = {}
    factors = {'nsa_qnorm': 8.0,
     'nsa_knorm': 3.765,
     'rwkv_kk': 12.747,
     'rwkv_ln_w': 4.736,
     'rwkv_ln_b': 4.561,
     'gla_norm': 17.015}
    for name, (base, spread) in spreads.items():
        noise = np.random.default_rng([zlib.crc32(name.encode()), seed]).standard_normal(out[name].shape)
        drawn = base * np.exp(spread * noise) if base else spread * noise
        out[name] = __import__('jax').numpy.asarray(drawn.astype(out[name].dtype))
    for name, factor in factors.items():
        out[name] = (out[name] * factor).astype(out[name].dtype)
    return out
```

```python
from contextlib import ExitStack

import numpy as np

import concourse.bass as bass
from concourse import mybir

F32 = mybir.dt.float32
I32 = mybir.dt.int32
ALU = mybir.AluOpType
ACT = mybir.ActivationFunctionType
AX = mybir.AxisListType.X
ds = bass.ds

P = 128
D = 1024
KT = D // P
NP = 1024
NB, SS = 8, 8
NS = NB * SS
TOK = NP + NS
HD = 64
FF = 2816
FT = FF // P
PARTS = ((0, 12), (12, 10))
CH = ((0, 384), (384, 384), (768, 320))
NCMP = 63
NSEL = 17
NEG = -1e30
KSETS = 3
QK = 512 + KSETS * P
NSAW = QK + KSETS * P + 24
RT = 14
EPS = 1e-6
GN_EPS = 64e-5


def _constants():
    i = np.arange(P)
    t64, c64 = i[:, None] % 64, np.arange(64)[None, :]
    same8 = (t64 // 8) == (c64 // 8)
    parts = {
        "ident": np.eye(P),
        "mean": np.full((P, P), 1.0 / D),
        "blk": (i[:, None] // 64 == i[None, :] // 64) * 1.0,
        "ones": np.ones((P, P)),
        "causal": np.where(i[None, :] <= i[:, None], 0.0, NEG),
        "window": np.where(i[None, :] > i[:, None], 0.0, NEG),
        "cmpmask": np.where(16 * np.arange(NCMP)[None, None, :] + 31 <= (i[:, None] + 128 * np.arange(8)[None, :])[:, :, None], 0.0, NEG),
        "seen": (i[:, None] >= 31) * 1.0,
        "id2": (t64 == c64) * 1.0,
        "below": (c64 < t64) * 1.0,
        "above": (c64 > t64) * 1.0,
        "upto": (c64 >= t64) * 1.0,
        "below8": (c64 < t64) * same8 * 1.0,
        "above8": (c64 > t64) * same8 * 1.0,
        "upto8": (c64 >= t64) * same8 * 1.0,
        "bcol": np.broadcast_to((np.arange(8)[:, None] == c64[0][None, :] // 8) * 1.0, (P, 8, 64)),
        "brow": (t64 // 8 == np.arange(8)[None, :]) * 1.0,
        "smask": np.where(np.arange(8)[None, :] <= i[:, None] % 8, 0.0, NEG),
        "swmask": np.where(np.arange(8)[None, :] > i[:, None] % 8, 0.0, NEG),
        "selmap": ((16 * i[:, None] <= 64 * np.arange(NSEL)[None, :] + 63) & (16 * i[:, None] + 31 >= 64 * np.arange(NSEL)[None, :]) & (i[:, None] < NCMP)) * 1.0,
        "samerow": ((i[:, None] // 32 == i[None, :] // 32) & (i[:, None] % 8 == i[None, :] % 8)) * 1.0,
        "blkid": np.broadcast_to(np.arange(NSEL)[None, :] * 1.0, (P, NSEL)),
        "scan": np.broadcast_to(np.where(np.arange(TOK) < NP, np.arange(TOK) % 64, np.arange(TOK) % 8)[None, :] != 0, (P, TOK)) * 1.0,
    }
    half = 8
    inv = (np.float32(500000.0) ** (-np.arange(half, dtype=np.float32) / np.float32(half))).astype(np.float32)
    pos = np.concatenate([np.arange(NP), 1024 + np.arange(NS) % SS, np.zeros(64)]).astype(np.float32)
    ang = pos[:, None] * inv[None, :]
    rope = np.concatenate([np.cos(ang), np.sin(ang)], axis=1).reshape(9, P, 16).transpose(1, 0, 2)
    parts["rope"] = rope
    return {k: np.ascontiguousarray(v, dtype=np.float32) for k, v in parts.items()}


PARAMS = (("mix", 16), ("ffn", 16), ("mu", 14), ("w0", 4), ("a0", 4), ("kk", 4), ("ka", 4), ("rk", 4),
          ("lnw", 4), ("lnb", 4), ("gb", 4), ("gn", 2), ("eps", 1), ("gneps", 1))


def names(**items):
    return type("Names", (), items)()


class Signal:

    def __init__(self, nc, ctx, name):
        self.sem = ctx.enter_context(nc.semaphore(name))
        self.waited = {}

    def mark(self, instruction):
        instruction.then_inc(self.sem, 1)

    def next(self, engine, n=1):
        who = str(engine.engine)
        self.waited[who] = self.waited.get(who, 0) + n
        engine.wait_ge(self.sem, self.waited[who])


def signals(nc, ctx, prefix, listed):
    return names(**{n: Signal(nc, ctx, prefix + n) for n in listed.split()})


def allocate(nc, ctx, shapes):
    sb = lambda name, shape: ctx.enter_context(nc.sbuf_tensor(name, shape, F32))
    const = sb("const", [P, sum(int(np.prod(s[1:])) for s in shapes.values())])
    param = sb("param", [P, sum(n for _, n in PARAMS)])
    items, at = {}, 0
    for name, s in shapes.items():
        n = int(np.prod(s[1:]))
        v = const[:, at:at + n]
        items[name] = v.rearrange("p (a b) -> p a b", b=s[2]) if len(s) == 3 else v
        at += n
    col, at = {}, 0
    for name, n in PARAMS:
        col[name] = param[:, at:at + n]
        at += n
    g = names(nc=nc, const=const, param=param, col=col, resid=sb("resid", [P, KT, TOK]), act=sb("act", [P, KT, TOK]), **items)
    sem = lambda n: ctx.enter_context(nc.semaphore(n))
    g.ff_sems = (sem("gate_here"), sem("up_here"), (sem("down_here0"), sem("down_here1")), sem("gate_done"), sem("up_done"),
                 sem("down_done"), sem("gate_out"), sem("up_out"), sem("down_out"))
    g.out_sems = ((sem("wo_here0"), sem("wo_here1")), sem("wo_done"), sem("wo_out"))
    g.norm_signals = signals(nc, ctx, "norm_", "squared mean_ready root_ready")
    g.ps = ctx.enter_context(nc.psum_tensor("ps", [P, 8, 512], F32))
    return g


def load_inputs(g, d):
    nc = g.nc
    with ExitStack() as ctx:
        s_in = ctx.enter_context(nc.semaphore("inputs_here"))
        block = ctx.enter_context(nc.Block())

        @block.sync
        def _(sp):
            sp.dma_start(g.resid[:, :, :], d.x).then_inc(s_in, 16)
            sp.dma_start(g.const[:, :], d.const).then_inc(s_in, 16)
            sp.dma_start(g.param[:, :], d.param).then_inc(s_in, 16)
            sp.wait_ge(s_in, 48)


def rmsnorm(g, name, gain):
    nc = g.nc
    s = g.norm_signals
    with ExitStack() as ctx:
        sq = ctx.enter_context(nc.sbuf_tensor(name + "sq", [P, 2, KT, 384], F32))
        rs = ctx.enter_context(nc.sbuf_tensor(name + "rs", [P, 3, 384], F32))
        block = ctx.enter_context(nc.Block())

        @block.scalar
        def _(act):
            def square(c):
                o, n = CH[c]
                s.squared.mark(act.activation(sq[:, c % 2, :, 0:n], g.resid[:, :, o:o + n], ACT.Square))

            square(0)
            square(1)
            for c, (o, n) in enumerate(CH):
                s.mean_ready.next(act)
                s.root_ready.mark(act.activation(rs[:, c, 0:n], g.ps[:, c, 0:n], ACT.Sqrt, bias=g.col["eps"]))
                if c == 0:
                    square(2)

        @block.tensor
        def _(pe):
            for c, (o, n) in enumerate(CH):
                s.squared.next(pe)
                for k in range(KT):
                    mm = pe.matmul(g.ps[:, c, 0:n], g.mean, sq[:, c % 2, k, 0:n], start=(k == 0), stop=(k == KT - 1))
                s.mean_ready.mark(mm)

        @block.vector
        def _(dve):
            for c, (o, n) in enumerate(CH):
                s.root_ready.next(dve)
                dve.reciprocal(rs[:, c, 0:n], rs[:, c, 0:n])
                dve.drain()
                for k in range(KT):
                    dve.scalar_tensor_tensor(g.act[:, k, o:o + n], g.resid[:, k, o:o + n], gain[:, k:k + 1],
                                             rs[:, c, 0:n], ALU.mult, ALU.mult)


def feed_forward(g, layer, w_gate, w_up, w_down):
    nc = g.nc
    name = f"ff{layer}_"
    P0, F0, D0 = layer * FT // 2, layer * FT, layer * 2 * KT
    gate_here, up_here, down_here, gate_done, up_done, down_done, gate_out, up_out, down_out = g.ff_sems
    with ExitStack() as ctx:
        wg = ctx.enter_context(nc.sbuf_tensor(name + "wg", [P, KT, 2 * P], F32))
        wu = ctx.enter_context(nc.sbuf_tensor(name + "wu", [P, KT, 2 * P], F32))
        wd = [ctx.enter_context(nc.sbuf_tensor(name + f"wd{i}", [P, PARTS[0][1], P], F32)) for i in range(2)]
        hid = ctx.enter_context(nc.sbuf_tensor(name + "hid", [P, PARTS[0][1], TOK], F32))
        block = ctx.enter_context(nc.Block())
        pairs = FT // 2

        @block.sync
        def _(sp):
            sp.dma_start(wg[:, :, :], w_gate[0]).then_inc(gate_here, 16)
            sp.dma_start(wu[:, :, :], w_up[0]).then_inc(up_here, 16)
            with sp.Fori(0, pairs - 1) as i:
                sp.wait_ge(gate_done, 2 * i + F0 + 2)
                sp.dma_start(wg[:, :, :], w_gate[ds(i + 1, 1)].rearrange("a p k n -> (a p) k n")).then_inc(gate_here, 16)
                sp.wait_ge(up_done, 2 * i + F0 + 2)
                sp.dma_start(wu[:, :, :], w_up[ds(i + 1, 1)].rearrange("a p k n -> (a p) k n")).then_inc(up_here, 16)

        @block.gpsimd
        def _(pool):
            for part, (f0, nf) in enumerate(PARTS):
                for t in range(2):
                    if part == 1:
                        pool.wait_ge(down_done, D0 + 7 + t)
                    pool.dma_start(wd[t][:, 0:nf, :], w_down[t, :, f0:f0 + nf, :]).then_inc(down_here[t], 16)
                with pool.Fori(1, KT // 2) as i:
                    for t in range(2):
                        pool.wait_ge(down_done, 2 * i + (D0 + 8 * part + t - 1))
                        pool.dma_start(wd[t][:, 0:nf, :], w_down[ds(2 * i + t, 1), :, f0:f0 + nf, :]
                                       .rearrange("a p k n -> (a p) k n")).then_inc(down_here[t], 16)

        @block.tensor
        def _(pe):
            for part, (f0, nf) in enumerate(PARTS):
                if part == 1:
                    pe.wait_ge(down_out, D0 + 8 + 2)
                with pe.Fori(0, nf // 2) as i:
                    for t in range(2):
                        if t == 0:
                            pe.wait_ge(gate_here, 16 * (i + P0 + f0 // 2 + 1))
                        pe.wait_ge(gate_out, 2 * i + F0 + f0 + t + 1)
                        for k in range(KT):
                            for c, (o, n) in enumerate(CH):
                                mm = pe.matmul(g.ps[:, c, 0:n], wg[:, k, t * P:t * P + P], g.act[:, k, o:o + n],
                                               start=(k == 0), stop=(k == KT - 1))
                        mm.then_inc(gate_done, 1)
                        if t == 0:
                            pe.wait_ge(up_here, 16 * (i + P0 + f0 // 2 + 1))
                        pe.wait_ge(up_out, 2 * i + F0 + f0 + t + 1)
                        for k in range(KT):
                            for c, (o, n) in enumerate(CH):
                                mm = pe.matmul(g.ps[:, 3 + c, 0:n], wu[:, k, t * P:t * P + P], g.act[:, k, o:o + n],
                                               start=(k == 0), stop=(k == KT - 1))
                        mm.then_inc(up_done, 1)
                pe.wait_ge(up_out, F0 + f0 + nf + 1)
                with pe.Fori(0, KT // 2) as i:
                    for t in range(2):
                        pe.wait_ge(down_here[t], 16 * (i + D0 // 2 + 4 * part + 1))
                        pe.wait_ge(down_out, 2 * i + D0 + 8 * part + t + 1)
                        for k in range(nf):
                            for c, (o, n) in enumerate(CH):
                                mm = pe.matmul(g.ps[:, 3 * t + c, 0:n], wd[t][:, k, :], hid[:, k, o:o + n],
                                               start=(k == 0), stop=(k == nf - 1))
                        mm.then_inc(down_done, 1)

        @block.scalar
        def _(act):
            if layer == 0:
                act.sem_inc(gate_out, 1)
            for part, (f0, nf) in enumerate(PARTS):
                with act.Fori(0, nf) as i:
                    act.wait_ge(gate_done, i + F0 + f0 + 1)
                    for c, (o, n) in enumerate(CH):
                        a = act.activation(hid[:, ds(i, 1), o:o + n].rearrange("p a n -> p (a n)"), g.ps[:, c, 0:n], ACT.Silu)
                    a.then_inc(gate_out, 1)

        @block.vector
        def _(dve):
            if layer == 0:
                dve.sem_inc(up_out, 1)
                dve.sem_inc(down_out, 2)
            for part, (f0, nf) in enumerate(PARTS):
                with dve.Fori(0, nf) as i:
                    dve.wait_ge(gate_out, i + F0 + f0 + 2)
                    dve.wait_ge(up_done, i + F0 + f0 + 1)
                    for c, (o, n) in enumerate(CH):
                        h = hid[:, ds(i, 1), o:o + n].rearrange("p a n -> p (a n)")
                        a = dve.tensor_tensor(h, h, g.ps[:, 3 + c, 0:n], ALU.mult)
                    a.then_inc(up_out, 1)
                with dve.Fori(0, KT // 2) as i:
                    for t in range(2):
                        dve.wait_ge(down_done, 2 * i + D0 + 8 * part + t + 1)
                        for c, (o, n) in enumerate(CH):
                            r = g.resid[:, ds(2 * i + t, 1), o:o + n].rearrange("p a n -> p (a n)")
                            a = dve.tensor_tensor(r, r, g.ps[:, 3 * t + c, 0:n], ALU.add)
                        a.then_inc(down_out, 1)


def project_out(g, layer, w):
    T0 = layer * KT
    name = f"out{layer}_"
    here, done, out = g.out_sems
    nc = g.nc
    with ExitStack() as ctx:
        wo = [ctx.enter_context(nc.sbuf_tensor(name + f"w{i}", [P, KT, P], F32)) for i in range(2)]
        block = ctx.enter_context(nc.Block())

        @block.sync
        def _(sp):
            for t in range(2):
                sp.dma_start(wo[t][:, :, :], w[t]).then_inc(here[t], 16)
            with sp.Fori(1, KT // 2) as i:
                for t in range(2):
                    sp.wait_ge(done, 2 * i + (T0 + t - 1))
                    sp.dma_start(wo[t][:, :, :], w[ds(2 * i + t, 1)].rearrange("a p k n -> (a p) k n")).then_inc(here[t], 16)

        @block.tensor
        def _(pe):
            with pe.Fori(0, KT // 2) as i:
                for t in range(2):
                    pe.wait_ge(here[t], 16 * (i + T0 // 2 + 1))
                    pe.wait_ge(out, 2 * i + T0 + t + 1)
                    for k in range(KT):
                        for c, (o, n) in enumerate(CH):
                            mm = pe.matmul(g.ps[:, 3 * t + c, 0:n], wo[t][:, k, :], g.act[:, k, o:o + n],
                                           start=(k == 0), stop=(k == KT - 1))
                    mm.then_inc(done, 1)

        @block.vector
        def _(dve):
            if layer == 0:
                dve.sem_inc(out, 2)
            with dve.Fori(0, KT // 2) as i:
                for t in range(2):
                    dve.wait_ge(done, 2 * i + T0 + t + 1)
                    for c, (o, n) in enumerate(CH):
                        r = g.resid[:, ds(2 * i + t, 1), o:o + n].rearrange("p a n -> p (a n)")
                        a = dve.tensor_tensor(r, r, g.ps[:, 3 * t + c, 0:n], ALU.add)
                    a.then_inc(out, 1)


def nsa_project(g, d):
    nc = g.nc
    tiles = [(t, min(P, TOK - t * P)) for t in range(9)]
    H = QK // HD
    with ExitStack() as ctx:
        sem = lambda s: ctx.enter_context(nc.semaphore("np_" + s))
        sb = lambda s, shape: ctx.enter_context(nc.sbuf_tensor("np_" + s, shape, F32))
        w = sb("w", [P, KT, NSAW])
        gain = sb("gain", [P, QK])
        sq = sb("sq", [P, QK])
        qk = [sb("qk0", [P, QK]), sb("qk1", [P, QK])]
        rn = sb("rn", [P, 2, H])
        rot = sb("rot", [P, 4, H, 8])
        w_here = [sem(f"w_here{i}") for i in range(2)]
        product, squared, summed, root, scaled = sem("product"), sem("squared"), sem("summed"), sem("root"), sem("scaled")
        freed_a, freed_v = sem("freed_a"), sem("freed_v")
        normed, turned, moved, stored = sem("normed"), sem("turned"), sem("moved"), [sem("stored0"), sem("stored1")]
        block = ctx.enter_context(nc.Block())

        @block.sync
        def _(sp):
            for i in range(2):
                sp.dma_start(w[:, 4 * i:4 * i + 4, :], d.w_nsa[:, 4 * i:4 * i + 4, :]).then_inc(w_here[i], 16)
            sp.dma_start(gain[:, :], d.qk_gain.partition_broadcast(P)).then_inc(w_here[0], 16)
            for t, R in tiles:
                sp.wait_ge(normed, t + 1)
                sp.dma_start(d.kv[t * P:t * P + R, 0:384], qk[t % 2][0:R, 512:QK]).then_inc(stored[t % 2], 16)
                sp.wait_ge(freed_v, t + 1)
                sp.dma_start(d.kv[t * P:t * P + R, 384:768], g.vtok[0:R, t, :]).then_inc(stored[t % 2], 16)
            sp.wait_ge(stored[0], 5 * 32)
            sp.wait_ge(stored[1], 4 * 32)

        @block.tensor
        def _(pe):
            def project(t, R):
                b = 3 * (t % 2)
                if t >= 2:
                    pe.wait_ge(scaled, t - 1)
                    pe.wait_ge(freed_v, t - 1)
                for k in range(KT):
                    x = g.act[:, k, t * P:t * P + R]
                    if t == 0 and k % 4 == 0:
                        pe.wait_ge(w_here[k // 4], 32 if k == 0 else 16)
                    for j, (o, n) in enumerate(((0, 512), (512, 384), (QK, 408))):
                        mm = pe.matmul(g.ps[0:R, b + j, 0:n], x, w[:, k, o:o + n], start=(k == 0), stop=(k == KT - 1))
                mm.then_inc(product, 1)

            def turn(t, R):
                pe.wait_ge(normed, t + 1)
                if t >= 1:
                    pe.wait_ge(moved, 2 * t)
                for j in range(7):
                    mm = pe.transpose(g.ps[:, 6 + j // 4, (j % 4) * P:(j % 4) * P + R], qk[t % 2][0:R, j * P:j * P + P],
                                      g.ident[0:R, 0:R])
                mm.then_inc(turned, 1)

            project(*tiles[0])
            for t, R in tiles:
                if t + 1 < 9:
                    project(*tiles[t + 1])
                turn(t, R)

        @block.scalar
        def _(act):
            def move(t, R):
                act.wait_ge(turned, t + 1)
                act.activation(g.qT[:, :, t * P:t * P + R], g.ps[:, 6, :].rearrange("p (a b) -> p a b", b=P)[:, :, 0:R], ACT.Copy)\
                   .then_inc(moved, 1)

            for t, R in tiles:
                b = 3 * (t % 2)
                act.wait_ge(product, t + 1)
                if t >= 1:
                    act.wait_ge(summed, t)
                act.activation(sq[0:R, 0:512], g.ps[0:R, b, 0:512], ACT.Square)
                act.activation(sq[0:R, 512:QK], g.ps[0:R, b + 1, 0:384], ACT.Square).then_inc(squared, 1)
                act.activation(g.vtok[0:R, t, :], g.ps[0:R, b + 2, 0:384], ACT.Copy)
                act.activation(g.gates[0:R, t, :], g.ps[0:R, b + 2, 384:408], ACT.Copy).then_inc(freed_v, 1)
                act.wait_ge(summed, t + 1)
                if t >= 1:
                    act.wait_ge(scaled, t)
                act.activation(rn[0:R, 0, :], rn[0:R, 1, :], ACT.Sqrt, bias=g.col["eps"][0:R, :], scale=1.0 / HD).then_inc(root, 1)
                if t >= 1:
                    move(t - 1, P)
            move(8, NS)
            act.drain()
            act.activation(g.gates[:, 0:8, :], g.gates[:, 0:8, :], ACT.Sigmoid)
            act.activation(g.gates[0:NS, 8, :], g.gates[0:NS, 8, :], ACT.Sigmoid)

        @block.vector
        def _(dve):
            def move(t, R):
                dve.wait_ge(turned, t + 1)
                dve.tensor_copy(g.kT[:, :, t * P:t * P + R], g.ps[:, 7, 0:384].rearrange("p (a b) -> p a b", b=P)[:, :, 0:R])\
                   .then_inc(moved, 1)

            for t, R in tiles:
                b = 3 * (t % 2)
                x = qk[t % 2]
                v = x[0:R, :].rearrange("p (h c) -> p h c", c=HD)
                dve.wait_ge(squared, t + 1)
                if t >= 1:
                    dve.wait_ge(root, t)
                dve.tensor_reduce(rn[0:R, 1, :], sq[0:R, :].rearrange("p (h c) -> p h c", c=HD), AX, ALU.add).then_inc(summed, 1)
                if t == 0:
                    dve.wait_ge(w_here[0], 32)
                if t >= 2:
                    dve.wait_ge(turned, t - 1)
                    dve.wait_ge(stored[t % 2], 32 * (t // 2))
                dve.tensor_tensor(x[0:R, 0:512], g.ps[0:R, b, 0:512], gain[0:R, 0:512], ALU.mult)
                dve.tensor_tensor(x[0:R, 512:QK], g.ps[0:R, b + 1, 0:384], gain[0:R, 512:QK], ALU.mult)
                dve.wait_ge(root, t + 1)
                dve.reciprocal(rn[0:R, 0, :], rn[0:R, 0, :])
                dve.drain()
                dve.tensor_tensor(v, v, rn[0:R, 0, :].unsqueeze(2).to_broadcast([R, H, HD]), ALU.mult).then_inc(scaled, 1)
                dve.drain()
                cos = g.rope[0:R, t, 0:8].unsqueeze(1).to_broadcast([R, H, 8])
                sin = g.rope[0:R, t, 8:16].unsqueeze(1).to_broadcast([R, H, 8])
                dve.tensor_tensor(rot[0:R, 0], v[:, :, 0:8], cos, ALU.mult)
                dve.tensor_tensor(rot[0:R, 1], v[:, :, 8:16], sin, ALU.mult)
                dve.tensor_tensor(rot[0:R, 2], v[:, :, 8:16], cos, ALU.mult)
                dve.tensor_tensor(rot[0:R, 3], v[:, :, 0:8], sin, ALU.mult)
                dve.drain()
                dve.tensor_tensor(v[:, :, 0:8], rot[0:R, 0], rot[0:R, 1], ALU.subtract)
                dve.tensor_tensor(v[:, :, 8:16], rot[0:R, 2], rot[0:R, 3], ALU.add).then_inc(normed, 1)
                dve.drain()
                if t >= 1:
                    move(t - 1, P)
            move(8, NS)


def nsa_compress(g, d):
    nc = g.nc
    with ExitStack() as ctx:
        sem = lambda s: ctx.enter_context(nc.semaphore("nc_" + s))
        sb = lambda s, shape: ctx.enter_context(nc.sbuf_tensor("nc_" + s, shape, F32))
        past = [sb("past0", [P, NB, 512]), sb("past1", [P, NB, 512])]
        rows = sb("rows", [P, 4, 4, P])
        pairs = sb("pairs", [P, 4, 512])
        w1 = sb("w1", [P, 2, 16, P])
        w2 = sb("w2", [P, 2, HD])
        pe_in = sb("pe", [P, 2, 16])
        bias = sb("bias", [P, 2])
        hid = sb("hid", [P, 2, 9, NCMP])
        pt = ctx.enter_context(nc.sbuf_tensor("nc_pages", [1, NB * 8], I32))
        w_here, rows_here, pt_here = sem("w_here"), sem("rows_here"), sem("pt_here")
        past_here = [sem("past_here0"), sem("past_here1")]
        turned, moved, biased, bias_ready = sem("turned"), sem("moved"), sem("biased"), sem("bias_ready")
        h_done, h_out, c_done, c_out = sem("h_done"), sem("h_out"), sem("c_done"), sem("c_out")
        block = ctx.enter_context(nc.Block())

        @block.sync
        def _(sp):
            sp.dma_start(pt[:, :], d.pages).then_inc(pt_here, 16)
            for i in range(4):
                src = d.kv[i * 256:(i + 1) * 256, :].rearrange("(p e) c -> p e c", e=2)
                for s in range(4):
                    at = 384 * (s // 2) + 64 * (s % 2)
                    sp.dma_start(rows[:, i, s, :].rearrange("p (e c) -> p e c", e=2), src[:, :, at:at + 64]).then_inc(rows_here, 16)
            sp.dma_start(w1[:, :, :, :], d.cmp_w1).then_inc(w_here, 16)
            sp.dma_start(w2[:, :, :], d.cmp_w2).then_inc(w_here, 16)
            sp.dma_start(pe_in[:, :, :], d.cmp_pe).then_inc(w_here, 16)
            sp.wait_ge(pt_here, 16)
            for s in range(4):
                if s >= 2:
                    sp.wait_ge(h_done, s - 1)
                for b in range(NB):
                    for i in range(8):
                        page = sp.value_load(pt[0:1, b * 8 + i:b * 8 + i + 1], min_val=0, max_val=79)
                        sp.dma_start(past[s % 2][:, b, i * 64:(i + 1) * 64],
                                     d.cache_cmp[ds(page, 1), :, s, :].rearrange("a p n -> (a p) n")).then_inc(past_here[s % 2], 16)

        @block.tensor
        def _(pe):
            pe.wait_ge(w_here, 48)
            for s in range(2):
                for l in range(16):
                    mm = pe.matmul(g.ps[:, 4, s:s + 1], w1[:, s, l, :], pe_in[:, s, l:l + 1], start=(l == 0), stop=(l == 15))
            mm.then_inc(biased, 1)
            pe.wait_ge(rows_here, 16 * 16)
            for s in range(4):
                for i in range(4):
                    mm = pe.transpose(g.ps[:, s, i * P:(i + 1) * P], rows[:, i, s, :], g.ident)
                mm.then_inc(turned, 1)
            pe.wait_ge(moved, 4)

            def hidden(s):
                pe.wait_ge(past_here[s % 2], 64 * 16 * (s // 2 + 1))
                if s >= 2:
                    pe.wait_ge(h_out, s - 1)
                b = 2 * (s % 2)
                for l in range(16):
                    w = w1[:, s // 2, l, :]
                    pe.matmul(g.ps[:, b, 0:504].rearrange("p (a n) -> p a n", n=NCMP), w, past[s % 2][:, :, l:l + 497:8],
                              start=(l == 0), stop=(l == 15))
                    mm = pe.matmul(g.ps[:, b + 1, 0:NCMP], w, pairs[:, s, l:l + 497:8], start=(l == 0), stop=(l == 15))
                mm.then_inc(h_done, 1)

            def compressed(s):
                pe.wait_ge(h_out, s + 1)
                q = 64 * (s % 2)
                if s < 2:
                    if s == 0:
                        pe.wait_ge(bias_ready, 1)
                    pe.matmul(g.ps[q:q + 64, 6, 0:504], w2[:, 0, :], hid[:, s % 2, 0:8, :].rearrange("p a n -> p (a n)"), start=True, stop=True)
                    mm = pe.matmul(g.ps[q:q + 64, 7, 0:NCMP], w2[:, 0, :], hid[:, s % 2, 8, :], start=True, stop=True)
                else:
                    for b in range(9):
                        mm = pe.matmul(g.ps[0:NCMP, 4 + b // 8, 64 * (b % 8):64 * (b % 8) + 64], hid[:, s % 2, b, :], w2[:, 1, :],
                                       start=True, stop=True)
                mm.then_inc(c_done, 1)

            hidden(0)
            for s in range(4):
                if s + 1 < 4:
                    hidden(s + 1)
                if s >= 1:
                    pe.wait_ge(c_out, s)
                compressed(s)

        @block.scalar
        def _(act):
            act.wait_ge(biased, 1)
            act.activation(bias[:, :], g.ps[:, 4, 0:2], ACT.Copy).then_inc(bias_ready, 1)
            act.wait_ge(bias_ready, 1)
            for s in range(4):
                act.wait_ge(h_done, s + 1)
                if s >= 2:
                    act.wait_ge(c_done, s - 1)
                b = 2 * (s % 2)
                act.activation(hid[:, s % 2, 0:8, :].rearrange("p a n -> p (a n)"), g.ps[:, b, 0:504], ACT.Gelu_apprx_tanh, bias=bias[:, s // 2:s // 2 + 1])
                act.activation(hid[:, s % 2, 8, :], g.ps[:, b + 1, 0:NCMP], ACT.Gelu_apprx_tanh, bias=bias[:, s // 2:s // 2 + 1])\
                   .then_inc(h_out, 1)

        @block.vector
        def _(dve):
            for s in range(4):
                dve.wait_ge(turned, s + 1)
                dve.tensor_copy(pairs[:, s, :], g.ps[:, s, :]).then_inc(moved, 1)
            for s in range(4):
                q = 64 * (s % 2)
                dve.wait_ge(c_done, s + 1)
                if s < 2:
                    dve.tensor_copy(g.kcT[q:q + 64, 0:8, :], g.ps[q:q + 64, 6, 0:504].rearrange("p (a n) -> p a n", n=NCMP))
                    dve.tensor_copy(g.kcT[q:q + 64, 8, :], g.ps[q:q + 64, 7, 0:NCMP]).then_inc(c_out, 1)
                else:
                    dve.tensor_copy(g.vc[0:NCMP, 0:8, s % 2, :], g.ps[0:NCMP, 4, :].rearrange("p (a n) -> p a n", n=HD))
                    dve.tensor_copy(g.vc[0:NCMP, 8, s % 2, :], g.ps[0:NCMP, 5, 0:HD]).then_inc(c_out, 1)


def nsa_prompt(g, d):
    nc = g.nc
    items = [(t, h, part) for t in range(8) for h in range(8) for part in range(2)]

    def keys(t, part):
        return list(range(t + 1)) if part == 0 else list(range(max(0, t - 4), t + 1))

    chunks = []
    for t, h, part in items:
        n = len(keys(t, part)) + part
        chunks.append([(a, min(4, n - a)) for a in range(0, n, 4)])
    first = np.concatenate([[0], np.cumsum([len(c) for c in chunks])]).tolist()
    with ExitStack() as ctx:
        sem = lambda s: ctx.enter_context(nc.semaphore("na_" + s))
        sb = lambda s, shape: ctx.enter_context(nc.sbuf_tensor("na_" + s, shape, F32))
        prob = sb("prob", [P, 2, 1024])
        probT = sb("probT", [P, 2, 512])
        top = sb("top", [P, 2, 2])
        total = sb("total", [P, 4, 2])
        weight = sb("weight", [P, 2, 4])
        o = sb("o", [P, 2, 512])
        scored, maxed, expd, turned, moved = sem("scored"), sem("maxed"), sem("expd"), sem("turned"), sem("moved")
        summed, mixed, row_turned, row_out = sem("summed"), sem("mixed"), sem("row_turned"), sem("row_out")
        block = ctx.enter_context(nc.Block())

        @block.tensor
        def _(pe):
            def scores(i):
                t, h, part = items[i]
                q0 = 64 * (h // 4)
                q = g.qT[q0:q0 + 64, h % 4, t * P:t * P + P]
                b = 2 * (i % 2)
                if i >= 2:
                    pe.wait_ge(expd, i - 1)
                ks = keys(t, part)
                kset = 1 + part
                lo, n = ks[0] * P, len(ks) * P
                masks = {len(ks) - 1: g.causal}
                if part == 1 and t >= 4:
                    masks[0] = g.window
                for a in range(0, n, 512):
                    m = min(512, n - a)
                    inside = [j for j in masks if a <= j * P < a + m]
                    mm = pe.matmul(g.ps[:, b + a // 512, 0:m], q, g.kT[q0:q0 + 64, kset, lo + a:lo + a + m],
                                   start=True, stop=not inside)
                    for j in inside:
                        mm = pe.matmul(g.ps[:, b + a // 512, j * P - a:j * P - a + P], g.ident, masks[j], start=False,
                                       stop=(j == inside[-1]))
                if part == 1:
                    out = g.ps[:, b + 1, 256:256 + NCMP]
                    pe.matmul(out, q, g.kcT[q0:q0 + 64, 8, :], start=True, stop=False, skip_group_check=True)
                    mm = pe.matmul(out, g.ident, g.cmpmask[:, t, :], start=False, stop=True, skip_group_check=True)
                mm.then_inc(scored, 1)

            def values(i):
                t, h, part = items[i]
                ks = keys(t, part)
                pe.wait_ge(expd, i + 1)
                out = g.ps[:, 6, :]
                col = lambda j: 64 * (3 * (i // 2 % 2) + j)
                if part == 0 and i >= 4:
                    pe.wait_ge(mixed, i // 2 - 1)
                for c, (a, n) in enumerate(chunks[i]):
                    e = first[i] + c
                    if e >= 2:
                        pe.wait_ge(moved, e - 1)
                    for j in range(a, a + n):
                        if j < len(ks):
                            mm = pe.transpose(g.ps[:, 4 + e % 2, (j - a) * P:(j - a) * P + P], prob[:, i % 2, j * P:j * P + P], g.ident)
                        else:
                            mm = pe.transpose(g.ps[0:NCMP, 4 + e % 2, (j - a) * P:(j - a) * P + P], prob[:, i % 2, 768:768 + NCMP], g.ident)
                    mm.then_inc(turned, 1)
                    pe.wait_ge(moved, e + 1)
                    for j in range(a, a + n):
                        if j < len(ks):
                            v = g.vtok[:, ks[j], (1 + part) * P + 64 * (h // 4):(1 + part) * P + 64 * (h // 4) + 64]
                            mm = pe.matmul(out[:, col(part):col(part) + 64], probT[:, e % 2, (j - a) * P:(j - a) * P + P], v,
                                           start=(j == 0), stop=(j == len(ks) - 1), skip_group_check=True)
                        else:
                            mm = pe.matmul(out[:, col(2):col(2) + 64], probT[0:NCMP, e % 2, (j - a) * P:(j - a) * P + P],
                                           g.vc[0:NCMP, 8, h // 4, :], start=True, stop=True, skip_group_check=True)
                mm.then_inc(summed, 1)

            def turn_rows(t):
                pe.wait_ge(mixed, 8 * (t + 1))
                if t >= 1:
                    pe.wait_ge(row_out, t)
                for j in range(4):
                    mm = pe.transpose(g.ps[:, 7, j * P:j * P + P], o[:, t % 2, j * P:j * P + P], g.ident)
                mm.then_inc(row_turned, 1)

            scores(0)
            for i, (t, h, part) in enumerate(items):
                if i + 1 < len(items):
                    scores(i + 1)
                values(i)
                if h == 1 and part == 1 and t >= 1:
                    turn_rows(t - 1)
            turn_rows(7)

        @block.scalar
        def _(act):
            for i, (t, h, part) in enumerate(items):
                n = len(keys(t, part)) * P
                b = 2 * (i % 2)
                act.wait_ge(maxed, i + 1)
                if i >= 2:
                    act.wait_ge(summed, i - 1)
                if i >= 4:
                    act.wait_ge(mixed, i // 2 - 1)
                tot = total[:, 2 * (i // 2 % 2):2 * (i // 2 % 2) + 2, :]
                s = g.ps[:, b:b + 2, :].rearrange("p a n -> p (a n)")[:, 0:n]
                a = act.activation(prob[:, i % 2, 0:n], s, ACT.Exp, bias=top[:, i % 2, 0:1], scale=0.125, accum_out=tot[:, 0, part:part + 1])
                if part == 1:
                    a = act.activation(prob[:, 1, 768:768 + NCMP], g.ps[:, b + 1, 256:256 + NCMP], ACT.Exp, bias=top[:, i % 2, 1:2], scale=0.125,
                                       accum_out=tot[:, 1, 0:1])
                a.then_inc(expd, 1)

        @block.vector
        def _(dve):
            def maxima(i):
                t, h, part = items[i]
                n = len(keys(t, part)) * P
                b = 2 * (i % 2)
                dve.wait_ge(scored, i + 1)
                if i >= 2:
                    dve.wait_ge(expd, i - 1)
                s = g.ps[:, b:b + 2, :].rearrange("p a n -> p (a n)")[:, 0:n]
                dve.tensor_reduce(top[:, i % 2, 0:1], s, AX, ALU.max)
                if part == 1:
                    dve.tensor_reduce(top[:, i % 2, 1:2], g.ps[:, b + 1, 256:256 + NCMP], AX, ALU.max)
                dve.drain()
                dve.tensor_scalar(top[:, i % 2, 0:1 + part], top[:, i % 2, 0:1 + part], -0.125, None, ALU.mult).then_inc(maxed, 1)

            def move(i):
                for c, (a, n) in enumerate(chunks[i]):
                    e = first[i] + c
                    dve.wait_ge(turned, e + 1)
                    whole = n - (items[i][2] == 1 and a + n == len(keys(*items[i][::2])) + 1)
                    m = None
                    if whole:
                        m = dve.tensor_copy(probT[:, e % 2, 0:whole * P], g.ps[:, 4 + e % 2, 0:whole * P])
                    if whole < n:
                        m = dve.tensor_copy(probT[0:NCMP, e % 2, whole * P:n * P], g.ps[0:NCMP, 4 + e % 2, whole * P:n * P])
                    m.then_inc(moved, 1)

            def mix(i):
                t, h, _ = items[i]
                u = i // 2 % 2
                dve.wait_ge(expd, i + 1)
                dve.reciprocal(weight[:, u, 0:2], total[:, 2 * u, :])
                dve.reciprocal(weight[:, u, 2:3], total[:, 2 * u + 1, 0:1])
                dve.drain()
                dve.tensor_tensor(weight[:, u, 0:2], weight[:, u, 0:2], g.gates[:, t, 3 * h + 1:3 * h + 3], ALU.mult)
                if t == 0:
                    dve.scalar_tensor_tensor(weight[:, u, 2:3], weight[:, u, 2:3], g.seen, g.gates[:, t, 3 * h:3 * h + 1], ALU.mult, ALU.mult)
                else:
                    dve.tensor_tensor(weight[:, u, 2:3], weight[:, u, 2:3], g.gates[:, t, 3 * h:3 * h + 1], ALU.mult)
                dve.wait_ge(summed, i + 1)
                if h == 0 and t >= 2:
                    dve.wait_ge(row_turned, t - 1)
                dve.drain()
                out = o[:, t % 2, 64 * h:64 * h + 64]
                for j in range(3):
                    s = g.ps[:, 6, 64 * (3 * u + j):64 * (3 * u + j) + 64]
                    if j == 0:
                        m = dve.tensor_scalar(out, s, weight[:, u, 0:1], None, ALU.mult)
                    else:
                        dve.drain()
                        m = dve.scalar_tensor_tensor(out, s, weight[:, u, j:j + 1], out, ALU.mult, ALU.add)
                m.then_inc(mixed, 1)

            def rows_out(t):
                dve.wait_ge(row_turned, t + 1)
                dve.tensor_copy(g.act[:, 0:4, t * P:t * P + P], g.ps[:, 7, :].rearrange("p (a b) -> p a b", b=P)).then_inc(row_out, 1)

            maxima(0)
            for i, (t, h, part) in enumerate(items):
                if i + 1 < len(items):
                    maxima(i + 1)
                move(i)
                if part == 1:
                    mix(i)
                    if h == 1 and t >= 1:
                        rows_out(t - 1)
            rows_out(7)


def nsa_sample(g, d):
    nc = g.nc
    with ExitStack() as ctx:
        sem = lambda s: ctx.enter_context(nc.semaphore("ns_" + s))
        sb = lambda s, shape: ctx.enter_context(nc.sbuf_tensor("ns_" + s, shape, F32))
        past = [sb("past0", [P, 8, 2 * P]), sb("past1", [P, 8, 2 * P])]
        win = [sb("win0", [P, 4, 2 * P]), sb("win1", [P, 4, 2 * P])]
        newv = sb("newv", [SS, NB, 2 * P])
        gate = sb("gate", [P, 4, 3])
        qs = sb("qs", [P, NB, 32])
        prob = sb("prob", [P, 1536 + 80])
        probT = sb("probT", [P, 15, P])
        top = sb("top", [P, 3])
        total = sb("total", [P, 3])
        weight = sb("weight", [P, 3])
        imp = sb("imp", [P, 4, NSEL])
        least = sb("least", [P, 2])
        o = sb("o", [P, HD])
        oT = sb("oT", [HD, P])
        pt = ctx.enter_context(nc.sbuf_tensor("ns_pages", [1, NB * 8], I32))
        pt_here, small_here, gates_out, queries = sem("pt_here"), sem("small_here"), sem("gates_out"), sem("queries")
        past_here = [sem("past_here0"), sem("past_here1")]
        scored, maxed, cmp_exp, cmp_norm, cmp_turned, cmp_moved = (sem(s) for s in
            ("scored", "maxed", "cmp_exp", "cmp_norm", "cmp_turned", "cmp_moved"))
        imp_row, imp_moved, imp_sum, dropped, expd = (sem(s) for s in ("imp_row", "imp_moved", "imp_sum", "dropped", "expd"))
        turned, moved, summed, mixed, o_turned, o_out = (sem(s) for s in ("turned", "moved", "summed", "mixed", "o_turned", "o_out"))
        block = ctx.enter_context(nc.Block())

        @block.sync
        def _(sp):
            sp.dma_start(pt[:, :], d.pages).then_inc(pt_here, 16)
            sp.dma_start(newv[:, :, 0:2 * P], d.kv[NP:TOK, 512:768].rearrange("(b q) c -> q b c", q=SS)).then_inc(small_here, 16)
            sp.dma_start(d.gate_rows, g.gates[0:NS, 8, :]).then_inc(gates_out, 16)
            sp.wait_ge(gates_out, 16)
            for i in range(4):
                for b2 in range(2):
                    for h in range(8):
                        r0 = 64 * b2 + 8 * h
                        sp.dma_start(gate[r0:r0 + 8, i, :], d.gate_rows[(2 * i + b2) * 8:(2 * i + b2) * 8 + 8, 3 * h:3 * h + 3])\
                          .then_inc(small_here, 16)
            sp.wait_ge(pt_here, 16)
            for b in range(NB):
                if b >= 2:
                    sp.wait_ge(summed, b // 2)
                for i in range(8):
                    page = sp.value_load(pt[0:1, b * 8 + i:b * 8 + i + 1], min_val=0, max_val=79)
                    sp.dma_start(past[b % 2][:, i, :], d.cache_slc[ds(page, 1), :, :].rearrange("a p n -> (a p) n")).then_inc(past_here[b % 2], 16)
                sp.dma_start(win[b % 2][:, :, :], d.cache_win[b]).then_inc(past_here[b % 2], 16)

        @block.tensor
        def _(pe):
            def combos(i):
                for j in range(4):
                    b, gr = 2 * i + j // 2, j % 2
                    yield j, b, gr, qs[64 * gr:64 * gr + 64, b, :]

            pe.wait_ge(queries, 1)
            for i in range(4):
                for j, b, gr, q in combos(i):
                    if gr == 0:
                        pe.wait_ge(past_here[b % 2], 9 * 16 * (i + 1))
                    if i >= 1 and j == 0:
                        pe.wait_ge(expd, i)
                    rows = slice(32 * j, 32 * j + 32)
                    f = slice(64 * gr, 64 * gr + 64)
                    new = slice(NP + 8 * b, NP + 8 * b + 8)
                    for half in range(2):
                        pe.matmul(g.ps[rows, half, :].rearrange("p (a n) -> p a n", n=P), q, past[b % 2][f, 4 * half:4 * half + 4, 0:P],
                                  start=True, stop=True)
                    pe.matmul(g.ps[rows, 2, :].rearrange("p (a n) -> p a n", n=P), q, win[b % 2][f, :, 0:P], start=True, stop=True)
                    pe.matmul(g.ps[rows, 3, 0:8], q, g.kT[f, 1, new], start=True, stop=True, skip_group_check=True)
                    pe.matmul(g.ps[rows, 3, 8:16], q, g.kT[f, 2, new], start=True, stop=True, skip_group_check=True)
                    mm = pe.matmul(g.ps[rows, 3, 16:16 + NCMP], q, g.kcT[f, b, :], start=True, stop=True, skip_group_check=True)
                mm.then_inc(scored, 1)
                pe.wait_ge(cmp_norm, i + 1)
                if i >= 1:
                    pe.wait_ge(o_out, i)
                pe.transpose(g.ps[0:NCMP, 4, 0:P], prob[:, 1536 + 16:1536 + 16 + NCMP], g.ident).then_inc(cmp_turned, 1)
                pe.wait_ge(cmp_moved, i + 1)
                pe.matmul(g.ps[:, 5, 0:NSEL], probT[0:NCMP, 14, :], g.selmap[0:NCMP, :], start=True, stop=True).then_inc(imp_row, 1)
                pe.wait_ge(imp_moved, i + 1)
                pe.matmul(g.ps[:, 5, 64:64 + NSEL], g.samerow, imp[:, 0, :], start=True, stop=True, skip_group_check=True).then_inc(imp_sum, 1)
                pe.wait_ge(expd, i + 1)
                for a in range(14):
                    if a < 12:
                        mm = pe.transpose(g.ps[:, 4 + a // 4, (a % 4) * P:(a % 4) * P + P], prob[:, a * P:a * P + P], g.ident)
                    else:
                        c = 1536 + 8 * (a - 12)
                        mm = pe.transpose(g.ps[0:8, 7, (a - 12) * P:(a - 12) * P + P], prob[:, c:c + 8], g.ident)
                    if a == 11:
                        mm.then_inc(turned, 1)
                mm.then_inc(turned, 1)
                pe.wait_ge(moved, i + 1)
                for j, b, gr, q in combos(i):
                    rows = slice(32 * j, 32 * j + 32)
                    f = slice(64 * gr, 64 * gr + 64)
                    fv = slice(P + 64 * gr, P + 64 * gr + 64)
                    for a in range(8):
                        pe.matmul(g.ps[rows, 4, 0:64], probT[:, a, rows], past[b % 2][:, a, fv], start=(a == 0), stop=False)
                    pe.matmul(g.ps[rows, 4, 0:64], probT[0:8, 12, rows], newv[:, b, f], start=False, stop=True)
                    for a in range(4):
                        pe.matmul(g.ps[rows, 5, 0:64], probT[:, 8 + a, rows], win[b % 2][:, a, fv], start=(a == 0), stop=False)
                    pe.matmul(g.ps[rows, 5, 0:64], probT[0:8, 13, rows], newv[:, b, fv], start=False, stop=True)
                    mm = pe.matmul(g.ps[rows, 6, 0:64], probT[0:NCMP, 14, rows], g.vc[0:NCMP, b, gr, :], start=True, stop=True)
                mm.then_inc(summed, 1)
                pe.wait_ge(mixed, i + 1)
                pe.transpose(g.ps[0:64, 7, 256:256 + P], o[:, :], g.ident).then_inc(o_turned, 1)

        @block.scalar
        def _(act):
            for i in range(4):
                act.wait_ge(maxed, i + 1)
                act.activation(prob[:, 1552:1552 + NCMP], g.ps[:, 3, 16:16 + NCMP], ACT.Exp, bias=top[:, 2:3], scale=0.125,
                               accum_out=total[:, 2:3]).then_inc(cmp_exp, 1)
                act.wait_ge(dropped, i + 1)
                act.activation(prob[:, 0:1024], g.ps[:, 0:2, :].rearrange("p a n -> p (a n)"), ACT.Exp, bias=top[:, 0:1], scale=0.125)
                act.activation(prob[:, 1024:1536], g.ps[:, 2, :], ACT.Exp, bias=top[:, 1:2], scale=0.125)
                act.activation(prob[:, 1536:1544], g.ps[:, 3, 0:8], ACT.Exp, bias=top[:, 0:1], scale=0.125)
                act.activation(prob[:, 1544:1552], g.ps[:, 3, 8:16], ACT.Exp, bias=top[:, 1:2], scale=0.125).then_inc(expd, 1)

        @block.vector
        def _(dve):
            part = sb("part", [P, 4])
            dve.tensor_copy(qs[:, :, :].rearrange("p b (r q) -> p b r q", q=8),
                            g.qT[:, :, NP:TOK].rearrange("p r (b q) -> p b r q", q=8)).then_inc(queries, 1)
            for i in range(4):
                dve.wait_ge(scored, i + 1)
                dve.tensor_tensor(g.ps[:, 3, 0:8], g.ps[:, 3, 0:8], g.smask, ALU.add)
                dve.tensor_tensor(g.ps[:, 3, 8:16], g.ps[:, 3, 8:16], g.smask, ALU.add)
                dve.tensor_tensor(g.ps[:, 2, 0:8], g.ps[:, 2, 0:8], g.swmask, ALU.add)
                dve.tensor_reduce(top[:, 2:3], g.ps[:, 3, 16:16 + NCMP], AX, ALU.max)
                dve.drain()
                dve.tensor_reduce(part[:, 0:1], g.ps[:, 2, :], AX, ALU.max)
                dve.tensor_reduce(part[:, 1:2], g.ps[:, 3, 8:16], AX, ALU.max)
                dve.drain()
                dve.tensor_tensor(top[:, 1:2], part[:, 0:1], part[:, 1:2], ALU.max)
                dve.drain()
                dve.tensor_scalar(top[:, 1:3], top[:, 1:3], -0.125, None, ALU.mult).then_inc(maxed, 1)
                dve.wait_ge(cmp_exp, i + 1)
                dve.reciprocal(weight[:, 2:3], total[:, 2:3])
                dve.drain()
                c = prob[:, 1552:1552 + NCMP]
                dve.tensor_scalar(c, c, weight[:, 2:3], None, ALU.mult).then_inc(cmp_norm, 1)
                dve.wait_ge(cmp_turned, i + 1)
                dve.tensor_copy(probT[0:NCMP, 14, :], g.ps[0:NCMP, 4, 0:P]).then_inc(cmp_moved, 1)
                dve.wait_ge(imp_row, i + 1)
                dve.tensor_copy(imp[:, 0, :], g.ps[:, 5, 0:NSEL]).then_inc(imp_moved, 1)
                dve.wait_ge(imp_sum, i + 1)
                dve.tensor_copy(imp[:, 1, :], g.ps[:, 5, 64:64 + NSEL])
                dve.drain()
                dve.tensor_reduce(least[:, 0:1], imp[:, 1, 1:15], AX, ALU.min)
                dve.drain()
                dve.scalar_tensor_tensor(imp[:, 2, 1:15], imp[:, 1, 1:15], least[:, 0:1], g.blkid[:, 1:15], ALU.is_equal, ALU.mult)
                dve.drain()
                dve.tensor_reduce(least[:, 1:2], imp[:, 2, 1:15], AX, ALU.max)
                dve.drain()
                dve.tensor_scalar(imp[:, 3, 0:16], g.blkid[:, 0:16], least[:, 1:2], NEG, ALU.is_equal, ALU.mult)
                dve.drain()
                s = g.ps[:, 0:2, :].rearrange("p a (m n) -> p (a m) n", n=64)
                dve.tensor_tensor(s, s, imp[:, 3, 0:16].unsqueeze(2).to_broadcast([P, 16, 64]), ALU.add)
                dve.drain()
                dve.tensor_reduce(part[:, 0:1], g.ps[:, 0:2, :].rearrange("p a n -> p (a n)"), AX, ALU.max)
                dve.tensor_reduce(part[:, 1:2], g.ps[:, 3, 0:8], AX, ALU.max)
                dve.drain()
                dve.tensor_tensor(top[:, 0:1], part[:, 0:1], part[:, 1:2], ALU.max)
                dve.drain()
                dve.tensor_scalar(top[:, 0:1], top[:, 0:1], -0.125, None, ALU.mult).then_inc(dropped, 1)
                dve.wait_ge(expd, i + 1)
                dve.tensor_reduce(part[:, 0:1], prob[:, 0:1024], AX, ALU.add)
                dve.tensor_reduce(part[:, 1:2], prob[:, 1024:1536], AX, ALU.add)
                dve.tensor_reduce(part[:, 2:4], prob[:, 1536:1552].rearrange("p (a b) -> p a b", b=8), AX, ALU.add)
                dve.drain()
                dve.tensor_tensor(total[:, 0:2], part[:, 0:2], part[:, 2:4], ALU.add)
                dve.drain()
                dve.reciprocal(weight[:, 0:2], total[:, 0:2])
                dve.wait_ge(turned, 2 * i + 1)
                dve.tensor_copy(probT[:, 0:12, :], g.ps[:, 4:7, :].rearrange("p a (b n) -> p (a b) n", n=P))
                dve.wait_ge(turned, 2 * i + 2)
                dve.tensor_copy(probT[0:8, 12:14, :], g.ps[0:8, 7, 0:256].rearrange("p (b n) -> p b n", n=P)).then_inc(moved, 1)
                if i == 0:
                    dve.wait_ge(small_here, 65 * 16)
                dve.drain()
                dve.tensor_tensor(weight[:, 0:2], weight[:, 0:2], gate[:, i, 1:3], ALU.mult)
                dve.wait_ge(summed, i + 1)
                dve.drain()
                dve.tensor_scalar(o[:, :], g.ps[:, 4, 0:64], weight[:, 0:1], None, ALU.mult)
                dve.drain()
                dve.scalar_tensor_tensor(o[:, :], g.ps[:, 5, 0:64], weight[:, 1:2], o[:, :], ALU.mult, ALU.add)
                dve.drain()
                dve.scalar_tensor_tensor(o[:, :], g.ps[:, 6, 0:64], gate[:, i, 0:1], o[:, :], ALU.mult, ALU.add).then_inc(mixed, 1)
                dve.wait_ge(o_turned, i + 1)
                for gr in range(2):
                    for r in range(4):
                        h = 4 * gr + r
                        src = g.ps[0:64, 7, 256:256 + P].rearrange("p (b s) -> p b s", b=2)[:, :, 8 * h:8 * h + 8]
                        dst = g.act[64 * (h % 2):64 * (h % 2) + 64, h // 2, NP + 16 * i:NP + 16 * i + 16].rearrange("p (b s) -> p b s", b=2)
                        m = dve.tensor_copy(dst, src)
                m.then_inc(o_out, 1)


def nsa_layer_buffers(g, ctx):
    sb = lambda name, shape: ctx.enter_context(g.nc.sbuf_tensor(name, shape, F32))
    g.qT = sb("qT", [P, 4, TOK])
    g.kT = sb("kT", [P, KSETS, TOK])
    g.vtok = sb("vtok", [P, 9, KSETS * P])
    g.gates = sb("gates", [P, 9, 24])
    g.kcT = sb("kcT", [P, 9, NCMP])
    g.vc = sb("vc", [P, 9, 2, HD])


RWKV_GROUPS = [(0, 4), (4, 4), (8, 4), (12, 4), (16, 1)]


def rwkv_mix(g, d):
    nc = g.nc
    with ExitStack() as ctx:
        sb = lambda s, shape: ctx.enter_context(nc.sbuf_tensor("rw_" + s, shape, F32))
        b = names(
            w=[sb("w0", [P, KT, P]), sb("w1", [P, KT, P])],
            lora=sb("lora", [P, 2, TOK]),
            lw=sb("lw", [P, 2, 512]),
            shift=sb("shift", [P, RT, NB]), last=sb("last", [P, RT, 9]),
            raw=sb("raw", [P, TOK]),
            r=sb("r", [P, TOK]), k=sb("k", [P, TOK]), v=sb("v", [P, TOK]),
            ar=sb("ar", [P, 17, 2, 64]),
            bt=sb("bt", [P, TOK]), kt=sb("kt", [P, TOK]), cum=sb("cum", [P, TOK]),
            lw_=sb("logw", [P, TOK]), a=sb("a", [P, TOK]), e=sb("e", [P, TOK]), kk=sb("kkn", [P, TOK]),
            bonus=sb("bonus", [P, TOK]), y=sb("y", [P, TOK]),
            endp=sb("endp", [P, 16 + NB]),
            tok=sb("tok", [P, 4, 4, 64]),
            tri=sb("tri", [P, 4, 4, 64]),
            low=sb("low", [P, 4, 64]), up=sb("up", [P, 4, 2, 64]),
            wg=sb("wg", [P, 4, 2, 64]),
            u=sb("u", [P, 64]), st=sb("st", [P, 64]), st8=sb("st8", [P, NB, 64]),
            m8=sb("m8", [P, 3, NB, 64]),
        )
        s = signals(nc, ctx, "rw_", "product raw_ready mixed_in za_ready kk_squared kk_summed kk_root "
                    "log_ready a_ready decay decay_read bonus_in bonus_sum scored masked tokens powers "
                    "wg_ready wg_out u_ready u_out y_ready y_out s_ready s_out m8_s centered mean_ready sq_ready var_ready var_root gated")
        w_here = [ctx.enter_context(nc.semaphore("rw_w_here0")), ctx.enter_context(nc.semaphore("rw_w_here1"))]
        small, st_here, stored = (ctx.enter_context(nc.semaphore("rw_" + n)) for n in ("small", "st_here", "stored"))
        for i in range(2):
            rwkv_features(g, d, b, s, i, w_here, small)
        for j in range(4):
            for i in range(2 + 3 * j, 5 + 3 * j):
                rwkv_features(g, d, b, s, i, w_here, small)
            rwkv_prepare(g, d, b, s, j, st_here)
            rwkv_chunks(g, d, b, s, j, st_here, stored)
            rwkv_finish(g, d, b, s, j, stored)
        with ExitStack() as c2:
            block = c2.enter_context(nc.Block())

            @block.sync
            def _(sp):
                sp.dma_start(d.last, b.last[:, :, :]).then_inc(small, 16)
                sp.wait_ge(small, 48)


def rwkv_features(g, d, b, s, i, w_here, small):
    nc = g.nc
    out = b.lora[:, i, :] if i < 2 else (b.r, b.k, b.v)[(i - 2) % 3][:, :]
    t = b.cum[:, :] if i < 2 else b.e[:, :]
    with nc.Block() as block:
        @block.sync
        def _(sp):
            if i == 0:
                sp.dma_start(b.lw[:, :, :].rearrange("p a n -> p (a n)"), d.lora).then_inc(small, 16)
                sp.dma_start(b.shift[:, :, :], d.shift).then_inc(small, 16)
                sp.dma_start(b.w[0][:, :, :], d.w_rwkv[0]).then_inc(w_here[0], 16)
            if i + 1 < RT:
                sp.dma_start(b.w[(i + 1) % 2][:, :, :], d.w_rwkv[i + 1]).then_inc(w_here[(i + 1) % 2], 16)

        @block.tensor
        def _(pe):
            pe.wait_ge(w_here[i % 2], 16 * (i // 2 + 1))
            for k in range(KT):
                for c, (o, n) in enumerate(CH):
                    mm = pe.matmul(g.ps[:, c, 0:n], b.w[i % 2][:, k, :], g.act[:, k, o:o + n], start=(k == 0), stop=(k == KT - 1))
            s.product.mark(mm)

        @block.scalar
        def _(act):
            s.product.next(act)
            for c, (o, n) in enumerate(CH):
                a = act.activation(b.raw[:, o:o + n], g.ps[:, c, 0:n], ACT.Copy)
            s.raw_ready.mark(a)
            if i < 2:
                s.mixed_in.next(act)
                if i == 0:
                    act.activation(b.lora[0:64, 0, :], b.lora[0:64, 0, :], ACT.Tanh)
                else:
                    act.activation(b.lora[:, 1, :], b.lora[:, 1, :], ACT.Sigmoid)

        @block.vector
        def _(dve):
            s.raw_ready.next(dve)
            if i == 0:
                dve.wait_ge(small, 32)
            x = b.raw
            x8 = x[:, NP:TOK].rearrange("p (b q) -> p b q", q=SS)
            t8 = t[:, NP:TOK].rearrange("p (b q) -> p b q", q=SS)
            dve.tensor_tensor(t[:, 1:NP], x[:, 0:NP - 1], x[:, 1:NP], ALU.subtract)
            dve.tensor_scalar(t[:, 0:1], x[:, 0:1], -1.0, None, ALU.mult)
            dve.tensor_tensor(t8[:, :, 1:8], x8[:, :, 0:7], x8[:, :, 1:8], ALU.subtract)
            dve.tensor_tensor(t8[:, :, 0:1], b.shift[:, i, :].unsqueeze(2), x8[:, :, 0:1], ALU.subtract)
            dve.tensor_copy(b.last[:, i, 0:8].unsqueeze(2), x8[:, :, 7:8])
            dve.tensor_copy(b.last[:, i, 8:9], x[:, NP - 1:NP])
            dve.drain()
            m = dve.scalar_tensor_tensor(out, t, g.col["mu"][:, i:i + 1], x[:, :], ALU.mult, ALU.add)
            if i < 2:
                s.mixed_in.mark(m)


def rwkv_prepare(g, d, b, s, j, st_here):
    nc = g.nc
    col = lambda name: g.col[name][:, j:j + 1]
    pj = slice(P * j, P * j + P)
    ps3 = lambda first: [(g.ps[:, first + c, 0:n], o, n) for c, (o, n) in enumerate(CH)]
    with nc.Block() as block:
        @block.sync
        def _(sp):
            sp.dma_start(b.st8[:, :, :], d.srwkv[j]).then_inc(st_here, 16)

        @block.tensor
        def _(pe):
            for p, o, n in ps3(0):
                pe.matmul(p, b.lw[0:64, 0, pj], b.lora[0:64, 0, o:o + n], start=True, stop=True)
            for p, o, n in ps3(3):
                mm = pe.matmul(p, b.lw[64:P, 0, pj], b.lora[64:P, 0, o:o + n], start=True, stop=True)
            s.za_ready.mark(mm)
            s.kk_squared.next(pe)
            s.a_ready.next(pe)
            for p, o, n in ps3(0):
                mm = pe.matmul(p, g.blk, b.e[:, o:o + n], start=True, stop=True)
            s.kk_summed.mark(mm)
            s.bonus_in.next(pe)
            for p, o, n in ps3(3):
                mm = pe.matmul(p, g.blk, b.y[:, o:o + n], start=True, stop=True)
            s.bonus_sum.mark(mm)

        @block.scalar
        def _(act):
            s.za_ready.next(act)
            for p, o, n in ps3(0):
                a = act.activation(b.lw_[:, o:o + n], p, ACT.Sigmoid, bias=col("w0"))
            s.log_ready.mark(a)
            for p, o, n in ps3(3):
                a = act.activation(b.a[:, o:o + n], p, ACT.Sigmoid, bias=col("a0"))
            s.a_ready.mark(a)
            s.kk_root.next(act)
            s.sq_ready.mark(act.activation(b.e[:, :], b.e[:, :], ACT.Sqrt))
            s.decay_read.next(act)
            s.decay.mark(act.activation(b.e[:, :], b.e[:, :], ACT.Exp))
            s.decay_read.next(act)
            s.decay.mark(act.activation(b.e[:, :], b.cum[:, :], ACT.Exp, scale=-1.0))
            s.decay_read.next(act)
            s.decay.mark(act.activation(b.e[:, :], b.cum[:, :], ACT.Exp))

        @block.vector
        def _(dve):
            ar = lambda which: (b.ar[:, :, which, :])
            chunked = lambda x: x.rearrange("p (c t) -> p c t", t=64)
            dve.tensor_scalar(b.kk[:, :], b.k[:, :], col("kk"), None, ALU.mult)
            dve.drain()
            s.log_ready.next(dve)
            s.kk_squared.mark(dve.tensor_tensor(b.e[:, :], b.kk[:, :], b.kk[:, :], ALU.mult))
            dve.tensor_scalar(b.lw_[:, :], b.lw_[:, :], -float(np.exp(-0.5)), None, ALU.mult)
            dve.drain()
            dve.tensor_tensor_scan(b.cum[:, :], g.scan, b.lw_[:, :], 0.0, ALU.mult, ALU.add)
            s.kk_summed.next(dve)
            for p, o, n in ps3(0):
                m = dve.tensor_scalar(b.e[:, o:o + n], p, 1e-24, None, ALU.max)
            s.kk_root.mark(m)
            dve.tensor_scalar(b.raw[:, :], b.a[:, :], 1.0, col("ka"), ALU.subtract, ALU.mult)
            dve.drain()
            dve.scalar_tensor_tensor(b.k[:, :], b.raw[:, :], 1.0, b.k[:, :], ALU.add, ALU.mult)
            dve.drain()
            s.bonus_in.mark(dve.scalar_tensor_tensor(b.y[:, :], b.k[:, :], col("rk"), b.r[:, :], ALU.mult, ALU.mult))
            s.sq_ready.next(dve)
            dve.reciprocal(b.e[:, :], b.e[:, :])
            dve.drain()
            dve.tensor_tensor(b.kk[:, :], b.kk[:, :], b.e[:, :], ALU.mult)
            dve.drain()
            s.decay_read.mark(dve.tensor_tensor(b.e[:, :], b.cum[:, :], b.lw_[:, :], ALU.subtract))
            s.bonus_sum.next(dve)
            for p, o, n in ps3(3):
                dve.tensor_tensor(b.bonus[:, o:o + n], p, b.v[:, o:o + n], ALU.mult)
            s.decay.next(dve)
            s.decay_read.mark(dve.scalar_tensor_tensor(ar(0), chunked(b.kk[:, :]), -1.0, chunked(b.e[:, :]), ALU.mult, ALU.mult))
            dve.tensor_tensor(b.kk[:, :], b.kk[:, :], b.a[:, :], ALU.mult)
            s.decay.next(dve)
            dve.drain()
            dve.tensor_tensor(b.bt[:, :], b.kk[:, :], b.e[:, :], ALU.mult)
            s.decay_read.mark(dve.tensor_tensor(b.kt[:, :], b.k[:, :], b.e[:, :], ALU.mult))
            s.decay.next(dve)
            dve.tensor_tensor(ar(1), chunked(b.r[:, :]), chunked(b.e[:, :]), ALU.mult)
            dve.tensor_copy(b.endp[:, 0:16].unsqueeze(2), chunked(b.e[:, 0:NP])[:, :, 63:64])
            dve.tensor_copy(b.endp[:, 16:24].unsqueeze(2), b.e[:, NP:TOK].rearrange("p (b q) -> p b q", q=SS)[:, :, 7:8])


def rwkv_chunks(g, d, b, s, j, st_here, stored):
    nc = g.nc
    halves = [slice(0, 64), slice(64, P)]
    with nc.Block() as block:
        @block.tensor
        def _(pe):
            for c0, n in RWKV_GROUPS:
                sampled = c0 == 16
                for c in range(n):
                    t = slice(64 * (c0 + c), 64 * (c0 + c) + 64)
                    for h in halves:
                        at, art = b.ar[h, c0 + c, 0, :], b.ar[h, c0 + c, :, :].rearrange("p a t -> p (a t)")
                        tri = g.ps[h, c // 2, 256 * (c % 2):256 * (c % 2) + 256]
                        pe.matmul(tri[:, 0:P], b.bt[h, t], art, start=True, stop=True)
                        pe.matmul(tri[:, P:2 * P], b.kt[h, t], art, start=True, stop=True)
                        pe.matmul(g.ps[h, 2, 64 * c:64 * c + 64], at, b.bt[h, t], start=True, stop=True)
                        for x, src in enumerate((at, b.bt[h, t], b.kt[h, t], b.v[h, t])):
                            o = 256 * (c % 2) + 64 * x
                            mm = pe.matmul(g.ps[h, 3 + c // 2, o:o + 64], src, g.id2[h, :], start=True, stop=True)
                s.scored.mark(mm)
                for level in range(6):
                    s.masked.next(pe)
                    for c in range(n):
                        for h in halves:
                            low, up = b.low[h, c, :], b.up[h, c, :, :].rearrange("p a t -> p (a t)")
                            mm = pe.matmul(g.ps[h, 5, P * c:P * c + P], low, up, start=True, stop=True)
                            if level < 5:
                                mm = pe.matmul(g.ps[h, 6, 64 * c:64 * c + 64], b.up[h, c, 0, :], low, start=True, stop=True)
                    s.powers.mark(mm)
                s.masked.next(pe)
                s.tokens.next(pe)
                for c in range(n):
                    for h in halves:
                        pe.matmul(g.ps[h, 5, P * c:P * c + 64], b.tok[h, c, 0, :], b.up[h, c, 1, :], start=True, stop=True)
                        mm = pe.matmul(g.ps[h, 5, P * c + 64:P * c + P], b.tri[h, c, 2, :], b.tok[h, c, 3, :], start=True, stop=True)
                s.wg_ready.mark(mm)
                s.wg_out.next(pe)
                for c in range(n):
                    for h in halves:
                        pu = g.ps[h, 6, 0:64]
                        pe.matmul(pu, b.up[h, c, 1, :], b.wg[h, c, 1, :], start=True, stop=False)
                        if sampled:
                            for q in range(NB):
                                mm = pe.matmul(pu, b.m8[h, 0, q, :], b.st8[h, q, :], start=False, stop=(q == NB - 1))
                        else:
                            mm = pe.matmul(pu, b.wg[h, c, 0, :], b.st[h, :], start=False, stop=True)
                    s.u_ready.mark(mm)
                    s.u_out.next(pe)
                    for h in halves:
                        if sampled:
                            for q in range(NB):
                                ps = g.ps[h, 2, 64 * q:64 * q + 64]
                                pe.matmul(ps, b.m8[h, 2, q, :], b.u[h, :], start=True, stop=False)
                                pe.matmul(ps, b.m8[h, 1, q, :], b.tok[h, c, 3, :], start=False, stop=False)
                                mm = pe.matmul(ps, g.id2[h, :], b.st8[h, q, :], start=False, stop=True)
                        else:
                            ps = g.ps[h, 2, 0:64]
                            pe.matmul(ps, b.tok[h, c, 1, :], b.u[h, :], start=True, stop=False)
                            pe.matmul(ps, b.tok[h, c, 2, :], b.tok[h, c, 3, :], start=False, stop=False)
                            mm = pe.matmul(ps, g.id2[h, :], b.st[h, :], start=False, stop=True)
                    s.s_ready.mark(mm)
                    if sampled:
                        s.m8_s.next(pe)
                    for h in halves:
                        py = g.ps[h, 7, 64 * c:64 * c + 64]
                        pe.matmul(py, b.u[h, :], b.tri[h, c, 1, :], start=True, stop=False)
                        pe.matmul(py, b.tok[h, c, 3, :], b.tri[h, c, 3, :], start=False, stop=False)
                        if sampled:
                            for q in range(NB):
                                mm = pe.matmul(py, b.st8[h, q, :], b.m8[h, 1, q, :], start=False, stop=(q == NB - 1))
                        else:
                            mm = pe.matmul(py, b.st[h, :], b.ar[h, c0 + c, 1, :], start=False, stop=True)
                    s.y_ready.mark(mm)
                    s.s_out.next(pe)
                s.y_out.next(pe)

        @block.scalar
        def _(act):
            for c0, n in RWKV_GROUPS:
                s.scored.next(act)
                for q in range(0, n, 2):
                    m = min(2, n - q)
                    a = act.activation(b.tok[:, q:q + m, :, :].rearrange("p a x t -> p (a x t)"), g.ps[:, 3 + q // 2, 0:256 * m], ACT.Copy)
                s.tokens.mark(a)
                s.y_ready.next(act, n)
                s.y_out.mark(act.activation(b.y[:, 64 * c0:64 * (c0 + n)], g.ps[:, 7, 0:64 * n], ACT.Copy))

        @block.vector
        def _(dve):
            dve.memset(b.st[:, :], 0.0)
            dve.wait_ge(st_here, 16 * (j + 1))
            for c0, n in RWKV_GROUPS:
                sampled = c0 == 16
                above, upto, below = (g.above8, g.upto8, g.below8) if sampled else (g.above, g.upto, g.below)
                over = lambda m: m.unsqueeze(1).to_broadcast([P, n, 64])
                s.scored.next(dve)
                tri = g.ps[:, 0:2, :].rearrange("p a (c x t) -> p (a c) x t", x=4, t=64)[:, 0:n]
                for x, m in enumerate((above, upto, above, upto)):
                    dve.tensor_tensor(b.tri[:, 0:n, x, :], tri[:, :, x, :], over(m), ALU.mult)
                dve.tensor_tensor(b.up[:, 0:n, 0, :], tri[:, :, 0, :], over(above), ALU.mult)
                dve.tensor_copy(b.up[:, 0:n, 1, :], over(g.id2))
                s.masked.mark(dve.tensor_tensor(b.low[:, 0:n, :], g.ps[:, 2, 0:64 * n].rearrange("p (c t) -> p c t", t=64), over(below), ALU.mult))
                for level in range(6):
                    s.powers.next(dve)
                    up = g.ps[:, 5, 0:P * n].rearrange("p (c x t) -> p c x t", x=2, t=64)
                    m = dve.tensor_tensor(b.up[:, 0:n, 1, :], b.up[:, 0:n, 1, :], up[:, :, 1, :], ALU.add)
                    if level < 5:
                        dve.tensor_copy(b.up[:, 0:n, 0, :], up[:, :, 0, :])
                        m = dve.tensor_copy(b.low[:, 0:n, :], g.ps[:, 6, 0:64 * n].rearrange("p (c t) -> p c t", t=64))
                    s.masked.mark(m)
                s.wg_ready.next(dve)
                m = dve.tensor_copy(b.wg[:, 0:n, :, :].rearrange("p c x t -> p (c x t)"), g.ps[:, 5, 0:P * n])
                if sampled:
                    dve.drain()
                    eight = lambda x: x.unsqueeze(1).to_broadcast([P, NB, 64])
                    rows = g.brow.unsqueeze(2).to_broadcast([P, NB, 64])
                    dve.tensor_tensor(b.m8[:, 0, :, :], eight(b.wg[:, 0, 0, :]), g.bcol, ALU.mult)
                    dve.tensor_tensor(b.m8[:, 1, :, :], eight(b.tok[:, 0, 2, :]), rows, ALU.mult)
                    m = dve.tensor_tensor(b.m8[:, 2, :, :], eight(b.tok[:, 0, 1, :]), rows, ALU.mult)
                s.wg_out.mark(m)
                for c in range(n):
                    s.u_ready.next(dve)
                    s.u_out.mark(dve.tensor_copy(b.u[:, :], g.ps[:, 6, 0:64]))
                    s.s_ready.next(dve)
                    if sampled:
                        s.m8_s.mark(dve.tensor_tensor(b.m8[:, 1, :, :], eight(b.ar[:, 16, 1, :]), g.bcol, ALU.mult))
                        s.y_ready.next(dve)
                        m = dve.tensor_tensor(b.st8[:, :, :], g.ps[:, 2, :].rearrange("p (q t) -> p q t", t=64),
                                              b.endp[:, 16:24].unsqueeze(2).to_broadcast([P, NB, 64]), ALU.mult)
                    else:
                        s.y_ready.next(dve)
                        m = dve.tensor_scalar(b.st[:, :], g.ps[:, 2, 0:64], b.endp[:, c0 + c:c0 + c + 1], None, ALU.mult)
                    s.s_out.mark(m)

        @block.sync
        def _(sp):
            s.s_out.next(sp, 17)
            sp.dma_start(d.rw_p[j], b.st[:, :]).then_inc(stored, 16)
            sp.dma_start(d.rw_s[j], b.st8[:, :, :]).then_inc(stored, 16)
            sp.wait_ge(stored, 48 * j + 32)


def rwkv_finish(g, d, b, s, j, stored):
    nc = g.nc
    col = lambda name: g.col[name][:, j:j + 1]
    ps3 = lambda first: [(g.ps[:, first + c, 0:n], o, n) for c, (o, n) in enumerate(CH)]
    with nc.Block() as block:
        @block.tensor
        def _(pe):
            for p, o, n in ps3(0):
                mm = pe.matmul(p, g.blk, b.y[:, o:o + n], start=True, stop=True)
            s.mean_ready.mark(mm)
            for p, o, n in ps3(3):
                mm = pe.matmul(p, b.lw[:, 1, P * j:P * j + P], b.lora[:, 1, o:o + n], start=True, stop=True)
            s.centered.next(pe)
            for p, o, n in ps3(0):
                mm = pe.matmul(p, g.blk, b.e[:, o:o + n], start=True, stop=True)
            s.var_ready.mark(mm)

        @block.scalar
        def _(act):
            s.var_ready.next(act)
            for p, o, n in ps3(0):
                a = act.activation(b.cum[:, o:o + n], p, ACT.Sqrt, bias=g.col["gneps"], scale=1.0 / HD)
            s.var_root.mark(a)

        @block.vector
        def _(dve):
            s.mean_ready.next(dve)
            for p, o, n in ps3(0):
                dve.scalar_tensor_tensor(b.y[:, o:o + n], p, -1.0 / HD, b.y[:, o:o + n], ALU.mult, ALU.add)
            dve.drain()
            s.centered.mark(dve.tensor_tensor(b.e[:, :], b.y[:, :], b.y[:, :], ALU.mult))
            s.var_root.next(dve)
            dve.reciprocal(b.cum[:, :], b.cum[:, :])
            dve.drain()
            dve.tensor_tensor(b.y[:, :], b.y[:, :], b.cum[:, :], ALU.mult)
            dve.drain()
            dve.tensor_scalar(b.y[:, :], b.y[:, :], col("lnw"), col("lnb"), ALU.mult, ALU.add)
            dve.drain()
            dve.tensor_tensor(b.y[:, :], b.y[:, :], b.bonus[:, :], ALU.add)
            dve.drain()
            for p, o, n in ps3(3):
                m = dve.tensor_tensor(b.y[:, o:o + n], b.y[:, o:o + n], p, ALU.mult)
            s.gated.mark(m)

        @block.sync
        def _(sp):
            s.gated.next(sp)
            sp.dma_start(d.rwkv_out[:, j, :], b.y[:, :]).then_inc(stored, 16)
            sp.wait_ge(stored, 48 * (j + 1))


def gla_mix(g, d):
    nc = g.nc
    with ExitStack() as ctx:
        sb = lambda s, shape: ctx.enter_context(nc.sbuf_tensor("gl_" + s, shape, F32))
        b = names(
            wq=sb("wq", [P, KT, P]), wk=sb("wk", [P, KT, P]), wv=sb("wv", [P, KT, 256]), wgd=sb("wgd", [P, KT, 16]),
            up=sb("up", [16, 512]), gd=sb("gd", [16, TOK]),
            q=sb("q", [P, TOK]), k=sb("k", [P, TOK]), v=sb("v", [P, 9, 256]), cum=sb("cum", [P, TOK]), e=sb("e", [P, TOK]),
            qs=sb("qs", [P, TOK]), ks=sb("ks", [P, TOK]), qe=sb("qe", [P, TOK]), kd=sb("kd", [P, TOK]),
            ref=sb("ref", [P, 2, 24]), dec=sb("dec", [P, 24]),
            at=sb("at", [P, 2, 64]), kt=sb("kt", [P, 2, P]), kt8=sb("kt8", [NS, NB, P]),
            st=sb("st", [P, 4, 256]), st8=sb("st8", [P, NB, 256]), o=sb("o", [P, 2, TOK]))
        s = signals(nc, ctx, "gl_", "gd_ready gd_out product q_out v_ready v_out logit x_ready soft cum_ready exp_ready exp_read scored turned_out "
                    "outer state o_ready o_out squared mean_ready root r_ready r_out gated")
        here, v_here, st_here, stored = (ctx.enter_context(nc.semaphore("gl_" + n)) for n in ("here", "v_here", "st_here", "stored"))
        with nc.Block() as block:
            @block.sync
            def _(sp):
                sp.dma_start(b.wgd[:, :, :], d.w_gla_gd).then_inc(here, 16)
                sp.dma_start(b.up[:, :], d.gate_up).then_inc(here, 16)

            @block.tensor
            def _(pe):
                pe.wait_ge(here, 32)
                for k in range(KT):
                    for c, (o, n) in enumerate(CH):
                        mm = pe.matmul(g.ps[0:16, c, 0:n], b.wgd[:, k, :], g.act[:, k, o:o + n], start=(k == 0), stop=(k == KT - 1))
                s.gd_ready.mark(mm)

            @block.scalar
            def _(act):
                s.gd_ready.next(act)
                for c, (o, n) in enumerate(CH):
                    act.activation(b.gd[:, o:o + n], g.ps[0:16, c, 0:n], ACT.Copy)
        for h in range(4):
            gla_project(g, d, b, s, h, here, v_here, st_here)
            gla_chunks(g, d, b, s, h, stored)
            gla_finish(g, d, b, s, h, here, stored)


def gla_project(g, d, b, s, h, here, v_here, st_here):
    nc = g.nc
    ps3 = lambda first: [(g.ps[:, first + c, 0:n], o, n) for c, (o, n) in enumerate(CH)]
    with nc.Block() as block:
        @block.sync
        def _(sp):
            sp.dma_start(b.wk[:, :, :], d.w_gla_qk[4 + h]).then_inc(here, 16)
            sp.dma_start(b.wq[:, :, :], d.w_gla_qk[h]).then_inc(here, 16)
            sp.dma_start(b.wv[:, :, :], d.w_gla_v[h]).then_inc(v_here, 16)
            sp.dma_start(b.st8[:, :, :], d.sgla[h]).then_inc(st_here, 16)
            sp.wait_ge(st_here, 16 * (h + 1))

        @block.tensor
        def _(pe):
            for p, o, n in ps3(0):
                mm = pe.matmul(p, b.up[:, h * P:h * P + P], b.gd[:, o:o + n], start=True, stop=True)
            s.logit.mark(mm)
            pe.wait_ge(here, 32 + 64 * h + 32)
            for w, first in ((b.wk, 3), (b.wq, 0)):
                if first == 0:
                    s.x_ready.next(pe)
                for k in range(KT):
                    for p, o, n in ps3(first):
                        mm = pe.matmul(p, w[:, k, :], g.act[:, k, o:o + n], start=(k == 0), stop=(k == KT - 1))
                s.product.mark(mm)
            pe.wait_ge(v_here, 16 * (h + 1))
            for t in range(9):
                R = P if t < 8 else NS
                if t >= 2:
                    s.v_out.next(pe)
                for k in range(KT):
                    mm = pe.matmul(g.ps[0:R, 6 + t % 2, 0:256], g.act[:, k, t * P:t * P + R], b.wv[:, k, :], start=(k == 0), stop=(k == KT - 1))
                s.v_ready.mark(mm)
            s.v_out.next(pe, 2)

        @block.scalar
        def _(act):
            s.x_ready.next(act)
            act.activation(b.e[:, :], b.cum[:, :], ACT.Abs)
            act.drain()
            act.activation(b.e[:, :], b.e[:, :], ACT.Exp, scale=-1.0)
            act.drain()
            s.soft.mark(act.activation(b.e[:, :], b.e[:, :], ACT.Ln, bias=g.ones[:, 0:1]))
            for x in (b.k, b.q):
                s.product.next(act)
                for p, o, n in ps3(3 if x is b.k else 0):
                    a = act.activation(x[:, o:o + n], p, ACT.Copy, scale=1.0 if x is b.k else float(P) ** -0.5)
            s.q_out.mark(a)
            for t in range(9):
                R = P if t < 8 else NS
                s.v_ready.next(act)
                s.v_out.mark(act.activation(b.v[0:R, t, :], g.ps[0:R, 6 + t % 2, 0:256], ACT.Copy))
            for i in range(4):
                s.cum_ready.next(act)
                s.exp_ready.mark(act.activation(b.e[:, :], b.e[:, :], ACT.Exp))
            act.activation(b.dec[:, :], b.ref[:, 1, :], ACT.Exp)

        @block.vector
        def _(dve):
            s.logit.next(dve)
            for p, o, n in ps3(0):
                m = dve.tensor_scalar(b.cum[:, o:o + n], p, g.col["gb"][:, h:h + 1], None, ALU.add)
            s.x_ready.mark(m)
            dve.drain()
            dve.tensor_scalar(b.kd[:, :], b.cum[:, :], 0.0, None, ALU.min)
            s.soft.next(dve)
            dve.drain()
            dve.tensor_tensor(b.kd[:, :], b.kd[:, :], b.e[:, :], ALU.subtract)
            dve.drain()
            dve.tensor_scalar(b.kd[:, :], b.kd[:, :], 1.0 / 16.0, None, ALU.mult)
            dve.drain()
            dve.tensor_tensor_scan(b.cum[:, :], g.scan, b.kd[:, :], 0.0, ALU.mult, ALU.add)
            dve.drain()
            cp, cs = b.cum[:, 0:NP].rearrange("p (c t) -> p c t", t=64), b.cum[:, NP:TOK].rearrange("p (c t) -> p c t", t=8)
            for i, (a, z) in enumerate(((31, 3), (63, 7))):
                dve.tensor_copy(b.ref[:, i, 0:16].unsqueeze(2), cp[:, :, a:a + 1])
                m = dve.tensor_copy(b.ref[:, i, 16:24].unsqueeze(2), cs[:, :, z:z + 1])
            dve.drain()
            s.q_out.next(dve)

            def exponent(i, sign):
                e = b.e
                if i is None:
                    return dve.tensor_copy(e[:, :], b.cum[:, :])
                r = b.ref[:, i, :]
                for lo, hi, size, ra in ((0, NP, 64, r[:, 0:16]), (NP, TOK, 8, r[:, 16:24])):
                    x = b.cum[:, lo:hi].rearrange("p (c t) -> p c t", t=size)
                    y = e[:, lo:hi].rearrange("p (c t) -> p c t", t=size)
                    ra = ra.unsqueeze(2).to_broadcast([P, (hi - lo) // size, size])
                    m = dve.tensor_tensor(y, x, ra, ALU.subtract) if sign > 0 else dve.tensor_tensor(y, ra, x, ALU.subtract)
                return m

            for i, sign, src, dst in ((0, 1, b.q, b.qs), (0, -1, b.k, b.ks), (None, 1, b.q, b.qe), (1, -1, b.k, b.kd)):
                s.cum_ready.mark(exponent(i, sign))
                s.exp_ready.next(dve)
                dve.tensor_tensor(dst[:, :], src[:, :], b.e[:, :], ALU.mult)
                dve.drain()


def gla_chunks(g, d, b, s, h, stored):
    nc = g.nc
    with nc.Block() as block:
        @block.tensor
        def _(pe):
            def first(t):
                R = P if t < 8 else NS
                for c in range(2 if t < 8 else 1):
                    x = slice(t * P + 64 * c, t * P + 64 * c + 64)
                    pe.matmul(g.ps[64 * c:64 * c + 64, 6 + t % 2, 0:64], b.ks[:, x], b.qs[:, x], start=True, stop=True)
                s.scored.mark(pe.transpose(g.ps[0:R, 6 + t % 2, P:2 * P], b.kd[:, t * P:t * P + R], g.ident))

            first(0)
            for t in range(9):
                s.turned_out.next(pe)
                if t + 1 < 9:
                    first(t + 1)
                if t < 8:
                    if t >= 1:
                        s.state.next(pe)
                    for c in range(2):
                        hr = slice(64 * c, 64 * c + 64)
                        mm = pe.matmul(g.ps[:, c, 0:256], b.kt[hr, t % 2, :], b.v[hr, t, :], start=True, stop=True)
                    s.outer.mark(mm)
                    if t >= 2:
                        s.o_out.next(pe)
                    for c in range(2):
                        hr = slice(64 * c, 64 * c + 64)
                        if c == 1:
                            s.state.next(pe)
                        for x in range(2):
                            p = g.ps[:, 2 + 2 * (t % 2) + c, 64 * x:64 * x + 64]
                            pe.matmul(p, b.v[hr, t, P * x:P * x + P], b.at[hr, t % 2, :], start=True, stop=False)
                            mm = pe.matmul(p, b.st[:, (2 * t + c) % 4, P * x:P * x + P], b.qe[:, t * P + 64 * c:t * P + 64 * c + 64], start=False, stop=True)
                    s.o_ready.mark(mm)
                else:
                    s.o_out.next(pe, 2)
                    s.state.next(pe)
                    for x in range(2):
                        p = g.ps[:, 4, P * x:P * x + 64]
                        pe.matmul(p, b.v[0:NS, 8, P * x:P * x + P], b.at[0:64, 0, :], start=True, stop=False)
                        for q in range(NB):
                            mm = pe.matmul(p[:, 8 * q:8 * q + 8], b.st8[:, q, P * x:P * x + P], b.qe[:, NP + 8 * q:NP + 8 * q + 8],
                                           start=False, stop=(q == NB - 1))
                    s.o_ready.mark(mm)
                    for q in range(NB):
                        mm = pe.matmul(g.ps[:, q // 2, 256 * (q % 2):256 * (q % 2) + 256], b.kt8[:, q, :], b.v[0:NS, 8, :], start=True, stop=True)
                    s.outer.mark(mm)
            s.o_out.next(pe)
            s.state.next(pe)

        @block.scalar
        def _(act):
            for t in range(9):
                s.o_ready.next(act)
                if t < 8:
                    for c in range(2):
                        at = t * P + 64 * c
                        a = act.activation(b.o[:, :, at:at + 64], g.ps[:, 2 + 2 * (t % 2) + c, 0:P].rearrange("p (x t) -> p x t", x=2), ACT.Copy)
                else:
                    a = act.activation(b.o[:, :, NP:TOK], g.ps[:, 4, 0:256].rearrange("p (x t) -> p x t", x=2)[:, :, 0:64], ACT.Copy)
                s.o_out.mark(a)

        @block.vector
        def _(dve):
            dve.memset(b.st[:, 0, :], 0.0)
            for t in range(9):
                R = P if t < 8 else NS
                s.scored.next(dve)
                m = dve.tensor_tensor(b.at[0:R, t % 2, :], g.ps[0:R, 6 + t % 2, 0:64], (g.upto if t < 8 else g.upto8)[0:R, :], ALU.mult)
                if t < 8:
                    m = dve.tensor_copy(b.kt[0:R, t % 2, :], g.ps[0:R, 6 + t % 2, P:2 * P])
                else:
                    m = dve.tensor_tensor(b.kt8[:, :, :], g.ps[0:NS, 6, P:2 * P].unsqueeze(1).to_broadcast([NS, NB, P]),
                                          g.brow[0:NS, :].unsqueeze(2).to_broadcast([NS, NB, P]), ALU.mult)
                s.turned_out.mark(m)
                if t >= 1:
                    s.o_ready.next(dve)
                if t < 8:
                    s.outer.next(dve)
                    for c in range(2):
                        n = 2 * t + c
                        dve.drain()
                        m = dve.scalar_tensor_tensor(b.st[:, (n + 1) % 4, :], b.st[:, n % 4, :], b.dec[:, n:n + 1],
                                                     g.ps[:, c, 0:256], ALU.mult, ALU.add)
                        s.state.mark(m)
                else:
                    s.outer.next(dve)
                    dve.tensor_tensor(b.st8[:, :, :], b.st8[:, :, :], b.dec[:, 16:24].unsqueeze(2).to_broadcast([P, NB, 256]), ALU.mult)
                    dve.drain()
                    s.state.mark(dve.tensor_tensor(b.st8[:, :, :].rearrange("p (a q) t -> p a (q t)", q=2), b.st8[:, :, :].rearrange("p (a q) t -> p a (q t)", q=2),
                                                   g.ps[:, 0:4, :], ALU.add))
            s.o_ready.next(dve)

        @block.sync
        def _(sp):
            s.state.next(sp, 17)
            sp.dma_start(d.gl_p[h], b.st[:, 0, :]).then_inc(stored, 16)
            sp.dma_start(d.gl_s[h], b.st8[:, :, :]).then_inc(stored, 16)
            sp.wait_ge(stored, 64 * h + 32)


def gla_finish(g, d, b, s, h, here, stored):
    nc = g.nc
    ps3 = lambda first: [(g.ps[:, first + c, 0:n], o, n) for c, (o, n) in enumerate(CH)]
    w = (b.wq, b.wk)
    silu = (b.qs, b.ks)
    sq = (b.qe, b.kd)
    with nc.Block() as block:
        @block.sync
        def _(sp):
            for x in range(2):
                sp.dma_start(w[x][:, :, :], d.w_gla_r[2 * h + x]).then_inc(here, 16)
            for x in range(2):
                s.gated.next(sp)
                sp.dma_start(d.gla_out[:, 2 * h + x, :], b.o[:, x, :]).then_inc(stored, 16)
            sp.wait_ge(stored, 64 * (h + 1))

        @block.tensor
        def _(pe):
            s.squared.next(pe)
            for x in range(2):
                for p, o, n in ps3(0):
                    mm = pe.matmul(p, g.ones, sq[x][:, o:o + n], start=(x == 0), stop=(x == 1))
            s.mean_ready.mark(mm)
            pe.wait_ge(here, 64 * (h + 1) + 32)
            for x in range(2):
                if x == 1:
                    s.root.next(pe)
                for k in range(KT):
                    for p, o, n in ps3(3 - 3 * x):
                        mm = pe.matmul(p, w[x][:, k, :], g.act[:, k, o:o + n], start=(k == 0), stop=(k == KT - 1))
                s.r_ready.mark(mm)

        @block.scalar
        def _(act):
            act.activation(sq[0][:, :], b.o[:, 0, :], ACT.Square)
            s.squared.mark(act.activation(sq[1][:, :], b.o[:, 1, :], ACT.Square))
            s.mean_ready.next(act)
            for p, o, n in ps3(0):
                a = act.activation(b.e[:, o:o + n], p, ACT.Sqrt, bias=g.col["eps"], scale=1.0 / 256)
            s.root.mark(a)
            for x in range(2):
                s.r_ready.next(act)
                for p, o, n in ps3(3 - 3 * x):
                    a = act.activation(silu[x][:, o:o + n], p, ACT.Silu)
                s.r_out.mark(a)

        @block.vector
        def _(dve):
            s.root.next(dve)
            dve.reciprocal(b.e[:, :], b.e[:, :])
            dve.drain()
            for x in range(2):
                dve.scalar_tensor_tensor(b.o[:, x, :], b.o[:, x, :], g.col["gn"][:, x:x + 1], b.e[:, :], ALU.mult, ALU.mult)
            dve.drain()
            for x in range(2):
                s.r_out.next(dve)
                s.gated.mark(dve.tensor_tensor(b.o[:, x, :], b.o[:, x, :], silu[x][:, :], ALU.mult))


def load_act(g, name, src, first):
    with ExitStack() as ctx:
        here = ctx.enter_context(g.nc.semaphore(name))
        block = ctx.enter_context(g.nc.Block())

        @block.sync
        def _(sp):
            sp.dma_start(g.act[:, first:KT, :], src).then_inc(here, 16)
            sp.wait_ge(here, 16)


def window_rows(g, d):
    with ExitStack() as ctx:
        s_win = ctx.enter_context(g.nc.semaphore("window_written"))
        block = ctx.enter_context(g.nc.Block())

        @block.gpsimd
        def _(pool):
            pool.dma_start(d.win_rows, d.cache_win_rows[:, 8:512, :]).then_inc(s_win, 16)
            pool.wait_ge(s_win, 16)


def program(nc, d, shapes):
    with ExitStack() as ctx:
        g = allocate(nc, ctx, shapes)
        load_inputs(g, d)
        rmsnorm(g, "n0", g.col["mix"][:, 0:8])
        rwkv_mix(g, d)
        with ExitStack() as sub:
            nsa_layer_buffers(g, sub)
            nsa_project(g, d)
            nsa_compress(g, d)
            nsa_prompt(g, d)
            nsa_sample(g, d)
        load_act(g, "rwkv_here", d.rwkv_out, 4)
        window_rows(g, d)
        project_out(g, 0, d.w_out_even)
        rmsnorm(g, "n1", g.col["ffn"][:, 0:8])
        feed_forward(g, 0, d.wg[0], d.wu[0], d.wd[0])
        rmsnorm(g, "n2", g.col["mix"][:, 8:16])
        gla_mix(g, d)
        load_act(g, "gla_here", d.gla_out, 0)
        project_out(g, 1, d.w_out_odd)
        rmsnorm(g, "n3", g.col["ffn"][:, 8:16])
        feed_forward(g, 1, d.wg[1], d.wu[1], d.wd[1])
        store_tokens(g, d)


def store_tokens(g, d):
    nc = g.nc
    with ExitStack() as ctx:
        s_out = ctx.enter_context(nc.semaphore("outputs_written"))
        block = ctx.enter_context(nc.Block())

        @block.sync
        def _(sp):
            sp.dma_start(d.y, g.resid[:, :, :]).then_inc(s_out, 16)
            sp.wait_ge(s_out, 16)


def pack(inp):
    inp = {k: np.asarray(v) for k, v in inp.items()}
    out = {}

    def weight(w, n):
        a, b = w.shape
        return np.ascontiguousarray(w.reshape(a // P, P, b // n, n).transpose(2, 1, 0, 3))

    def column(v):
        return v.reshape(-1, P).T

    x = np.concatenate([inp["x_prompt"].reshape(NP, D), inp["x_sample"].reshape(NS, D)])
    out["x"] = np.ascontiguousarray(x.T.reshape(KT, P, TOK).transpose(1, 0, 2))
    out["const"] = np.concatenate([v.reshape(P, -1) for v in _constants().values()], axis=1)
    w = inp["w_in_even"][0]
    q = w[:, 0:512].reshape(D, 2, 4, HD).transpose(0, 2, 1, 3).reshape(D, 512)
    kv = w[:, 512:1280].reshape(D, 3, 2, P)
    nsa = np.concatenate([q, kv[:, :, 0].reshape(D, 384), kv[:, :, 1].reshape(D, 384), w[:, 1280:1304]], axis=1)
    out["w_nsa"] = np.ascontiguousarray(nsa.reshape(KT, P, NSAW).transpose(1, 0, 2))
    order = np.concatenate([np.arange(1536, 1792)] + [np.arange(P) + 512 * s + P * j for j in range(4) for s in range(3)])
    out["w_rwkv"] = weight(w[:, 1304:][:, order], P)
    out["qk_gain"] = np.concatenate([np.tile(inp["nsa_qnorm"][0], 8), np.tile(inp["nsa_knorm"][0][:, None, :], (1, 2, 1)).reshape(-1)])
    out["cmp_w1"] = np.ascontiguousarray(inp["cmp_w1"][0].reshape(2, 16, P, P).transpose(2, 0, 1, 3))
    out["cmp_w2"] = np.ascontiguousarray(inp["cmp_w2"][0].transpose(1, 0, 2))
    out["cmp_pe"] = np.ascontiguousarray(inp["cmp_pe"][0].reshape(2, 16, P).transpose(2, 0, 1))
    cache = inp["cache_nsa_kv"][0]
    out["cache_cmp"] = np.ascontiguousarray(cache[:, :, 0:2].reshape(80, 64, 2, 2, 2, HD).transpose(0, 2, 5, 3, 4, 1).reshape(80, P, 4, 64))
    out["cache_slc"] = np.ascontiguousarray(np.concatenate([cache[:, :, 2].reshape(80, P, P).transpose(0, 2, 1), cache[:, :, 3].reshape(80, P, P)], axis=2))
    win = inp["cache_nsa_win"][0].reshape(NB, 4, P, 2, P)
    out["cache_win"] = np.ascontiguousarray(np.concatenate([win[:, :, :, 0].transpose(0, 3, 1, 2), win[:, :, :, 1].transpose(0, 2, 1, 3)], axis=3))
    out["cache_win_rows"] = np.ascontiguousarray(inp["cache_nsa_win"][0].reshape(NB, 512, 2 * P))
    out["pages"] = np.ascontiguousarray(inp["page_table"].reshape(1, NB * 8))
    out["shift"] = np.ascontiguousarray(inp["state_rwkv_shift"][0][:, order].reshape(NB, RT, P).transpose(2, 1, 0))
    out["lora"] = np.concatenate([np.concatenate([inp["rwkv_wB"][0], inp["rwkv_aB"][0]]), inp["rwkv_gB"][0]], axis=1)
    out["srwkv"] = np.ascontiguousarray(inp["state_rwkv"][0].reshape(NB, 4, 2, HD, HD).transpose(1, 2, 4, 0, 3).reshape(4, P, NB, HD))
    wo = inp["w_in_odd"][0]
    out["w_gla_qk"] = weight(wo[:, 0:1024], P)
    out["w_gla_v"] = np.ascontiguousarray(wo[:, 1024:2048].reshape(KT, P, 4, 256).transpose(2, 1, 0, 3))
    out["w_gla_gd"] = np.ascontiguousarray(wo[:, 2048:2064].reshape(KT, P, 16).transpose(1, 0, 2))
    out["w_gla_r"] = weight(wo[:, 2064:3088], P)
    out["gate_up"] = inp["gla_gate_up"][0]
    out["sgla"] = np.ascontiguousarray(inp["state_gla"][0].transpose(1, 2, 0, 3))
    out["w_out_even"] = weight(inp["w_out_even"][0], P)
    out["w_out_odd"] = weight(inp["w_out_odd"][0], P)
    out["wg"] = np.stack([weight(inp["ffn_gate"][i], 2 * P) for i in range(2)])
    out["wu"] = np.stack([weight(inp["ffn_up"][i], 2 * P) for i in range(2)])
    out["wd"] = np.stack([weight(inp["ffn_down"][i], P) for i in range(2)])
    cols = {"mix": inp["norm_mix"], "ffn": inp["norm_ffn"], "mu": inp["rwkv_mu"][0][order], "w0": inp["rwkv_w0"], "a0": inp["rwkv_a0"],
            "kk": inp["rwkv_kk"], "ka": inp["rwkv_ka"], "rk": inp["rwkv_rk"], "lnw": inp["rwkv_ln_w"], "lnb": inp["rwkv_ln_b"],
            "gb": inp["gla_gate_b"], "gn": inp["gla_norm"], "eps": np.full(P, EPS, np.float32), "gneps": np.full(P, GN_EPS, np.float32)}
    out["param"] = np.concatenate([column(cols[n]) for n, _ in PARAMS], axis=1)
    return {k: np.ascontiguousarray(v) for k, v in out.items()}


SCRATCH = {"gate_rows": (NS, 24), "rwkv_out": (P, 4, TOK), "gla_out": (P, KT, TOK)}
OUTS = {"y": (P, KT, TOK), "kv": (TOK, 768), "win_rows": (NB, 504, 2 * P), "last": (P, RT, 9),
        "rw_p": (4, P, HD), "rw_s": (4, P, NB, HD), "gl_p": (4, P, 256), "gl_s": (4, P, NB, 256)}


def kernel(**inputs):
    import concourse.bacc as _bacc
    from concourse.bass_utils import run_bass_kernel_spmd as _run

    nc = _bacc.Bacc("TRN2", target_bir_lowering=False, num_devices=1)
    arrays = pack(inputs)
    d = {n: nc.dram_tensor(f"in_{n}", a.shape, mybir.dt.from_np(a.dtype), kind="ExternalInput").ap() for n, a in arrays.items()}
    d |= {n: nc.dram_tensor(f"out_{n}", s, F32, kind="ExternalOutput").ap() for n, s in OUTS.items()}
    d |= {n: nc.dram_tensor(f"scratch_{n}", s, F32, kind="Internal").ap() for n, s in SCRATCH.items()}
    program(nc, names(**d), {k: v.shape for k, v in _constants().items()})
    r = _run(nc, [{f"in_{n}": a for n, a in arrays.items()}], core_ids=[0]).results[0]
    o = {n: r[f"out_{n}"] for n in OUTS}
    y = o["y"].transpose(2, 1, 0).reshape(TOK, D)
    k, v = o["kv"][:, 0:384].reshape(TOK, 3, 1, 2, HD), o["kv"][:, 384:768].reshape(TOK, 3, 1, 2, HD)
    kv = np.concatenate([k, v], axis=2)
    rows, win = kv[:, 0:2].reshape(TOK, 4, 2, HD), kv[:, 2]
    win_s = np.concatenate([o["win_rows"].reshape(NB, 504, 2, 2, HD), win[NP:].reshape(NB, SS, 2, 2, HD)], axis=1)
    last = o["last"].transpose(2, 1, 0).reshape(9, RT * P)
    order = np.concatenate([np.arange(1536, 1792)] + [np.arange(P) + 512 * s + P * j for j in range(4) for s in range(3)])
    last = last[:, np.argsort(order)]
    rw_p = o["rw_p"].reshape(4, 2, HD, HD).transpose(0, 1, 3, 2).reshape(1, 1, 8, HD, HD)
    rw_s = o["rw_s"].reshape(4, 2, HD, NB, HD).transpose(3, 0, 1, 4, 2).reshape(1, NB, 8, HD, HD)
    out = (y[:NP].reshape(1, NP, D), y[NP:].reshape(NB, SS, D), rows[:NP].reshape(1, 1, NP, 4, 2, HD),
           rows[NP:].reshape(1, NB, SS, 4, 2, HD), win[NP - 512:NP].reshape(1, 1, 512, 2, 2, HD), win_s[None],
           rw_p, rw_s, last[8:9][None], last[0:8][None], o["gl_p"][None, None], o["gl_s"].transpose(2, 0, 1, 3)[None])
    return tuple(np.ascontiguousarray(a) for a in out)
```

```python
from contextlib import ExitStack

import numpy as np

import concourse.bass as bass
from concourse import mybir

F32 = mybir.dt.float32
F32R = mybir.dt.float32r
I32 = mybir.dt.int32
ALU = mybir.AluOpType
ACT = mybir.ActivationFunctionType
AX = mybir.AxisListType.X
ds = bass.ds

P = 128
D = 1024
KT = D // P
NP = 1024
NB, SS = 8, 8
NS = NB * SS
TOK = NP + NS
HD = 64
FF = 2816
FT = FF // P
PARTS = ((0, 5), (5, 5), (10, 4), (14, 4), (18, 4))
CH = ((0, 384), (384, 384), (768, 320))
NCMP = 63
NSEL = 17
NEG = -1e30
KSETS = 3
QK = 512 + KSETS * P
NSAW = QK + KSETS * P + 24
RT = 14
EPS = 1e-6
GN_EPS = 64e-5


def _constants():
    i = np.arange(P)
    t64, c64 = i[:, None] % 64, np.arange(64)[None, :]
    same8 = (t64 // 8) == (c64 // 8)
    parts = {
        "ident": np.eye(P),
        "blk": (i[:, None] // 64 == i[None, :] // 64) * 1.0,
        "ones": np.ones((P, P)),
        "causal": np.where(i[None, :] <= i[:, None], 0.0, NEG),
        "window": np.where(i[None, :] > i[:, None], 0.0, NEG),
        "cmpmask": np.where(16 * np.arange(NCMP)[None, None, :] + 31 <= (i[:, None] + 128 * np.arange(8)[None, :])[:, :, None], 0.0, NEG),
        "seen": (i[:, None] >= 31) * 1.0,
        "id2": (t64 == c64) * 1.0,
        "below": (c64 < t64) * 1.0,
        "above": (c64 > t64) * 1.0,
        "upto": (c64 >= t64) * 1.0,
        "below8": (c64 < t64) * same8 * 1.0,
        "above8": (c64 > t64) * same8 * 1.0,
        "upto8": (c64 >= t64) * same8 * 1.0,
        "bcol": np.broadcast_to((np.arange(8)[:, None] == c64[0][None, :] // 8) * 1.0, (P, 8, 64)),
        "brow": (t64 // 8 == np.arange(8)[None, :]) * 1.0,
        "smask": np.where(np.arange(8)[None, :] <= i[:, None] % 8, 0.0, NEG),
        "swmask": np.where(np.arange(8)[None, :] > i[:, None] % 8, 0.0, NEG),
        "selmap": ((16 * i[:, None] <= 64 * np.arange(NSEL)[None, :] + 63) & (16 * i[:, None] + 31 >= 64 * np.arange(NSEL)[None, :]) & (i[:, None] < NCMP)) * 1.0,
        "samerow": ((i[:, None] // 32 == i[None, :] // 32) & (i[:, None] % 8 == i[None, :] % 8)) * 1.0,
        "blkid": np.broadcast_to(np.arange(NSEL)[None, :] * 1.0, (P, NSEL)),
        "scan": np.broadcast_to(np.where(np.arange(TOK) < NP, np.arange(TOK) % 64, np.arange(TOK) % 8)[None, :] != 0, (P, TOK)) * 1.0,
    }
    half = 8
    inv = (np.float32(500000.0) ** (-np.arange(half, dtype=np.float32) / np.float32(half))).astype(np.float32)
    pos = np.concatenate([np.arange(NP), 1024 + np.arange(NS) % SS, np.zeros(64)]).astype(np.float32)
    ang = pos[:, None] * inv[None, :]
    rope = np.concatenate([np.cos(ang), np.sin(ang)], axis=1).reshape(9, P, 16).transpose(1, 0, 2)
    parts["rope"] = rope
    return {k: np.ascontiguousarray(v, dtype=np.float32) for k, v in parts.items()}


PARAMS = (("mix", 16), ("ffn", 16), ("mu", 14), ("w0", 4), ("a0", 4), ("kk", 4), ("ka", 4), ("rk", 4),
          ("lnw", 4), ("lnb", 4), ("gb", 4), ("gn", 2), ("eps", 1), ("gneps", 1))


def names(**items):
    return type("Names", (), items)()


class Signal:

    def __init__(self, nc, ctx, name):
        self.sem = ctx.enter_context(nc.semaphore(name))
        self.waited = {}

    def mark(self, instruction):
        instruction.then_inc(self.sem, 1)

    def next(self, engine, n=1):
        who = str(engine.engine)
        self.waited[who] = self.waited.get(who, 0) + n
        engine.wait_ge(self.sem, self.waited[who])


def signals(nc, ctx, prefix, listed):
    return names(**{n: Signal(nc, ctx, prefix + n) for n in listed.split()})


def allocate(nc, ctx):
    sb = lambda name, shape: ctx.enter_context(nc.sbuf_tensor(name, shape, F32))
    sem = lambda n: ctx.enter_context(nc.semaphore(n))
    param = sb("param", [P, sum(n for _, n in PARAMS)])
    col, at = {}, 0
    for name, n in PARAMS:
        col[name] = param[:, at:at + n]
        at += n
    g = names(nc=nc, param=param, col=col, resid=sb("resid", [P, KT, TOK]), mean=sb("mean", [P, P]))
    g.norm_signals = signals(nc, ctx, "norm_", "squared mean_ready root_ready normed rounded")
    g.split_signals = signals(nc, ctx, "split_", "high both")
    g.const_here, g.acts_here, g.tokens_moved = sem("const_here"), sem("acts_here"), sem("tokens_moved")
    g.ff_sems = names(**{n: sem("ff_" + n) for n in (
        "gate_here", "up_here", "down_here0", "down_here1", "gate_hi", "up_hi", "down_hi", "gate_lo", "up_lo", "down_lo",
        "gate_done", "up_done", "down_done", "gate_out", "up_out", "down_out", "hid_ready")})
    g.out_sems = names(**{n: sem("wo_" + n) for n in ("here0", "here1", "hi", "lo", "done", "out")})
    g.ps = ctx.enter_context(nc.psum_tensor("ps", [P, 8, 512], F32))
    return g


def allocate_mixer(g, ctx, shapes):
    sb = lambda name, shape: ctx.enter_context(g.nc.sbuf_tensor(name, shape, F32))
    layer = g.layer
    const = sb(f"const{layer}", [P, sum(int(np.prod(s[1:])) for s in shapes.values())])
    items, at = {}, 0
    for name, s in shapes.items():
        n = int(np.prod(s[1:]))
        v = const[:, at:at + n]
        items[name] = v.rearrange("p (a b) -> p a b", b=s[2]) if len(s) == 3 else v
        at += n
    m = names(nc=g.nc, const=const, col=g.col, resid=g.resid, mean=g.mean, ps=g.ps, norm_signals=g.norm_signals,
              const_here=g.const_here, acts_here=g.acts_here, layer=layer, act=sb(f"act{layer}", [P, KT, TOK]), **items)
    return m


def load_inputs(g, d):
    nc = g.nc
    with nc.Block() as block:
        @block.sync
        def _(sp):
            for c, (o, n) in enumerate(CH):
                sp.dma_start(g.resid[:, :, o:o + n], d.x[:, :, o:o + n]).then_inc(g.tokens_moved, 16)
            sp.dma_start(g.param[:, :], d.param).then_inc(g.tokens_moved, 16)
            sp.wait_ge(g.tokens_moved, 64)

        @block.gpsimd
        def _(pool):
            pool.memset(g.mean[:, :], 1.0 / D)


def rmsnorm(g, name, gain, out, const=None):
    nc = g.nc
    s = g.norm_signals
    pair = len(out) == 2
    with ExitStack() as ctx:
        sq = ctx.enter_context(nc.sbuf_tensor(name + "sq", [P, 2, KT, 384], F32))
        rs = ctx.enter_context(nc.sbuf_tensor(name + "rs", [P, 3, 384], F32))
        normed = ctx.enter_context(nc.sbuf_tensor(name + "normed", [P, KT if pair else 1, 384], F32))
        block = ctx.enter_context(nc.Block())
        if const is not None:
            @block.sync
            def _(sp):
                sp.dma_start(g.const[:, :], const).then_inc(g.const_here, 16)
                sp.wait_ge(g.const_here, 16 * (g.layer + 1))

        @block.scalar
        def _(act):
            def square(c):
                o, n = CH[c]
                s.squared.mark(act.activation(sq[:, c % 2, :, 0:n], g.resid[:, :, o:o + n], ACT.Square))

            square(0)
            square(1)
            for c, (o, n) in enumerate(CH):
                s.mean_ready.next(act)
                s.root_ready.mark(act.activation(rs[:, c, 0:n], g.ps[:, c, 0:n], ACT.Sqrt, bias=g.col["eps"]))
                if c == 0:
                    square(2)
                if pair:
                    s.normed.next(act)
                    s.rounded.mark(act.activation(out[0][:, :, o:o + n], normed[:, :, 0:n], ACT.Copy))

        @block.tensor
        def _(pe):
            for c, (o, n) in enumerate(CH):
                s.squared.next(pe)
                for k in range(KT):
                    mm = pe.matmul(g.ps[:, c, 0:n], g.mean[:, :], sq[:, c % 2, k, 0:n], start=(k == 0), stop=(k == KT - 1))
                s.mean_ready.mark(mm)

        @block.vector
        def _(dve):
            for c, (o, n) in enumerate(CH):
                s.root_ready.next(dve)
                dve.reciprocal(rs[:, c, 0:n], rs[:, c, 0:n])
                dve.drain()
                for k in range(KT):
                    to = out[0][:, k, o:o + n] if not pair else normed[:, k, 0:n]
                    m = dve.scalar_tensor_tensor(to, g.resid[:, k, o:o + n], gain[:, k:k + 1],
                                                 rs[:, c, 0:n], ALU.mult, ALU.mult)
                if pair:
                    s.normed.mark(m)
                    s.rounded.next(dve)
                    dve.tensor_tensor(out[1][:, :, o:o + n], normed[:, :, 0:n], out[0][:, :, o:o + n].bitcast(F32), ALU.subtract)


def products(pe, g, bank, hi, lo, k, xh, xl, kx, first, last):
    passes = ((hi, xh), (lo, xh), (hi, xl))
    for i, (w, x) in enumerate(passes):
        for c, (o, n) in enumerate(CH):
            mm = pe.matmul(g.ps[:, bank + c, 0:n], w[:, k, :], x[:, kx, o:o + n],
                           start=(first and i == 0), stop=(last and i == 2))
    return mm


def feed_forward(g, layer, ah, al, w_gate, w_up, w_down):
    nc = g.nc
    name = f"ff{layer}_"
    F0, D0 = layer * FT, layer * len(PARTS) * KT
    s = g.ff_sems
    with ExitStack() as ctx:
        sb = lambda n, shape, dt=F32: ctx.enter_context(nc.sbuf_tensor(name + n, shape, dt))
        NF = PARTS[0][1]
        wg, wu = sb("wg", [P, KT, P]), sb("wu", [P, KT, P])
        gh, gl, uh, ul = (sb(n, [P, KT, P], F32R) for n in ("gh", "gl", "uh", "ul"))
        wd = [sb(f"wd{i}", [P, NF, P]) for i in range(2)]
        dh = [sb(f"dh{i}", [P, NF, P], F32R) for i in range(2)]
        dl = [sb(f"dl{i}", [P, NF, P], F32R) for i in range(2)]
        down_here = (s.down_here0, s.down_here1)
        silu, prod = sb("silu", [P, TOK]), sb("prod", [P, TOK])
        hh, hl = sb("hh", [P, NF, TOK], F32R), sb("hl", [P, NF, TOK], F32R)
        flat = lambda x: x.rearrange("p a n -> p (a n)")
        block = ctx.enter_context(nc.Block())

        @block.sync
        def _(sp):
            sp.dma_start(wg[:, :, :], w_gate[0]).then_inc(s.gate_here, 16)
            sp.dma_start(wu[:, :, :], w_up[0]).then_inc(s.up_here, 16)
            with sp.Fori(1, FT) as i:
                sp.wait_ge(s.gate_lo, i + F0)
                sp.dma_start(wg[:, :, :], w_gate[ds(i, 1)].rearrange("a p k n -> (a p) k n")).then_inc(s.gate_here, 16)
                sp.wait_ge(s.up_lo, i + F0)
                sp.dma_start(wu[:, :, :], w_up[ds(i, 1)].rearrange("a p k n -> (a p) k n")).then_inc(s.up_here, 16)

        @block.gpsimd
        def _(pool):
            def low_gate_up(f):
                pool.wait_ge(s.gate_hi, f + 1)
                pool.tensor_tensor(gl[:, :, :], wg[:, :, :], gh[:, :, :].bitcast(F32), ALU.subtract).then_inc(s.gate_lo, 1)
                pool.wait_ge(s.up_hi, f + 1)
                pool.tensor_tensor(ul[:, :, :], wu[:, :, :], uh[:, :, :].bitcast(F32), ALU.subtract).then_inc(s.up_lo, 1)

            def low_down(n, t, nf):
                pool.wait_ge(s.down_hi, n + 1)
                pool.tensor_tensor(dl[t][:, 0:nf, :], wd[t][:, 0:nf, :], dh[t][:, 0:nf, :].bitcast(F32), ALU.subtract).then_inc(s.down_lo, 1)

            for part, (f0, nf) in enumerate(PARTS):
                n0 = D0 + part * KT
                for t in range(2):
                    if n0 > 0:
                        pool.wait_ge(s.down_lo, n0)
                    pool.dma_start(wd[t][:, 0:nf, :], w_down[t, :, f0:f0 + nf, :]).then_inc(down_here[t], 16)
                if part == 0:
                    low_gate_up(F0)
                for t in range(2):
                    low_down(n0 + t, t, nf)
                with pool.Fori(0, nf - (part == len(PARTS) - 1)) as i:
                    low_gate_up(i + F0 + f0 + 1)
                with pool.Fori(1, KT // 2) as i:
                    for t in range(2):
                        pool.wait_ge(s.down_lo, 2 * i + n0 + t - 1)
                        pool.dma_start(wd[t][:, 0:nf, :], w_down[ds(2 * i + t, 1), :, f0:f0 + nf, :]
                                       .rearrange("a p k n -> (a p) k n")).then_inc(down_here[t], 16)
                    for t in range(2):
                        low_down(2 * i + n0 + t, t, nf)

        @block.tensor
        def _(pe):
            for part, (f0, nf) in enumerate(PARTS):
                n0 = D0 + part * KT
                pe.wait_ge(s.down_out, n0 + 2)
                with pe.Fori(0, nf) as i:
                    f = i + F0 + f0
                    pe.wait_ge(s.gate_lo, f + 1)
                    pe.wait_ge(s.gate_out, f + 1)
                    for k in range(KT):
                        mm = products(pe, g, 0, gh, gl, k, ah, al, k, k == 0, k == KT - 1)
                    mm.then_inc(s.gate_done, 1)
                    pe.wait_ge(s.up_lo, f + 1)
                    pe.wait_ge(s.up_out, f + 1)
                    for k in range(KT):
                        mm = products(pe, g, 3, uh, ul, k, ah, al, k, k == 0, k == KT - 1)
                    mm.then_inc(s.up_done, 1)
                pe.wait_ge(s.hid_ready, F0 + f0 + nf)
                with pe.Fori(0, KT // 2) as i:
                    for t in range(2):
                        n = 2 * i + n0 + t
                        pe.wait_ge(s.down_lo, n + 1)
                        pe.wait_ge(s.down_out, n + 1)
                        for k in range(nf):
                            mm = products(pe, g, 3 * t, dh[t], dl[t], k, hh, hl, k, k == 0, k == nf - 1)
                        mm.then_inc(s.down_done, 1)

        @block.scalar
        def _(act):
            def high_gate(f):
                act.wait_ge(s.gate_here, 16 * (f + 1))
                act.activation(gh[:, :, :], wg[:, :, :], ACT.Copy).then_inc(s.gate_hi, 1)

            def high_up(f):
                act.wait_ge(s.up_here, 16 * (f + 1))
                act.activation(uh[:, :, :], wu[:, :, :], ACT.Copy).then_inc(s.up_hi, 1)

            def high_down(n, t, nf, here):
                act.wait_ge(down_here[t], 16 * here)
                act.activation(dh[t][:, 0:nf, :], wd[t][:, 0:nf, :], ACT.Copy).then_inc(s.down_hi, 1)

            def swish(f):
                act.wait_ge(s.gate_done, f + 1)
                act.wait_ge(s.up_out, f + 1)
                for c, (o, n) in enumerate(CH):
                    a = act.activation(silu[:, o:o + n], g.ps[:, c, 0:n], ACT.Silu)
                a.then_inc(s.gate_out, 1)

            if layer == 0:
                act.sem_inc(s.gate_out, 1)
            high_gate(F0)
            high_up(F0)
            for part, (f0, nf) in enumerate(PARTS):
                n0 = D0 + part * KT
                if n0 > 0:
                    act.wait_ge(s.down_done, n0)
                for t in range(2):
                    high_down(n0 + t, t, nf, n0 // 2 + 1)
                last = part == len(PARTS) - 1
                with act.Fori(0, nf - last) as i:
                    f = i + F0 + f0
                    swish(f)
                    high_gate(f + 1)
                    act.wait_ge(s.up_done, f + 1)
                    high_up(f + 1)
                if last:
                    swish(F0 + FT - 1)
                with act.Fori(1, KT // 2) as i:
                    for t in range(2):
                        act.wait_ge(s.down_done, 2 * i + n0 + t - 1)
                        high_down(2 * i + n0 + t, t, nf, i + n0 // 2 + 1)

        @block.vector
        def _(dve):
            if layer == 0:
                dve.sem_inc(s.up_out, 1)
                dve.sem_inc(s.down_out, 2)
            for part, (f0, nf) in enumerate(PARTS):
                n0 = D0 + part * KT
                with dve.Fori(0, nf) as i:
                    f = i + F0 + f0
                    dve.wait_ge(s.gate_out, f + 2)
                    dve.wait_ge(s.up_done, f + 1)
                    for c, (o, n) in enumerate(CH):
                        m = dve.tensor_tensor(prod[:, o:o + n], silu[:, o:o + n], g.ps[:, 3 + c, 0:n], ALU.mult)
                    m.then_inc(s.up_out, 1)
                    dve.drain()
                    dve.tensor_copy(flat(hh[:, ds(i, 1), :]), prod[:, :])
                    dve.drain()
                    dve.tensor_tensor(flat(hl[:, ds(i, 1), :]), prod[:, :], flat(hh[:, ds(i, 1), :].bitcast(F32)), ALU.subtract)\
                       .then_inc(s.hid_ready, 1)
                    dve.drain()
                with dve.Fori(0, KT // 2) as i:
                    for t in range(2):
                        dve.wait_ge(s.down_done, 2 * i + n0 + t + 1)
                        for c, (o, n) in enumerate(CH):
                            r = flat(g.resid[:, ds(2 * i + t, 1), o:o + n])
                            m = dve.tensor_tensor(r, r, g.ps[:, 3 * t + c, 0:n], ALU.add)
                        m.then_inc(s.down_out, 1)


def project_out(g, layer, act_in, ah, al, w, waiting, first):
    nc = g.nc
    T0 = layer * KT
    name = f"out{layer}_"
    s = g.out_sems
    here = (s.here0, s.here1)
    split = g.split_signals
    with ExitStack() as ctx:
        wo = [ctx.enter_context(nc.sbuf_tensor(name + f"w{i}", [P, KT, P], F32)) for i in range(2)]
        oh = [ctx.enter_context(nc.sbuf_tensor(name + f"h{i}", [P, KT, P], F32R)) for i in range(2)]
        ol = [ctx.enter_context(nc.sbuf_tensor(name + f"l{i}", [P, KT, P], F32R)) for i in range(2)]
        block = ctx.enter_context(nc.Block())

        @block.sync
        def _(sp):
            sp.dma_start(act_in[:, first:KT, :], waiting).then_inc(g.acts_here, 16)
            for t in range(2):
                sp.dma_start(wo[t][:, :, :], w[t]).then_inc(here[t], 16)
            with sp.Fori(1, KT // 2) as i:
                for t in range(2):
                    sp.wait_ge(s.lo, 2 * i + (T0 + t - 1))
                    sp.dma_start(wo[t][:, :, :], w[ds(2 * i + t, 1)].rearrange("a p k n -> (a p) k n")).then_inc(here[t], 16)

        @block.gpsimd
        def _(pool):
            with pool.Fori(0, KT // 2) as i:
                for t in range(2):
                    pool.wait_ge(s.hi, 2 * i + T0 + t + 1)
                    pool.tensor_tensor(ol[t][:, :, :], wo[t][:, :, :], oh[t][:, :, :].bitcast(F32), ALU.subtract).then_inc(s.lo, 1)

        @block.tensor
        def _(pe):
            split.both.next(pe)
            with pe.Fori(0, KT // 2) as i:
                for t in range(2):
                    pe.wait_ge(s.lo, 2 * i + T0 + t + 1)
                    pe.wait_ge(s.out, 2 * i + T0 + t + 1)
                    for k in range(KT):
                        mm = products(pe, g, 3 * t, oh[t], ol[t], k, ah, al, k, k == 0, k == KT - 1)
                    mm.then_inc(s.done, 1)

        @block.scalar
        def _(act):
            for t in range(2):
                act.wait_ge(here[t], 16 * (T0 // 2 + 1))
                act.activation(oh[t][:, :, :], wo[t][:, :, :], ACT.Copy).then_inc(s.hi, 1)
            for k in range(KT):
                if k == first:
                    act.wait_ge(g.acts_here, 16 * (layer + 1))
                split.high.mark(act.activation(ah[:, k, :], act_in[:, k, :], ACT.Copy))
            with act.Fori(1, KT // 2) as i:
                for t in range(2):
                    act.wait_ge(here[t], 16 * (i + T0 // 2 + 1))
                    act.wait_ge(s.done, 2 * i + (T0 + t - 1))
                    act.activation(oh[t][:, :, :], wo[t][:, :, :], ACT.Copy).then_inc(s.hi, 1)

        @block.vector
        def _(dve):
            for k in range(KT):
                split.high.next(dve)
                m = dve.tensor_tensor(al[:, k, :], act_in[:, k, :], ah[:, k, :].bitcast(F32), ALU.subtract)
            split.both.mark(m)
            if layer == 0:
                dve.sem_inc(s.out, 2)
            with dve.Fori(0, KT // 2) as i:
                for t in range(2):
                    dve.wait_ge(s.done, 2 * i + T0 + t + 1)
                    for c, (o, n) in enumerate(CH):
                        r = g.resid[:, ds(2 * i + t, 1), o:o + n].rearrange("p a n -> p (a n)")
                        m = dve.tensor_tensor(r, r, g.ps[:, 3 * t + c, 0:n], ALU.add)
                    m.then_inc(s.out, 1)


def nsa_project(g, d):
    nc = g.nc
    tiles = [(t, min(P, TOK - t * P)) for t in range(9)]
    H = QK // HD
    with ExitStack() as ctx:
        sem = lambda s: ctx.enter_context(nc.semaphore("np_" + s))
        sb = lambda s, shape: ctx.enter_context(nc.sbuf_tensor("np_" + s, shape, F32))
        w = sb("w", [P, KT, NSAW])
        gain = sb("gain", [P, QK])
        sq = sb("sq", [P, QK])
        qk = [sb("qk0", [P, QK]), sb("qk1", [P, QK])]
        rn = sb("rn", [P, 2, H])
        rot = sb("rot", [P, 4, H, 8])
        w_here = [sem(f"w_here{i}") for i in range(2)]
        product, squared, summed, root, scaled = sem("product"), sem("squared"), sem("summed"), sem("root"), sem("scaled")
        freed_a, freed_v = sem("freed_a"), sem("freed_v")
        normed, turned, moved, stored = sem("normed"), sem("turned"), sem("moved"), [sem("stored0"), sem("stored1")]
        block = ctx.enter_context(nc.Block())

        @block.sync
        def _(sp):
            for i in range(2):
                sp.dma_start(w[:, 4 * i:4 * i + 4, :], d.w_nsa[:, 4 * i:4 * i + 4, :]).then_inc(w_here[i], 16)
            sp.dma_start(gain[:, :], d.qk_gain.partition_broadcast(P)).then_inc(w_here[0], 16)
            for t, R in tiles:
                sp.wait_ge(normed, t + 1)
                sp.dma_start(d.kv[t * P:t * P + R, 0:384], qk[t % 2][0:R, 512:QK]).then_inc(stored[t % 2], 16)
                sp.wait_ge(freed_v, t + 1)
                sp.dma_start(d.kv[t * P:t * P + R, 384:768], g.vtok[0:R, t, :]).then_inc(stored[t % 2], 16)
            sp.wait_ge(stored[0], 5 * 32)
            sp.wait_ge(stored[1], 4 * 32)

        @block.tensor
        def _(pe):
            def project(t, R):
                b = 3 * (t % 2)
                if t >= 2:
                    pe.wait_ge(scaled, t - 1)
                    pe.wait_ge(freed_v, t - 1)
                for k in range(KT):
                    x = g.act[:, k, t * P:t * P + R]
                    if t == 0 and k % 4 == 0:
                        pe.wait_ge(w_here[k // 4], 32 if k == 0 else 16)
                    for j, (o, n) in enumerate(((0, 512), (512, 384), (QK, 408))):
                        mm = pe.matmul(g.ps[0:R, b + j, 0:n], x, w[:, k, o:o + n], start=(k == 0), stop=(k == KT - 1))
                mm.then_inc(product, 1)

            def turn(t, R):
                pe.wait_ge(normed, t + 1)
                if t >= 1:
                    pe.wait_ge(moved, 2 * t)
                for j in range(7):
                    mm = pe.transpose(g.ps[:, 6 + j // 4, (j % 4) * P:(j % 4) * P + R], qk[t % 2][0:R, j * P:j * P + P],
                                      g.ident[0:R, 0:R])
                mm.then_inc(turned, 1)

            project(*tiles[0])
            for t, R in tiles:
                if t + 1 < 9:
                    project(*tiles[t + 1])
                turn(t, R)

        @block.scalar
        def _(act):
            def move(t, R):
                act.wait_ge(turned, t + 1)
                act.activation(g.qT[:, :, t * P:t * P + R], g.ps[:, 6, :].rearrange("p (a b) -> p a b", b=P)[:, :, 0:R], ACT.Copy)\
                   .then_inc(moved, 1)

            for t, R in tiles:
                b = 3 * (t % 2)
                act.wait_ge(product, t + 1)
                if t >= 1:
                    act.wait_ge(summed, t)
                act.activation(sq[0:R, 0:512], g.ps[0:R, b, 0:512], ACT.Square)
                act.activation(sq[0:R, 512:QK], g.ps[0:R, b + 1, 0:384], ACT.Square).then_inc(squared, 1)
                act.activation(g.vtok[0:R, t, :], g.ps[0:R, b + 2, 0:384], ACT.Copy)
                act.activation(g.gates[0:R, t, :], g.ps[0:R, b + 2, 384:408], ACT.Copy).then_inc(freed_v, 1)
                act.wait_ge(summed, t + 1)
                if t >= 1:
                    act.wait_ge(scaled, t)
                act.activation(rn[0:R, 0, :], rn[0:R, 1, :], ACT.Sqrt, bias=g.col["eps"][0:R, :], scale=1.0 / HD).then_inc(root, 1)
                if t >= 1:
                    move(t - 1, P)
            move(8, NS)
            act.drain()
            act.activation(g.gates[:, 0:8, :], g.gates[:, 0:8, :], ACT.Sigmoid)
            act.activation(g.gates[0:NS, 8, :], g.gates[0:NS, 8, :], ACT.Sigmoid)

        @block.vector
        def _(dve):
            def move(t, R):
                dve.wait_ge(turned, t + 1)
                dve.tensor_copy(g.kT[:, :, t * P:t * P + R], g.ps[:, 7, 0:384].rearrange("p (a b) -> p a b", b=P)[:, :, 0:R])\
                   .then_inc(moved, 1)

            for t, R in tiles:
                b = 3 * (t % 2)
                x = qk[t % 2]
                v = x[0:R, :].rearrange("p (h c) -> p h c", c=HD)
                dve.wait_ge(squared, t + 1)
                if t >= 1:
                    dve.wait_ge(root, t)
                dve.tensor_reduce(rn[0:R, 1, :], sq[0:R, :].rearrange("p (h c) -> p h c", c=HD), AX, ALU.add).then_inc(summed, 1)
                if t == 0:
                    dve.wait_ge(w_here[0], 32)
                if t >= 2:
                    dve.wait_ge(turned, t - 1)
                    dve.wait_ge(stored[t % 2], 32 * (t // 2))
                dve.tensor_tensor(x[0:R, 0:512], g.ps[0:R, b, 0:512], gain[0:R, 0:512], ALU.mult)
                dve.tensor_tensor(x[0:R, 512:QK], g.ps[0:R, b + 1, 0:384], gain[0:R, 512:QK], ALU.mult)
                dve.wait_ge(root, t + 1)
                dve.reciprocal(rn[0:R, 0, :], rn[0:R, 0, :])
                dve.drain()
                dve.tensor_tensor(v, v, rn[0:R, 0, :].unsqueeze(2).to_broadcast([R, H, HD]), ALU.mult).then_inc(scaled, 1)
                dve.drain()
                cos = g.rope[0:R, t, 0:8].unsqueeze(1).to_broadcast([R, H, 8])
                sin = g.rope[0:R, t, 8:16].unsqueeze(1).to_broadcast([R, H, 8])
                dve.tensor_tensor(rot[0:R, 0], v[:, :, 0:8], cos, ALU.mult)
                dve.tensor_tensor(rot[0:R, 1], v[:, :, 8:16], sin, ALU.mult)
                dve.tensor_tensor(rot[0:R, 2], v[:, :, 8:16], cos, ALU.mult)
                dve.tensor_tensor(rot[0:R, 3], v[:, :, 0:8], sin, ALU.mult)
                dve.drain()
                dve.tensor_tensor(v[:, :, 0:8], rot[0:R, 0], rot[0:R, 1], ALU.subtract)
                dve.tensor_tensor(v[:, :, 8:16], rot[0:R, 2], rot[0:R, 3], ALU.add).then_inc(normed, 1)
                dve.drain()
                if t >= 1:
                    move(t - 1, P)
            move(8, NS)


def nsa_compress(g, d):
    nc = g.nc
    with ExitStack() as ctx:
        sem = lambda s: ctx.enter_context(nc.semaphore("nc_" + s))
        sb = lambda s, shape: ctx.enter_context(nc.sbuf_tensor("nc_" + s, shape, F32))
        past = [sb("past0", [P, NB, 512]), sb("past1", [P, NB, 512])]
        rows = sb("rows", [P, 4, 4, P])
        pairs = sb("pairs", [P, 4, 512])
        w1 = sb("w1", [P, 2, 16, P])
        w2 = sb("w2", [P, 2, HD])
        pe_in = sb("pe", [P, 2, 16])
        bias = sb("bias", [P, 2])
        hid = sb("hid", [P, 2, 9, NCMP])
        pt = ctx.enter_context(nc.sbuf_tensor("nc_pages", [1, NB * 8], I32))
        w_here, rows_here, pt_here = sem("w_here"), sem("rows_here"), sem("pt_here")
        past_here = [sem("past_here0"), sem("past_here1")]
        turned, moved, biased, bias_ready = sem("turned"), sem("moved"), sem("biased"), sem("bias_ready")
        h_done, h_out, c_done, c_out = sem("h_done"), sem("h_out"), sem("c_done"), sem("c_out")
        block = ctx.enter_context(nc.Block())

        @block.sync
        def _(sp):
            sp.dma_start(pt[:, :], d.pages).then_inc(pt_here, 16)
            for i in range(4):
                src = d.kv[i * 256:(i + 1) * 256, :].rearrange("(p e) c -> p e c", e=2)
                for s in range(4):
                    at = 384 * (s // 2) + 64 * (s % 2)
                    sp.dma_start(rows[:, i, s, :].rearrange("p (e c) -> p e c", e=2), src[:, :, at:at + 64]).then_inc(rows_here, 16)
            sp.dma_start(w1[:, :, :, :], d.cmp_w1).then_inc(w_here, 16)
            sp.dma_start(w2[:, :, :], d.cmp_w2).then_inc(w_here, 16)
            sp.dma_start(pe_in[:, :, :], d.cmp_pe).then_inc(w_here, 16)
            sp.wait_ge(pt_here, 16)
            for s in range(4):
                if s >= 2:
                    sp.wait_ge(h_done, s - 1)
                for b in range(NB):
                    for i in range(8):
                        page = sp.value_load(pt[0:1, b * 8 + i:b * 8 + i + 1], min_val=0, max_val=79)
                        sp.dma_start(past[s % 2][:, b, i * 64:(i + 1) * 64],
                                     d.cache_cmp[ds(page, 1), :, s, :].rearrange("a p n -> (a p) n")).then_inc(past_here[s % 2], 16)

        @block.tensor
        def _(pe):
            pe.wait_ge(w_here, 48)
            for s in range(2):
                for l in range(16):
                    mm = pe.matmul(g.ps[:, 4, s:s + 1], w1[:, s, l, :], pe_in[:, s, l:l + 1], start=(l == 0), stop=(l == 15))
            mm.then_inc(biased, 1)
            pe.wait_ge(rows_here, 16 * 16)
            for s in range(4):
                for i in range(4):
                    mm = pe.transpose(g.ps[:, s, i * P:(i + 1) * P], rows[:, i, s, :], g.ident)
                mm.then_inc(turned, 1)
            pe.wait_ge(moved, 4)

            def hidden(s):
                pe.wait_ge(past_here[s % 2], 64 * 16 * (s // 2 + 1))
                if s >= 2:
                    pe.wait_ge(h_out, s - 1)
                b = 2 * (s % 2)
                for l in range(16):
                    w = w1[:, s // 2, l, :]
                    pe.matmul(g.ps[:, b, 0:504].rearrange("p (a n) -> p a n", n=NCMP), w, past[s % 2][:, :, l:l + 497:8],
                              start=(l == 0), stop=(l == 15))
                    mm = pe.matmul(g.ps[:, b + 1, 0:NCMP], w, pairs[:, s, l:l + 497:8], start=(l == 0), stop=(l == 15))
                mm.then_inc(h_done, 1)

            def compressed(s):
                pe.wait_ge(h_out, s + 1)
                q = 64 * (s % 2)
                if s < 2:
                    if s == 0:
                        pe.wait_ge(bias_ready, 1)
                    pe.matmul(g.ps[q:q + 64, 6, 0:504], w2[:, 0, :], hid[:, s % 2, 0:8, :].rearrange("p a n -> p (a n)"), start=True, stop=True)
                    mm = pe.matmul(g.ps[q:q + 64, 7, 0:NCMP], w2[:, 0, :], hid[:, s % 2, 8, :], start=True, stop=True)
                else:
                    for b in range(9):
                        mm = pe.matmul(g.ps[0:NCMP, 4 + b // 8, 64 * (b % 8):64 * (b % 8) + 64], hid[:, s % 2, b, :], w2[:, 1, :],
                                       start=True, stop=True)
                mm.then_inc(c_done, 1)

            hidden(0)
            for s in range(4):
                if s + 1 < 4:
                    hidden(s + 1)
                if s >= 1:
                    pe.wait_ge(c_out, s)
                compressed(s)

        @block.scalar
        def _(act):
            act.wait_ge(biased, 1)
            act.activation(bias[:, :], g.ps[:, 4, 0:2], ACT.Copy).then_inc(bias_ready, 1)
            act.wait_ge(bias_ready, 1)
            for s in range(4):
                act.wait_ge(h_done, s + 1)
                if s >= 2:
                    act.wait_ge(c_done, s - 1)
                b = 2 * (s % 2)
                act.activation(hid[:, s % 2, 0:8, :].rearrange("p a n -> p (a n)"), g.ps[:, b, 0:504], ACT.Gelu_apprx_tanh, bias=bias[:, s // 2:s // 2 + 1])
                act.activation(hid[:, s % 2, 8, :], g.ps[:, b + 1, 0:NCMP], ACT.Gelu_apprx_tanh, bias=bias[:, s // 2:s // 2 + 1])\
                   .then_inc(h_out, 1)

        @block.vector
        def _(dve):
            for s in range(4):
                dve.wait_ge(turned, s + 1)
                dve.tensor_copy(pairs[:, s, :], g.ps[:, s, :]).then_inc(moved, 1)
            for s in range(4):
                q = 64 * (s % 2)
                dve.wait_ge(c_done, s + 1)
                if s < 2:
                    dve.tensor_copy(g.kcT[q:q + 64, 0:8, :], g.ps[q:q + 64, 6, 0:504].rearrange("p (a n) -> p a n", n=NCMP))
                    dve.tensor_copy(g.kcT[q:q + 64, 8, :], g.ps[q:q + 64, 7, 0:NCMP]).then_inc(c_out, 1)
                else:
                    dve.tensor_copy(g.vc[0:NCMP, 0:8, s % 2, :], g.ps[0:NCMP, 4, :].rearrange("p (a n) -> p a n", n=HD))
                    dve.tensor_copy(g.vc[0:NCMP, 8, s % 2, :], g.ps[0:NCMP, 5, 0:HD]).then_inc(c_out, 1)


def nsa_prompt(g, d):
    nc = g.nc
    items = [(t, h, part) for t in range(8) for h in range(8) for part in range(2)]

    def keys(t, part):
        return list(range(t + 1)) if part == 0 else list(range(max(0, t - 4), t + 1))

    chunks = []
    for t, h, part in items:
        n = len(keys(t, part)) + part
        chunks.append([(a, min(4, n - a)) for a in range(0, n, 4)])
    first = np.concatenate([[0], np.cumsum([len(c) for c in chunks])]).tolist()
    with ExitStack() as ctx:
        sem = lambda s: ctx.enter_context(nc.semaphore("na_" + s))
        sb = lambda s, shape: ctx.enter_context(nc.sbuf_tensor("na_" + s, shape, F32))
        prob = sb("prob", [P, 2, 1024])
        probT = sb("probT", [P, 2, 512])
        top = sb("top", [P, 2, 2])
        total = sb("total", [P, 4, 2])
        weight = sb("weight", [P, 2, 4])
        o = sb("o", [P, 2, 512])
        scored, maxed, expd, turned, moved = sem("scored"), sem("maxed"), sem("expd"), sem("turned"), sem("moved")
        summed, mixed, row_turned, row_out = sem("summed"), sem("mixed"), sem("row_turned"), sem("row_out")
        block = ctx.enter_context(nc.Block())

        @block.tensor
        def _(pe):
            def scores(i):
                t, h, part = items[i]
                q0 = 64 * (h // 4)
                q = g.qT[q0:q0 + 64, h % 4, t * P:t * P + P]
                b = 2 * (i % 2)
                if i >= 2:
                    pe.wait_ge(expd, i - 1)
                ks = keys(t, part)
                kset = 1 + part
                lo, n = ks[0] * P, len(ks) * P
                masks = {len(ks) - 1: g.causal}
                if part == 1 and t >= 4:
                    masks[0] = g.window
                for a in range(0, n, 512):
                    m = min(512, n - a)
                    inside = [j for j in masks if a <= j * P < a + m]
                    mm = pe.matmul(g.ps[:, b + a // 512, 0:m], q, g.kT[q0:q0 + 64, kset, lo + a:lo + a + m],
                                   start=True, stop=not inside)
                    for j in inside:
                        mm = pe.matmul(g.ps[:, b + a // 512, j * P - a:j * P - a + P], g.ident, masks[j], start=False,
                                       stop=(j == inside[-1]))
                if part == 1:
                    out = g.ps[:, b + 1, 256:256 + NCMP]
                    pe.matmul(out, q, g.kcT[q0:q0 + 64, 8, :], start=True, stop=False, skip_group_check=True)
                    mm = pe.matmul(out, g.ident, g.cmpmask[:, t, :], start=False, stop=True, skip_group_check=True)
                mm.then_inc(scored, 1)

            def values(i):
                t, h, part = items[i]
                ks = keys(t, part)
                pe.wait_ge(expd, i + 1)
                out = g.ps[:, 6, :]
                col = lambda j: 64 * (3 * (i // 2 % 2) + j)
                if part == 0 and i >= 4:
                    pe.wait_ge(mixed, i // 2 - 1)
                for c, (a, n) in enumerate(chunks[i]):
                    e = first[i] + c
                    if e >= 2:
                        pe.wait_ge(moved, e - 1)
                    for j in range(a, a + n):
                        if j < len(ks):
                            mm = pe.transpose(g.ps[:, 4 + e % 2, (j - a) * P:(j - a) * P + P], prob[:, i % 2, j * P:j * P + P], g.ident)
                        else:
                            mm = pe.transpose(g.ps[0:NCMP, 4 + e % 2, (j - a) * P:(j - a) * P + P], prob[:, i % 2, 768:768 + NCMP], g.ident)
                    mm.then_inc(turned, 1)
                    pe.wait_ge(moved, e + 1)
                    for j in range(a, a + n):
                        if j < len(ks):
                            v = g.vtok[:, ks[j], (1 + part) * P + 64 * (h // 4):(1 + part) * P + 64 * (h // 4) + 64]
                            mm = pe.matmul(out[:, col(part):col(part) + 64], probT[:, e % 2, (j - a) * P:(j - a) * P + P], v,
                                           start=(j == 0), stop=(j == len(ks) - 1), skip_group_check=True)
                        else:
                            mm = pe.matmul(out[:, col(2):col(2) + 64], probT[0:NCMP, e % 2, (j - a) * P:(j - a) * P + P],
                                           g.vc[0:NCMP, 8, h // 4, :], start=True, stop=True, skip_group_check=True)
                mm.then_inc(summed, 1)

            def turn_rows(t):
                pe.wait_ge(mixed, 8 * (t + 1))
                if t >= 1:
                    pe.wait_ge(row_out, t)
                for j in range(4):
                    mm = pe.transpose(g.ps[:, 7, j * P:j * P + P], o[:, t % 2, j * P:j * P + P], g.ident)
                mm.then_inc(row_turned, 1)

            scores(0)
            for i, (t, h, part) in enumerate(items):
                if i + 1 < len(items):
                    scores(i + 1)
                values(i)
                if h == 1 and part == 1 and t >= 1:
                    turn_rows(t - 1)
            turn_rows(7)

        @block.scalar
        def _(act):
            for i, (t, h, part) in enumerate(items):
                n = len(keys(t, part)) * P
                b = 2 * (i % 2)
                act.wait_ge(maxed, i + 1)
                if i >= 2:
                    act.wait_ge(summed, i - 1)
                if i >= 4:
                    act.wait_ge(mixed, i // 2 - 1)
                tot = total[:, 2 * (i // 2 % 2):2 * (i // 2 % 2) + 2, :]
                s = g.ps[:, b:b + 2, :].rearrange("p a n -> p (a n)")[:, 0:n]
                a = act.activation(prob[:, i % 2, 0:n], s, ACT.Exp, bias=top[:, i % 2, 0:1], scale=0.125, accum_out=tot[:, 0, part:part + 1])
                if part == 1:
                    a = act.activation(prob[:, 1, 768:768 + NCMP], g.ps[:, b + 1, 256:256 + NCMP], ACT.Exp, bias=top[:, i % 2, 1:2], scale=0.125,
                                       accum_out=tot[:, 1, 0:1])
                a.then_inc(expd, 1)

        @block.vector
        def _(dve):
            def maxima(i):
                t, h, part = items[i]
                n = len(keys(t, part)) * P
                b = 2 * (i % 2)
                dve.wait_ge(scored, i + 1)
                if i >= 2:
                    dve.wait_ge(expd, i - 1)
                s = g.ps[:, b:b + 2, :].rearrange("p a n -> p (a n)")[:, 0:n]
                dve.tensor_reduce(top[:, i % 2, 0:1], s, AX, ALU.max)
                if part == 1:
                    dve.tensor_reduce(top[:, i % 2, 1:2], g.ps[:, b + 1, 256:256 + NCMP], AX, ALU.max)
                dve.drain()
                dve.tensor_scalar(top[:, i % 2, 0:1 + part], top[:, i % 2, 0:1 + part], -0.125, None, ALU.mult).then_inc(maxed, 1)

            def move(i):
                for c, (a, n) in enumerate(chunks[i]):
                    e = first[i] + c
                    dve.wait_ge(turned, e + 1)
                    whole = n - (items[i][2] == 1 and a + n == len(keys(*items[i][::2])) + 1)
                    m = None
                    if whole:
                        m = dve.tensor_copy(probT[:, e % 2, 0:whole * P], g.ps[:, 4 + e % 2, 0:whole * P])
                    if whole < n:
                        m = dve.tensor_copy(probT[0:NCMP, e % 2, whole * P:n * P], g.ps[0:NCMP, 4 + e % 2, whole * P:n * P])
                    m.then_inc(moved, 1)

            def mix(i):
                t, h, _ = items[i]
                u = i // 2 % 2
                dve.wait_ge(expd, i + 1)
                dve.reciprocal(weight[:, u, 0:2], total[:, 2 * u, :])
                dve.reciprocal(weight[:, u, 2:3], total[:, 2 * u + 1, 0:1])
                dve.drain()
                dve.tensor_tensor(weight[:, u, 0:2], weight[:, u, 0:2], g.gates[:, t, 3 * h + 1:3 * h + 3], ALU.mult)
                if t == 0:
                    dve.scalar_tensor_tensor(weight[:, u, 2:3], weight[:, u, 2:3], g.seen, g.gates[:, t, 3 * h:3 * h + 1], ALU.mult, ALU.mult)
                else:
                    dve.tensor_tensor(weight[:, u, 2:3], weight[:, u, 2:3], g.gates[:, t, 3 * h:3 * h + 1], ALU.mult)
                dve.wait_ge(summed, i + 1)
                if h == 0 and t >= 2:
                    dve.wait_ge(row_turned, t - 1)
                dve.drain()
                out = o[:, t % 2, 64 * h:64 * h + 64]
                for j in range(3):
                    s = g.ps[:, 6, 64 * (3 * u + j):64 * (3 * u + j) + 64]
                    if j == 0:
                        m = dve.tensor_scalar(out, s, weight[:, u, 0:1], None, ALU.mult)
                    else:
                        dve.drain()
                        m = dve.scalar_tensor_tensor(out, s, weight[:, u, j:j + 1], out, ALU.mult, ALU.add)
                m.then_inc(mixed, 1)

            def rows_out(t):
                dve.wait_ge(row_turned, t + 1)
                dve.tensor_copy(g.act[:, 0:4, t * P:t * P + P], g.ps[:, 7, :].rearrange("p (a b) -> p a b", b=P)).then_inc(row_out, 1)

            maxima(0)
            for i, (t, h, part) in enumerate(items):
                if i + 1 < len(items):
                    maxima(i + 1)
                move(i)
                if part == 1:
                    mix(i)
                    if h == 1 and t >= 1:
                        rows_out(t - 1)
            rows_out(7)


def nsa_sample(g, d):
    nc = g.nc
    with ExitStack() as ctx:
        sem = lambda s: ctx.enter_context(nc.semaphore("ns_" + s))
        sb = lambda s, shape: ctx.enter_context(nc.sbuf_tensor("ns_" + s, shape, F32))
        past = [sb("past0", [P, 8, 2 * P]), sb("past1", [P, 8, 2 * P])]
        win = [sb("win0", [P, 4, 2 * P]), sb("win1", [P, 4, 2 * P])]
        newv = sb("newv", [SS, NB, 2 * P])
        gate = sb("gate", [P, 4, 3])
        qs = sb("qs", [P, NB, 32])
        prob = sb("prob", [P, 1536 + 80])
        probT = sb("probT", [P, 15, P])
        top = sb("top", [P, 3])
        total = sb("total", [P, 3])
        weight = sb("weight", [P, 3])
        imp = sb("imp", [P, 4, NSEL])
        least = sb("least", [P, 2])
        o = sb("o", [P, HD])
        oT = sb("oT", [HD, P])
        pt = ctx.enter_context(nc.sbuf_tensor("ns_pages", [1, NB * 8], I32))
        pt_here, small_here, gates_out, queries = sem("pt_here"), sem("small_here"), sem("gates_out"), sem("queries")
        past_here = [sem("past_here0"), sem("past_here1")]
        scored, maxed, cmp_exp, cmp_norm, cmp_turned, cmp_moved = (sem(s) for s in
            ("scored", "maxed", "cmp_exp", "cmp_norm", "cmp_turned", "cmp_moved"))
        imp_row, imp_moved, imp_sum, dropped, expd = (sem(s) for s in ("imp_row", "imp_moved", "imp_sum", "dropped", "expd"))
        turned, moved, summed, mixed, o_turned, o_out = (sem(s) for s in ("turned", "moved", "summed", "mixed", "o_turned", "o_out"))
        block = ctx.enter_context(nc.Block())

        @block.sync
        def _(sp):
            sp.dma_start(pt[:, :], d.pages).then_inc(pt_here, 16)
            sp.dma_start(newv[:, :, 0:2 * P], d.kv[NP:TOK, 512:768].rearrange("(b q) c -> q b c", q=SS)).then_inc(small_here, 16)
            sp.dma_start(d.gate_rows, g.gates[0:NS, 8, :]).then_inc(gates_out, 16)
            sp.wait_ge(gates_out, 16)
            for i in range(4):
                for b2 in range(2):
                    for h in range(8):
                        r0 = 64 * b2 + 8 * h
                        sp.dma_start(gate[r0:r0 + 8, i, :], d.gate_rows[(2 * i + b2) * 8:(2 * i + b2) * 8 + 8, 3 * h:3 * h + 3])\
                          .then_inc(small_here, 16)
            sp.wait_ge(pt_here, 16)
            for b in range(NB):
                if b >= 2:
                    sp.wait_ge(summed, b // 2)
                for i in range(8):
                    page = sp.value_load(pt[0:1, b * 8 + i:b * 8 + i + 1], min_val=0, max_val=79)
                    sp.dma_start(past[b % 2][:, i, :], d.cache_slc[ds(page, 1), :, :].rearrange("a p n -> (a p) n")).then_inc(past_here[b % 2], 16)
                sp.dma_start(win[b % 2][:, :, :], d.cache_win[b]).then_inc(past_here[b % 2], 16)

        @block.tensor
        def _(pe):
            def combos(i):
                for j in range(4):
                    b, gr = 2 * i + j // 2, j % 2
                    yield j, b, gr, qs[64 * gr:64 * gr + 64, b, :]

            pe.wait_ge(queries, 1)
            for i in range(4):
                for j, b, gr, q in combos(i):
                    if gr == 0:
                        pe.wait_ge(past_here[b % 2], 9 * 16 * (i + 1))
                    if i >= 1 and j == 0:
                        pe.wait_ge(expd, i)
                    rows = slice(32 * j, 32 * j + 32)
                    f = slice(64 * gr, 64 * gr + 64)
                    new = slice(NP + 8 * b, NP + 8 * b + 8)
                    for half in range(2):
                        pe.matmul(g.ps[rows, half, :].rearrange("p (a n) -> p a n", n=P), q, past[b % 2][f, 4 * half:4 * half + 4, 0:P],
                                  start=True, stop=True)
                    pe.matmul(g.ps[rows, 2, :].rearrange("p (a n) -> p a n", n=P), q, win[b % 2][f, :, 0:P], start=True, stop=True)
                    pe.matmul(g.ps[rows, 3, 0:8], q, g.kT[f, 1, new], start=True, stop=True, skip_group_check=True)
                    pe.matmul(g.ps[rows, 3, 8:16], q, g.kT[f, 2, new], start=True, stop=True, skip_group_check=True)
                    mm = pe.matmul(g.ps[rows, 3, 16:16 + NCMP], q, g.kcT[f, b, :], start=True, stop=True, skip_group_check=True)
                mm.then_inc(scored, 1)
                pe.wait_ge(cmp_norm, i + 1)
                if i >= 1:
                    pe.wait_ge(o_out, i)
                pe.transpose(g.ps[0:NCMP, 4, 0:P], prob[:, 1536 + 16:1536 + 16 + NCMP], g.ident).then_inc(cmp_turned, 1)
                pe.wait_ge(cmp_moved, i + 1)
                pe.matmul(g.ps[:, 5, 0:NSEL], probT[0:NCMP, 14, :], g.selmap[0:NCMP, :], start=True, stop=True).then_inc(imp_row, 1)
                pe.wait_ge(imp_moved, i + 1)
                pe.matmul(g.ps[:, 5, 64:64 + NSEL], g.samerow, imp[:, 0, :], start=True, stop=True, skip_group_check=True).then_inc(imp_sum, 1)
                pe.wait_ge(expd, i + 1)
                for a in range(14):
                    if a < 12:
                        mm = pe.transpose(g.ps[:, 4 + a // 4, (a % 4) * P:(a % 4) * P + P], prob[:, a * P:a * P + P], g.ident)
                    else:
                        c = 1536 + 8 * (a - 12)
                        mm = pe.transpose(g.ps[0:8, 7, (a - 12) * P:(a - 12) * P + P], prob[:, c:c + 8], g.ident)
                    if a == 11:
                        mm.then_inc(turned, 1)
                mm.then_inc(turned, 1)
                pe.wait_ge(moved, i + 1)
                for j, b, gr, q in combos(i):
                    rows = slice(32 * j, 32 * j + 32)
                    f = slice(64 * gr, 64 * gr + 64)
                    fv = slice(P + 64 * gr, P + 64 * gr + 64)
                    for a in range(8):
                        pe.matmul(g.ps[rows, 4, 0:64], probT[:, a, rows], past[b % 2][:, a, fv], start=(a == 0), stop=False)
                    pe.matmul(g.ps[rows, 4, 0:64], probT[0:8, 12, rows], newv[:, b, f], start=False, stop=True)
                    for a in range(4):
                        pe.matmul(g.ps[rows, 5, 0:64], probT[:, 8 + a, rows], win[b % 2][:, a, fv], start=(a == 0), stop=False)
                    pe.matmul(g.ps[rows, 5, 0:64], probT[0:8, 13, rows], newv[:, b, fv], start=False, stop=True)
                    mm = pe.matmul(g.ps[rows, 6, 0:64], probT[0:NCMP, 14, rows], g.vc[0:NCMP, b, gr, :], start=True, stop=True)
                mm.then_inc(summed, 1)
                pe.wait_ge(mixed, i + 1)
                pe.transpose(g.ps[0:64, 7, 256:256 + P], o[:, :], g.ident).then_inc(o_turned, 1)

        @block.scalar
        def _(act):
            for i in range(4):
                act.wait_ge(maxed, i + 1)
                act.activation(prob[:, 1552:1552 + NCMP], g.ps[:, 3, 16:16 + NCMP], ACT.Exp, bias=top[:, 2:3], scale=0.125,
                               accum_out=total[:, 2:3]).then_inc(cmp_exp, 1)
                act.wait_ge(dropped, i + 1)
                act.activation(prob[:, 0:1024], g.ps[:, 0:2, :].rearrange("p a n -> p (a n)"), ACT.Exp, bias=top[:, 0:1], scale=0.125)
                act.activation(prob[:, 1024:1536], g.ps[:, 2, :], ACT.Exp, bias=top[:, 1:2], scale=0.125)
                act.activation(prob[:, 1536:1544], g.ps[:, 3, 0:8], ACT.Exp, bias=top[:, 0:1], scale=0.125)
                act.activation(prob[:, 1544:1552], g.ps[:, 3, 8:16], ACT.Exp, bias=top[:, 1:2], scale=0.125).then_inc(expd, 1)

        @block.vector
        def _(dve):
            part = sb("part", [P, 4])
            dve.tensor_copy(qs[:, :, :].rearrange("p b (r q) -> p b r q", q=8),
                            g.qT[:, :, NP:TOK].rearrange("p r (b q) -> p b r q", q=8)).then_inc(queries, 1)
            for i in range(4):
                dve.wait_ge(scored, i + 1)
                dve.tensor_tensor(g.ps[:, 3, 0:8], g.ps[:, 3, 0:8], g.smask, ALU.add)
                dve.tensor_tensor(g.ps[:, 3, 8:16], g.ps[:, 3, 8:16], g.smask, ALU.add)
                dve.tensor_tensor(g.ps[:, 2, 0:8], g.ps[:, 2, 0:8], g.swmask, ALU.add)
                dve.tensor_reduce(top[:, 2:3], g.ps[:, 3, 16:16 + NCMP], AX, ALU.max)
                dve.drain()
                dve.tensor_reduce(part[:, 0:1], g.ps[:, 2, :], AX, ALU.max)
                dve.tensor_reduce(part[:, 1:2], g.ps[:, 3, 8:16], AX, ALU.max)
                dve.drain()
                dve.tensor_tensor(top[:, 1:2], part[:, 0:1], part[:, 1:2], ALU.max)
                dve.drain()
                dve.tensor_scalar(top[:, 1:3], top[:, 1:3], -0.125, None, ALU.mult).then_inc(maxed, 1)
                dve.wait_ge(cmp_exp, i + 1)
                dve.reciprocal(weight[:, 2:3], total[:, 2:3])
                dve.drain()
                c = prob[:, 1552:1552 + NCMP]
                dve.tensor_scalar(c, c, weight[:, 2:3], None, ALU.mult).then_inc(cmp_norm, 1)
                dve.wait_ge(cmp_turned, i + 1)
                dve.tensor_copy(probT[0:NCMP, 14, :], g.ps[0:NCMP, 4, 0:P]).then_inc(cmp_moved, 1)
                dve.wait_ge(imp_row, i + 1)
                dve.tensor_copy(imp[:, 0, :], g.ps[:, 5, 0:NSEL]).then_inc(imp_moved, 1)
                dve.wait_ge(imp_sum, i + 1)
                dve.tensor_copy(imp[:, 1, :], g.ps[:, 5, 64:64 + NSEL])
                dve.drain()
                dve.tensor_reduce(least[:, 0:1], imp[:, 1, 1:15], AX, ALU.min)
                dve.drain()
                dve.scalar_tensor_tensor(imp[:, 2, 1:15], imp[:, 1, 1:15], least[:, 0:1], g.blkid[:, 1:15], ALU.is_equal, ALU.mult)
                dve.drain()
                dve.tensor_reduce(least[:, 1:2], imp[:, 2, 1:15], AX, ALU.max)
                dve.drain()
                dve.tensor_scalar(imp[:, 3, 0:16], g.blkid[:, 0:16], least[:, 1:2], NEG, ALU.is_equal, ALU.mult)
                dve.drain()
                s = g.ps[:, 0:2, :].rearrange("p a (m n) -> p (a m) n", n=64)
                dve.tensor_tensor(s, s, imp[:, 3, 0:16].unsqueeze(2).to_broadcast([P, 16, 64]), ALU.add)
                dve.drain()
                dve.tensor_reduce(part[:, 0:1], g.ps[:, 0:2, :].rearrange("p a n -> p (a n)"), AX, ALU.max)
                dve.tensor_reduce(part[:, 1:2], g.ps[:, 3, 0:8], AX, ALU.max)
                dve.drain()
                dve.tensor_tensor(top[:, 0:1], part[:, 0:1], part[:, 1:2], ALU.max)
                dve.drain()
                dve.tensor_scalar(top[:, 0:1], top[:, 0:1], -0.125, None, ALU.mult).then_inc(dropped, 1)
                dve.wait_ge(expd, i + 1)
                dve.tensor_reduce(part[:, 0:1], prob[:, 0:1024], AX, ALU.add)
                dve.tensor_reduce(part[:, 1:2], prob[:, 1024:1536], AX, ALU.add)
                dve.tensor_reduce(part[:, 2:4], prob[:, 1536:1552].rearrange("p (a b) -> p a b", b=8), AX, ALU.add)
                dve.drain()
                dve.tensor_tensor(total[:, 0:2], part[:, 0:2], part[:, 2:4], ALU.add)
                dve.drain()
                dve.reciprocal(weight[:, 0:2], total[:, 0:2])
                dve.wait_ge(turned, 2 * i + 1)
                dve.tensor_copy(probT[:, 0:12, :], g.ps[:, 4:7, :].rearrange("p a (b n) -> p (a b) n", n=P))
                dve.wait_ge(turned, 2 * i + 2)
                dve.tensor_copy(probT[0:8, 12:14, :], g.ps[0:8, 7, 0:256].rearrange("p (b n) -> p b n", n=P)).then_inc(moved, 1)
                if i == 0:
                    dve.wait_ge(small_here, 65 * 16)
                dve.drain()
                dve.tensor_tensor(weight[:, 0:2], weight[:, 0:2], gate[:, i, 1:3], ALU.mult)
                dve.wait_ge(summed, i + 1)
                dve.drain()
                dve.tensor_scalar(o[:, :], g.ps[:, 4, 0:64], weight[:, 0:1], None, ALU.mult)
                dve.drain()
                dve.scalar_tensor_tensor(o[:, :], g.ps[:, 5, 0:64], weight[:, 1:2], o[:, :], ALU.mult, ALU.add)
                dve.drain()
                dve.scalar_tensor_tensor(o[:, :], g.ps[:, 6, 0:64], gate[:, i, 0:1], o[:, :], ALU.mult, ALU.add).then_inc(mixed, 1)
                dve.wait_ge(o_turned, i + 1)
                for gr in range(2):
                    for r in range(4):
                        h = 4 * gr + r
                        src = g.ps[0:64, 7, 256:256 + P].rearrange("p (b s) -> p b s", b=2)[:, :, 8 * h:8 * h + 8]
                        dst = g.act[64 * (h % 2):64 * (h % 2) + 64, h // 2, NP + 16 * i:NP + 16 * i + 16].rearrange("p (b s) -> p b s", b=2)
                        m = dve.tensor_copy(dst, src)
                m.then_inc(o_out, 1)


def nsa_layer_buffers(g, ctx):
    sb = lambda name, shape: ctx.enter_context(g.nc.sbuf_tensor(name, shape, F32))
    g.qT = sb("qT", [P, 4, TOK])
    g.kT = sb("kT", [P, KSETS, TOK])
    g.vtok = sb("vtok", [P, 9, KSETS * P])
    g.gates = sb("gates", [P, 9, 24])
    g.kcT = sb("kcT", [P, 9, NCMP])
    g.vc = sb("vc", [P, 9, 2, HD])


RWKV_GROUPS = [(0, 4), (4, 4), (8, 4), (12, 4), (16, 1)]


def rwkv_mix(g, d):
    nc = g.nc
    with ExitStack() as ctx:
        sb = lambda s, shape: ctx.enter_context(nc.sbuf_tensor("rw_" + s, shape, F32))
        b = names(
            w=[sb("w0", [P, KT, P]), sb("w1", [P, KT, P])],
            lora=sb("lora", [P, 2, TOK]),
            lw=sb("lw", [P, 2, 512]),
            shift=sb("shift", [P, RT, NB]), last=sb("last", [P, RT, 9]),
            raw=sb("raw", [P, TOK]),
            r=sb("r", [P, TOK]), k=sb("k", [P, TOK]), v=sb("v", [P, TOK]),
            ar=sb("ar", [P, 17, 2, 64]),
            bt=sb("bt", [P, TOK]), kt=sb("kt", [P, TOK]), cum=sb("cum", [P, TOK]),
            lw_=sb("logw", [P, TOK]), a=sb("a", [P, TOK]), e=sb("e", [P, TOK]), kk=sb("kkn", [P, TOK]),
            bonus=sb("bonus", [P, TOK]), y=sb("y", [P, TOK]),
            endp=sb("endp", [P, 16 + NB]),
            tok=sb("tok", [P, 4, 4, 64]),
            tri=sb("tri", [P, 4, 4, 64]),
            low=sb("low", [P, 4, 64]), up=sb("up", [P, 4, 2, 64]),
            wg=sb("wg", [P, 4, 2, 64]),
            u=sb("u", [P, 64]), st=sb("st", [P, 64]), st8=sb("st8", [P, NB, 64]),
            m8=sb("m8", [P, 3, NB, 64]),
        )
        s = signals(nc, ctx, "rw_", "product raw_ready mixed_in za_ready kk_squared kk_summed kk_root "
                    "log_ready a_ready decay decay_read bonus_in bonus_sum scored masked tokens powers "
                    "wg_ready wg_out u_ready u_out y_ready y_out s_ready s_out m8_s centered mean_ready sq_ready var_ready var_root gated")
        w_here = [ctx.enter_context(nc.semaphore("rw_w_here0")), ctx.enter_context(nc.semaphore("rw_w_here1"))]
        small, st_here, stored = (ctx.enter_context(nc.semaphore("rw_" + n)) for n in ("small", "st_here", "stored"))
        for i in range(2):
            rwkv_features(g, d, b, s, i, w_here, small)
        for j in range(4):
            for i in range(2 + 3 * j, 5 + 3 * j):
                rwkv_features(g, d, b, s, i, w_here, small)
            rwkv_prepare(g, d, b, s, j, st_here)
            rwkv_chunks(g, d, b, s, j, st_here, stored)
            rwkv_finish(g, d, b, s, j, stored)
        with ExitStack() as c2:
            block = c2.enter_context(nc.Block())

            @block.sync
            def _(sp):
                sp.dma_start(d.last, b.last[:, :, :]).then_inc(small, 16)
                sp.wait_ge(small, 48)


def rwkv_features(g, d, b, s, i, w_here, small):
    nc = g.nc
    out = b.lora[:, i, :] if i < 2 else (b.r, b.k, b.v)[(i - 2) % 3][:, :]
    t = b.cum[:, :] if i < 2 else b.e[:, :]
    with nc.Block() as block:
        @block.sync
        def _(sp):
            if i == 0:
                sp.dma_start(b.lw[:, :, :].rearrange("p a n -> p (a n)"), d.lora).then_inc(small, 16)
                sp.dma_start(b.shift[:, :, :], d.shift).then_inc(small, 16)
                sp.dma_start(b.w[0][:, :, :], d.w_rwkv[0]).then_inc(w_here[0], 16)
            if i + 1 < RT:
                sp.dma_start(b.w[(i + 1) % 2][:, :, :], d.w_rwkv[i + 1]).then_inc(w_here[(i + 1) % 2], 16)

        @block.tensor
        def _(pe):
            pe.wait_ge(w_here[i % 2], 16 * (i // 2 + 1))
            for k in range(KT):
                for c, (o, n) in enumerate(CH):
                    mm = pe.matmul(g.ps[:, c, 0:n], b.w[i % 2][:, k, :], g.act[:, k, o:o + n], start=(k == 0), stop=(k == KT - 1))
            s.product.mark(mm)

        @block.scalar
        def _(act):
            s.product.next(act)
            for c, (o, n) in enumerate(CH):
                a = act.activation(b.raw[:, o:o + n], g.ps[:, c, 0:n], ACT.Copy)
            s.raw_ready.mark(a)
            if i < 2:
                s.mixed_in.next(act)
                if i == 0:
                    act.activation(b.lora[0:64, 0, :], b.lora[0:64, 0, :], ACT.Tanh)
                else:
                    act.activation(b.lora[:, 1, :], b.lora[:, 1, :], ACT.Sigmoid)

        @block.vector
        def _(dve):
            s.raw_ready.next(dve)
            if i == 0:
                dve.wait_ge(small, 32)
            x = b.raw
            x8 = x[:, NP:TOK].rearrange("p (b q) -> p b q", q=SS)
            t8 = t[:, NP:TOK].rearrange("p (b q) -> p b q", q=SS)
            dve.tensor_tensor(t[:, 1:NP], x[:, 0:NP - 1], x[:, 1:NP], ALU.subtract)
            dve.tensor_scalar(t[:, 0:1], x[:, 0:1], -1.0, None, ALU.mult)
            dve.tensor_tensor(t8[:, :, 1:8], x8[:, :, 0:7], x8[:, :, 1:8], ALU.subtract)
            dve.tensor_tensor(t8[:, :, 0:1], b.shift[:, i, :].unsqueeze(2), x8[:, :, 0:1], ALU.subtract)
            dve.tensor_copy(b.last[:, i, 0:8].unsqueeze(2), x8[:, :, 7:8])
            dve.tensor_copy(b.last[:, i, 8:9], x[:, NP - 1:NP])
            dve.drain()
            m = dve.scalar_tensor_tensor(out, t, g.col["mu"][:, i:i + 1], x[:, :], ALU.mult, ALU.add)
            if i < 2:
                s.mixed_in.mark(m)


def rwkv_prepare(g, d, b, s, j, st_here):
    nc = g.nc
    col = lambda name: g.col[name][:, j:j + 1]
    pj = slice(P * j, P * j + P)
    ps3 = lambda first: [(g.ps[:, first + c, 0:n], o, n) for c, (o, n) in enumerate(CH)]
    with nc.Block() as block:
        @block.sync
        def _(sp):
            sp.dma_start(b.st8[:, :, :], d.srwkv[j]).then_inc(st_here, 16)

        @block.tensor
        def _(pe):
            for p, o, n in ps3(0):
                pe.matmul(p, b.lw[0:64, 0, pj], b.lora[0:64, 0, o:o + n], start=True, stop=True)
            for p, o, n in ps3(3):
                mm = pe.matmul(p, b.lw[64:P, 0, pj], b.lora[64:P, 0, o:o + n], start=True, stop=True)
            s.za_ready.mark(mm)
            s.kk_squared.next(pe)
            s.a_ready.next(pe)
            for p, o, n in ps3(0):
                mm = pe.matmul(p, g.blk, b.e[:, o:o + n], start=True, stop=True)
            s.kk_summed.mark(mm)
            s.bonus_in.next(pe)
            for p, o, n in ps3(3):
                mm = pe.matmul(p, g.blk, b.y[:, o:o + n], start=True, stop=True)
            s.bonus_sum.mark(mm)

        @block.scalar
        def _(act):
            s.za_ready.next(act)
            for p, o, n in ps3(0):
                a = act.activation(b.lw_[:, o:o + n], p, ACT.Sigmoid, bias=col("w0"))
            s.log_ready.mark(a)
            for p, o, n in ps3(3):
                a = act.activation(b.a[:, o:o + n], p, ACT.Sigmoid, bias=col("a0"))
            s.a_ready.mark(a)
            s.kk_root.next(act)
            s.sq_ready.mark(act.activation(b.e[:, :], b.e[:, :], ACT.Sqrt))
            s.decay_read.next(act)
            s.decay.mark(act.activation(b.e[:, :], b.e[:, :], ACT.Exp))
            s.decay_read.next(act)
            s.decay.mark(act.activation(b.e[:, :], b.cum[:, :], ACT.Exp, scale=-1.0))
            s.decay_read.next(act)
            s.decay.mark(act.activation(b.e[:, :], b.cum[:, :], ACT.Exp))

        @block.vector
        def _(dve):
            ar = lambda which: (b.ar[:, :, which, :])
            chunked = lambda x: x.rearrange("p (c t) -> p c t", t=64)
            dve.tensor_scalar(b.kk[:, :], b.k[:, :], col("kk"), None, ALU.mult)
            dve.drain()
            s.log_ready.next(dve)
            s.kk_squared.mark(dve.tensor_tensor(b.e[:, :], b.kk[:, :], b.kk[:, :], ALU.mult))
            dve.tensor_scalar(b.lw_[:, :], b.lw_[:, :], -float(np.exp(-0.5)), None, ALU.mult)
            dve.drain()
            dve.tensor_tensor_scan(b.cum[:, :], g.scan, b.lw_[:, :], 0.0, ALU.mult, ALU.add)
            s.kk_summed.next(dve)
            for p, o, n in ps3(0):
                m = dve.tensor_scalar(b.e[:, o:o + n], p, 1e-24, None, ALU.max)
            s.kk_root.mark(m)
            dve.tensor_scalar(b.raw[:, :], b.a[:, :], 1.0, col("ka"), ALU.subtract, ALU.mult)
            dve.drain()
            dve.scalar_tensor_tensor(b.k[:, :], b.raw[:, :], 1.0, b.k[:, :], ALU.add, ALU.mult)
            dve.drain()
            s.bonus_in.mark(dve.scalar_tensor_tensor(b.y[:, :], b.k[:, :], col("rk"), b.r[:, :], ALU.mult, ALU.mult))
            s.sq_ready.next(dve)
            dve.reciprocal(b.e[:, :], b.e[:, :])
            dve.drain()
            dve.tensor_tensor(b.kk[:, :], b.kk[:, :], b.e[:, :], ALU.mult)
            dve.drain()
            s.decay_read.mark(dve.tensor_tensor(b.e[:, :], b.cum[:, :], b.lw_[:, :], ALU.subtract))
            s.bonus_sum.next(dve)
            for p, o, n in ps3(3):
                dve.tensor_tensor(b.bonus[:, o:o + n], p, b.v[:, o:o + n], ALU.mult)
            s.decay.next(dve)
            s.decay_read.mark(dve.scalar_tensor_tensor(ar(0), chunked(b.kk[:, :]), -1.0, chunked(b.e[:, :]), ALU.mult, ALU.mult))
            dve.tensor_tensor(b.kk[:, :], b.kk[:, :], b.a[:, :], ALU.mult)
            s.decay.next(dve)
            dve.drain()
            dve.tensor_tensor(b.bt[:, :], b.kk[:, :], b.e[:, :], ALU.mult)
            s.decay_read.mark(dve.tensor_tensor(b.kt[:, :], b.k[:, :], b.e[:, :], ALU.mult))
            s.decay.next(dve)
            dve.tensor_tensor(ar(1), chunked(b.r[:, :]), chunked(b.e[:, :]), ALU.mult)
            dve.tensor_copy(b.endp[:, 0:16].unsqueeze(2), chunked(b.e[:, 0:NP])[:, :, 63:64])
            dve.tensor_copy(b.endp[:, 16:24].unsqueeze(2), b.e[:, NP:TOK].rearrange("p (b q) -> p b q", q=SS)[:, :, 7:8])


def rwkv_chunks(g, d, b, s, j, st_here, stored):
    nc = g.nc
    halves = [slice(0, 64), slice(64, P)]
    with nc.Block() as block:
        @block.tensor
        def _(pe):
            for c0, n in RWKV_GROUPS:
                sampled = c0 == 16
                for c in range(n):
                    t = slice(64 * (c0 + c), 64 * (c0 + c) + 64)
                    for h in halves:
                        at, art = b.ar[h, c0 + c, 0, :], b.ar[h, c0 + c, :, :].rearrange("p a t -> p (a t)")
                        tri = g.ps[h, c // 2, 256 * (c % 2):256 * (c % 2) + 256]
                        pe.matmul(tri[:, 0:P], b.bt[h, t], art, start=True, stop=True)
                        pe.matmul(tri[:, P:2 * P], b.kt[h, t], art, start=True, stop=True)
                        pe.matmul(g.ps[h, 2, 64 * c:64 * c + 64], at, b.bt[h, t], start=True, stop=True)
                        for x, src in enumerate((at, b.bt[h, t], b.kt[h, t], b.v[h, t])):
                            o = 256 * (c % 2) + 64 * x
                            mm = pe.matmul(g.ps[h, 3 + c // 2, o:o + 64], src, g.id2[h, :], start=True, stop=True)
                s.scored.mark(mm)
                for level in range(6):
                    s.masked.next(pe)
                    for c in range(n):
                        for h in halves:
                            low, up = b.low[h, c, :], b.up[h, c, :, :].rearrange("p a t -> p (a t)")
                            mm = pe.matmul(g.ps[h, 5, P * c:P * c + P], low, up, start=True, stop=True)
                            if level < 5:
                                mm = pe.matmul(g.ps[h, 6, 64 * c:64 * c + 64], b.up[h, c, 0, :], low, start=True, stop=True)
                    s.powers.mark(mm)
                s.masked.next(pe)
                s.tokens.next(pe)
                for c in range(n):
                    for h in halves:
                        pe.matmul(g.ps[h, 5, P * c:P * c + 64], b.tok[h, c, 0, :], b.up[h, c, 1, :], start=True, stop=True)
                        mm = pe.matmul(g.ps[h, 5, P * c + 64:P * c + P], b.tri[h, c, 2, :], b.tok[h, c, 3, :], start=True, stop=True)
                s.wg_ready.mark(mm)
                s.wg_out.next(pe)
                for c in range(n):
                    for h in halves:
                        pu = g.ps[h, 6, 0:64]
                        pe.matmul(pu, b.up[h, c, 1, :], b.wg[h, c, 1, :], start=True, stop=False)
                        if sampled:
                            for q in range(NB):
                                mm = pe.matmul(pu, b.m8[h, 0, q, :], b.st8[h, q, :], start=False, stop=(q == NB - 1))
                        else:
                            mm = pe.matmul(pu, b.wg[h, c, 0, :], b.st[h, :], start=False, stop=True)
                    s.u_ready.mark(mm)
                    s.u_out.next(pe)
                    for h in halves:
                        if sampled:
                            for q in range(NB):
                                ps = g.ps[h, 2, 64 * q:64 * q + 64]
                                pe.matmul(ps, b.m8[h, 2, q, :], b.u[h, :], start=True, stop=False)
                                pe.matmul(ps, b.m8[h, 1, q, :], b.tok[h, c, 3, :], start=False, stop=False)
                                mm = pe.matmul(ps, g.id2[h, :], b.st8[h, q, :], start=False, stop=True)
                        else:
                            ps = g.ps[h, 2, 0:64]
                            pe.matmul(ps, b.tok[h, c, 1, :], b.u[h, :], start=True, stop=False)
                            pe.matmul(ps, b.tok[h, c, 2, :], b.tok[h, c, 3, :], start=False, stop=False)
                            mm = pe.matmul(ps, g.id2[h, :], b.st[h, :], start=False, stop=True)
                    s.s_ready.mark(mm)
                    if sampled:
                        s.m8_s.next(pe)
                    for h in halves:
                        py = g.ps[h, 7, 64 * c:64 * c + 64]
                        pe.matmul(py, b.u[h, :], b.tri[h, c, 1, :], start=True, stop=False)
                        pe.matmul(py, b.tok[h, c, 3, :], b.tri[h, c, 3, :], start=False, stop=False)
                        if sampled:
                            for q in range(NB):
                                mm = pe.matmul(py, b.st8[h, q, :], b.m8[h, 1, q, :], start=False, stop=(q == NB - 1))
                        else:
                            mm = pe.matmul(py, b.st[h, :], b.ar[h, c0 + c, 1, :], start=False, stop=True)
                    s.y_ready.mark(mm)
                    s.s_out.next(pe)
                s.y_out.next(pe)

        @block.scalar
        def _(act):
            for c0, n in RWKV_GROUPS:
                s.scored.next(act)
                for q in range(0, n, 2):
                    m = min(2, n - q)
                    a = act.activation(b.tok[:, q:q + m, :, :].rearrange("p a x t -> p (a x t)"), g.ps[:, 3 + q // 2, 0:256 * m], ACT.Copy)
                s.tokens.mark(a)
                s.y_ready.next(act, n)
                s.y_out.mark(act.activation(b.y[:, 64 * c0:64 * (c0 + n)], g.ps[:, 7, 0:64 * n], ACT.Copy))

        @block.vector
        def _(dve):
            dve.memset(b.st[:, :], 0.0)
            dve.wait_ge(st_here, 16 * (j + 1))
            for c0, n in RWKV_GROUPS:
                sampled = c0 == 16
                above, upto, below = (g.above8, g.upto8, g.below8) if sampled else (g.above, g.upto, g.below)
                over = lambda m: m.unsqueeze(1).to_broadcast([P, n, 64])
                s.scored.next(dve)
                tri = g.ps[:, 0:2, :].rearrange("p a (c x t) -> p (a c) x t", x=4, t=64)[:, 0:n]
                for x, m in enumerate((above, upto, above, upto)):
                    dve.tensor_tensor(b.tri[:, 0:n, x, :], tri[:, :, x, :], over(m), ALU.mult)
                dve.tensor_tensor(b.up[:, 0:n, 0, :], tri[:, :, 0, :], over(above), ALU.mult)
                dve.tensor_copy(b.up[:, 0:n, 1, :], over(g.id2))
                s.masked.mark(dve.tensor_tensor(b.low[:, 0:n, :], g.ps[:, 2, 0:64 * n].rearrange("p (c t) -> p c t", t=64), over(below), ALU.mult))
                for level in range(6):
                    s.powers.next(dve)
                    up = g.ps[:, 5, 0:P * n].rearrange("p (c x t) -> p c x t", x=2, t=64)
                    m = dve.tensor_tensor(b.up[:, 0:n, 1, :], b.up[:, 0:n, 1, :], up[:, :, 1, :], ALU.add)
                    if level < 5:
                        dve.tensor_copy(b.up[:, 0:n, 0, :], up[:, :, 0, :])
                        m = dve.tensor_copy(b.low[:, 0:n, :], g.ps[:, 6, 0:64 * n].rearrange("p (c t) -> p c t", t=64))
                    s.masked.mark(m)
                s.wg_ready.next(dve)
                m = dve.tensor_copy(b.wg[:, 0:n, :, :].rearrange("p c x t -> p (c x t)"), g.ps[:, 5, 0:P * n])
                if sampled:
                    dve.drain()
                    eight = lambda x: x.unsqueeze(1).to_broadcast([P, NB, 64])
                    rows = g.brow.unsqueeze(2).to_broadcast([P, NB, 64])
                    dve.tensor_tensor(b.m8[:, 0, :, :], eight(b.wg[:, 0, 0, :]), g.bcol, ALU.mult)
                    dve.tensor_tensor(b.m8[:, 1, :, :], eight(b.tok[:, 0, 2, :]), rows, ALU.mult)
                    m = dve.tensor_tensor(b.m8[:, 2, :, :], eight(b.tok[:, 0, 1, :]), rows, ALU.mult)
                s.wg_out.mark(m)
                for c in range(n):
                    s.u_ready.next(dve)
                    s.u_out.mark(dve.tensor_copy(b.u[:, :], g.ps[:, 6, 0:64]))
                    s.s_ready.next(dve)
                    if sampled:
                        s.m8_s.mark(dve.tensor_tensor(b.m8[:, 1, :, :], eight(b.ar[:, 16, 1, :]), g.bcol, ALU.mult))
                        s.y_ready.next(dve)
                        m = dve.tensor_tensor(b.st8[:, :, :], g.ps[:, 2, :].rearrange("p (q t) -> p q t", t=64),
                                              b.endp[:, 16:24].unsqueeze(2).to_broadcast([P, NB, 64]), ALU.mult)
                    else:
                        s.y_ready.next(dve)
                        m = dve.tensor_scalar(b.st[:, :], g.ps[:, 2, 0:64], b.endp[:, c0 + c:c0 + c + 1], None, ALU.mult)
                    s.s_out.mark(m)

        @block.sync
        def _(sp):
            s.s_out.next(sp, 17)
            sp.dma_start(d.rw_p[j], b.st[:, :]).then_inc(stored, 16)
            sp.dma_start(d.rw_s[j], b.st8[:, :, :]).then_inc(stored, 16)
            sp.wait_ge(stored, 48 * j + 32)


def rwkv_finish(g, d, b, s, j, stored):
    nc = g.nc
    col = lambda name: g.col[name][:, j:j + 1]
    ps3 = lambda first: [(g.ps[:, first + c, 0:n], o, n) for c, (o, n) in enumerate(CH)]
    with nc.Block() as block:
        @block.tensor
        def _(pe):
            for p, o, n in ps3(0):
                mm = pe.matmul(p, g.blk, b.y[:, o:o + n], start=True, stop=True)
            s.mean_ready.mark(mm)
            for p, o, n in ps3(3):
                mm = pe.matmul(p, b.lw[:, 1, P * j:P * j + P], b.lora[:, 1, o:o + n], start=True, stop=True)
            s.centered.next(pe)
            for p, o, n in ps3(0):
                mm = pe.matmul(p, g.blk, b.e[:, o:o + n], start=True, stop=True)
            s.var_ready.mark(mm)

        @block.scalar
        def _(act):
            s.var_ready.next(act)
            for p, o, n in ps3(0):
                a = act.activation(b.cum[:, o:o + n], p, ACT.Sqrt, bias=g.col["gneps"], scale=1.0 / HD)
            s.var_root.mark(a)

        @block.vector
        def _(dve):
            s.mean_ready.next(dve)
            for p, o, n in ps3(0):
                dve.scalar_tensor_tensor(b.y[:, o:o + n], p, -1.0 / HD, b.y[:, o:o + n], ALU.mult, ALU.add)
            dve.drain()
            s.centered.mark(dve.tensor_tensor(b.e[:, :], b.y[:, :], b.y[:, :], ALU.mult))
            s.var_root.next(dve)
            dve.reciprocal(b.cum[:, :], b.cum[:, :])
            dve.drain()
            dve.tensor_tensor(b.y[:, :], b.y[:, :], b.cum[:, :], ALU.mult)
            dve.drain()
            dve.tensor_scalar(b.y[:, :], b.y[:, :], col("lnw"), col("lnb"), ALU.mult, ALU.add)
            dve.drain()
            dve.tensor_tensor(b.y[:, :], b.y[:, :], b.bonus[:, :], ALU.add)
            dve.drain()
            for p, o, n in ps3(3):
                m = dve.tensor_tensor(b.y[:, o:o + n], b.y[:, o:o + n], p, ALU.mult)
            s.gated.mark(m)

        @block.sync
        def _(sp):
            s.gated.next(sp)
            sp.dma_start(d.rwkv_out[:, j, :], b.y[:, :]).then_inc(stored, 16)
            sp.wait_ge(stored, 48 * (j + 1))


def gla_mix(g, d):
    nc = g.nc
    with ExitStack() as ctx:
        sb = lambda s, shape: ctx.enter_context(nc.sbuf_tensor("gl_" + s, shape, F32))
        b = names(
            wq=sb("wq", [P, KT, P]), wk=sb("wk", [P, KT, P]), wv=sb("wv", [P, KT, 256]), wgd=sb("wgd", [P, KT, 16]),
            up=sb("up", [16, 512]), gd=sb("gd", [16, TOK]),
            q=sb("q", [P, TOK]), k=sb("k", [P, TOK]), v=sb("v", [P, 9, 256]), cum=sb("cum", [P, TOK]), e=sb("e", [P, TOK]),
            qs=sb("qs", [P, TOK]), ks=sb("ks", [P, TOK]), qe=sb("qe", [P, TOK]), kd=sb("kd", [P, TOK]),
            ref=sb("ref", [P, 2, 24]), dec=sb("dec", [P, 24]),
            at=sb("at", [P, 2, 64]), kt=sb("kt", [P, 2, P]), kt8=sb("kt8", [NS, NB, P]),
            st=sb("st", [P, 4, 256]), st8=sb("st8", [P, NB, 256]), o=sb("o", [P, 2, TOK]))
        s = signals(nc, ctx, "gl_", "gd_ready gd_out product q_out v_ready v_out logit x_ready soft cum_ready exp_ready exp_read scored turned_out "
                    "outer state o_ready o_out squared mean_ready root r_ready r_out gated")
        here, v_here, st_here, stored = (ctx.enter_context(nc.semaphore("gl_" + n)) for n in ("here", "v_here", "st_here", "stored"))
        with nc.Block() as block:
            @block.sync
            def _(sp):
                sp.dma_start(b.wgd[:, :, :], d.w_gla_gd).then_inc(here, 16)
                sp.dma_start(b.up[:, :], d.gate_up).then_inc(here, 16)

            @block.tensor
            def _(pe):
                pe.wait_ge(here, 32)
                for k in range(KT):
                    for c, (o, n) in enumerate(CH):
                        mm = pe.matmul(g.ps[0:16, c, 0:n], b.wgd[:, k, :], g.act[:, k, o:o + n], start=(k == 0), stop=(k == KT - 1))
                s.gd_ready.mark(mm)

            @block.scalar
            def _(act):
                s.gd_ready.next(act)
                for c, (o, n) in enumerate(CH):
                    act.activation(b.gd[:, o:o + n], g.ps[0:16, c, 0:n], ACT.Copy)
        for h in range(4):
            gla_project(g, d, b, s, h, here, v_here, st_here)
            gla_chunks(g, d, b, s, h, stored)
            gla_finish(g, d, b, s, h, here, stored)


def gla_project(g, d, b, s, h, here, v_here, st_here):
    nc = g.nc
    ps3 = lambda first: [(g.ps[:, first + c, 0:n], o, n) for c, (o, n) in enumerate(CH)]
    with nc.Block() as block:
        @block.sync
        def _(sp):
            sp.dma_start(b.wk[:, :, :], d.w_gla_qk[4 + h]).then_inc(here, 16)
            sp.dma_start(b.wq[:, :, :], d.w_gla_qk[h]).then_inc(here, 16)
            sp.dma_start(b.wv[:, :, :], d.w_gla_v[h]).then_inc(v_here, 16)
            sp.dma_start(b.st8[:, :, :], d.sgla[h]).then_inc(st_here, 16)
            sp.wait_ge(st_here, 16 * (h + 1))

        @block.tensor
        def _(pe):
            for p, o, n in ps3(0):
                mm = pe.matmul(p, b.up[:, h * P:h * P + P], b.gd[:, o:o + n], start=True, stop=True)
            s.logit.mark(mm)
            pe.wait_ge(here, 32 + 64 * h + 32)
            for w, first in ((b.wk, 3), (b.wq, 0)):
                if first == 0:
                    s.x_ready.next(pe)
                for k in range(KT):
                    for p, o, n in ps3(first):
                        mm = pe.matmul(p, w[:, k, :], g.act[:, k, o:o + n], start=(k == 0), stop=(k == KT - 1))
                s.product.mark(mm)
            pe.wait_ge(v_here, 16 * (h + 1))
            for t in range(9):
                R = P if t < 8 else NS
                if t >= 2:
                    s.v_out.next(pe)
                for k in range(KT):
                    mm = pe.matmul(g.ps[0:R, 6 + t % 2, 0:256], g.act[:, k, t * P:t * P + R], b.wv[:, k, :], start=(k == 0), stop=(k == KT - 1))
                s.v_ready.mark(mm)
            s.v_out.next(pe, 2)

        @block.scalar
        def _(act):
            s.x_ready.next(act)
            act.activation(b.e[:, :], b.cum[:, :], ACT.Abs)
            act.drain()
            act.activation(b.e[:, :], b.e[:, :], ACT.Exp, scale=-1.0)
            act.drain()
            s.soft.mark(act.activation(b.e[:, :], b.e[:, :], ACT.Ln, bias=g.ones[:, 0:1]))
            for x in (b.k, b.q):
                s.product.next(act)
                for p, o, n in ps3(3 if x is b.k else 0):
                    a = act.activation(x[:, o:o + n], p, ACT.Copy, scale=1.0 if x is b.k else float(P) ** -0.5)
            s.q_out.mark(a)
            for t in range(9):
                R = P if t < 8 else NS
                s.v_ready.next(act)
                s.v_out.mark(act.activation(b.v[0:R, t, :], g.ps[0:R, 6 + t % 2, 0:256], ACT.Copy))
            for i in range(4):
                s.cum_ready.next(act)
                s.exp_ready.mark(act.activation(b.e[:, :], b.e[:, :], ACT.Exp))
            act.activation(b.dec[:, :], b.ref[:, 1, :], ACT.Exp)

        @block.vector
        def _(dve):
            s.logit.next(dve)
            for p, o, n in ps3(0):
                m = dve.tensor_scalar(b.cum[:, o:o + n], p, g.col["gb"][:, h:h + 1], None, ALU.add)
            s.x_ready.mark(m)
            dve.drain()
            dve.tensor_scalar(b.kd[:, :], b.cum[:, :], 0.0, None, ALU.min)
            s.soft.next(dve)
            dve.drain()
            dve.tensor_tensor(b.kd[:, :], b.kd[:, :], b.e[:, :], ALU.subtract)
            dve.drain()
            dve.tensor_scalar(b.kd[:, :], b.kd[:, :], 1.0 / 16.0, None, ALU.mult)
            dve.drain()
            dve.tensor_tensor_scan(b.cum[:, :], g.scan, b.kd[:, :], 0.0, ALU.mult, ALU.add)
            dve.drain()
            cp, cs = b.cum[:, 0:NP].rearrange("p (c t) -> p c t", t=64), b.cum[:, NP:TOK].rearrange("p (c t) -> p c t", t=8)
            for i, (a, z) in enumerate(((31, 3), (63, 7))):
                dve.tensor_copy(b.ref[:, i, 0:16].unsqueeze(2), cp[:, :, a:a + 1])
                m = dve.tensor_copy(b.ref[:, i, 16:24].unsqueeze(2), cs[:, :, z:z + 1])
            dve.drain()
            s.q_out.next(dve)

            def exponent(i, sign):
                e = b.e
                if i is None:
                    return dve.tensor_copy(e[:, :], b.cum[:, :])
                r = b.ref[:, i, :]
                for lo, hi, size, ra in ((0, NP, 64, r[:, 0:16]), (NP, TOK, 8, r[:, 16:24])):
                    x = b.cum[:, lo:hi].rearrange("p (c t) -> p c t", t=size)
                    y = e[:, lo:hi].rearrange("p (c t) -> p c t", t=size)
                    ra = ra.unsqueeze(2).to_broadcast([P, (hi - lo) // size, size])
                    m = dve.tensor_tensor(y, x, ra, ALU.subtract) if sign > 0 else dve.tensor_tensor(y, ra, x, ALU.subtract)
                return m

            for i, sign, src, dst in ((0, 1, b.q, b.qs), (0, -1, b.k, b.ks), (None, 1, b.q, b.qe), (1, -1, b.k, b.kd)):
                s.cum_ready.mark(exponent(i, sign))
                s.exp_ready.next(dve)
                dve.tensor_tensor(dst[:, :], src[:, :], b.e[:, :], ALU.mult)
                dve.drain()


def gla_chunks(g, d, b, s, h, stored):
    nc = g.nc
    with nc.Block() as block:
        @block.tensor
        def _(pe):
            def first(t):
                R = P if t < 8 else NS
                for c in range(2 if t < 8 else 1):
                    x = slice(t * P + 64 * c, t * P + 64 * c + 64)
                    pe.matmul(g.ps[64 * c:64 * c + 64, 6 + t % 2, 0:64], b.ks[:, x], b.qs[:, x], start=True, stop=True)
                s.scored.mark(pe.transpose(g.ps[0:R, 6 + t % 2, P:2 * P], b.kd[:, t * P:t * P + R], g.ident))

            first(0)
            for t in range(9):
                s.turned_out.next(pe)
                if t + 1 < 9:
                    first(t + 1)
                if t < 8:
                    if t >= 1:
                        s.state.next(pe)
                    for c in range(2):
                        hr = slice(64 * c, 64 * c + 64)
                        mm = pe.matmul(g.ps[:, c, 0:256], b.kt[hr, t % 2, :], b.v[hr, t, :], start=True, stop=True)
                    s.outer.mark(mm)
                    if t >= 2:
                        s.o_out.next(pe)
                    for c in range(2):
                        hr = slice(64 * c, 64 * c + 64)
                        if c == 1:
                            s.state.next(pe)
                        for x in range(2):
                            p = g.ps[:, 2 + 2 * (t % 2) + c, 64 * x:64 * x + 64]
                            pe.matmul(p, b.v[hr, t, P * x:P * x + P], b.at[hr, t % 2, :], start=True, stop=False)
                            mm = pe.matmul(p, b.st[:, (2 * t + c) % 4, P * x:P * x + P], b.qe[:, t * P + 64 * c:t * P + 64 * c + 64], start=False, stop=True)
                    s.o_ready.mark(mm)
                else:
                    s.o_out.next(pe, 2)
                    s.state.next(pe)
                    for x in range(2):
                        p = g.ps[:, 4, P * x:P * x + 64]
                        pe.matmul(p, b.v[0:NS, 8, P * x:P * x + P], b.at[0:64, 0, :], start=True, stop=False)
                        for q in range(NB):
                            mm = pe.matmul(p[:, 8 * q:8 * q + 8], b.st8[:, q, P * x:P * x + P], b.qe[:, NP + 8 * q:NP + 8 * q + 8],
                                           start=False, stop=(q == NB - 1))
                    s.o_ready.mark(mm)
                    for q in range(NB):
                        mm = pe.matmul(g.ps[:, q // 2, 256 * (q % 2):256 * (q % 2) + 256], b.kt8[:, q, :], b.v[0:NS, 8, :], start=True, stop=True)
                    s.outer.mark(mm)
            s.o_out.next(pe)
            s.state.next(pe)

        @block.scalar
        def _(act):
            for t in range(9):
                s.o_ready.next(act)
                if t < 8:
                    for c in range(2):
                        at = t * P + 64 * c
                        a = act.activation(b.o[:, :, at:at + 64], g.ps[:, 2 + 2 * (t % 2) + c, 0:P].rearrange("p (x t) -> p x t", x=2), ACT.Copy)
                else:
                    a = act.activation(b.o[:, :, NP:TOK], g.ps[:, 4, 0:256].rearrange("p (x t) -> p x t", x=2)[:, :, 0:64], ACT.Copy)
                s.o_out.mark(a)

        @block.vector
        def _(dve):
            dve.memset(b.st[:, 0, :], 0.0)
            for t in range(9):
                R = P if t < 8 else NS
                s.scored.next(dve)
                m = dve.tensor_tensor(b.at[0:R, t % 2, :], g.ps[0:R, 6 + t % 2, 0:64], (g.upto if t < 8 else g.upto8)[0:R, :], ALU.mult)
                if t < 8:
                    m = dve.tensor_copy(b.kt[0:R, t % 2, :], g.ps[0:R, 6 + t % 2, P:2 * P])
                else:
                    m = dve.tensor_tensor(b.kt8[:, :, :], g.ps[0:NS, 6, P:2 * P].unsqueeze(1).to_broadcast([NS, NB, P]),
                                          g.brow[0:NS, :].unsqueeze(2).to_broadcast([NS, NB, P]), ALU.mult)
                s.turned_out.mark(m)
                if t >= 1:
                    s.o_ready.next(dve)
                if t < 8:
                    s.outer.next(dve)
                    for c in range(2):
                        n = 2 * t + c
                        dve.drain()
                        m = dve.scalar_tensor_tensor(b.st[:, (n + 1) % 4, :], b.st[:, n % 4, :], b.dec[:, n:n + 1],
                                                     g.ps[:, c, 0:256], ALU.mult, ALU.add)
                        s.state.mark(m)
                else:
                    s.outer.next(dve)
                    dve.tensor_tensor(b.st8[:, :, :], b.st8[:, :, :], b.dec[:, 16:24].unsqueeze(2).to_broadcast([P, NB, 256]), ALU.mult)
                    dve.drain()
                    s.state.mark(dve.tensor_tensor(b.st8[:, :, :].rearrange("p (a q) t -> p a (q t)", q=2), b.st8[:, :, :].rearrange("p (a q) t -> p a (q t)", q=2),
                                                   g.ps[:, 0:4, :], ALU.add))
            s.o_ready.next(dve)

        @block.sync
        def _(sp):
            s.state.next(sp, 17)
            sp.dma_start(d.gl_p[h], b.st[:, 0, :]).then_inc(stored, 16)
            sp.dma_start(d.gl_s[h], b.st8[:, :, :]).then_inc(stored, 16)
            sp.wait_ge(stored, 64 * h + 32)


def gla_finish(g, d, b, s, h, here, stored):
    nc = g.nc
    ps3 = lambda first: [(g.ps[:, first + c, 0:n], o, n) for c, (o, n) in enumerate(CH)]
    w = (b.wq, b.wk)
    silu = (b.qs, b.ks)
    sq = (b.qe, b.kd)
    with nc.Block() as block:
        @block.sync
        def _(sp):
            for x in range(2):
                sp.dma_start(w[x][:, :, :], d.w_gla_r[2 * h + x]).then_inc(here, 16)
            for x in range(2):
                s.gated.next(sp)
                sp.dma_start(d.gla_out[:, 2 * h + x, :], b.o[:, x, :]).then_inc(stored, 16)
            sp.wait_ge(stored, 64 * (h + 1))

        @block.tensor
        def _(pe):
            s.squared.next(pe)
            for x in range(2):
                for p, o, n in ps3(0):
                    mm = pe.matmul(p, g.ones, sq[x][:, o:o + n], start=(x == 0), stop=(x == 1))
            s.mean_ready.mark(mm)
            pe.wait_ge(here, 64 * (h + 1) + 32)
            for x in range(2):
                if x == 1:
                    s.root.next(pe)
                for k in range(KT):
                    for p, o, n in ps3(3 - 3 * x):
                        mm = pe.matmul(p, w[x][:, k, :], g.act[:, k, o:o + n], start=(k == 0), stop=(k == KT - 1))
                s.r_ready.mark(mm)

        @block.scalar
        def _(act):
            act.activation(sq[0][:, :], b.o[:, 0, :], ACT.Square)
            s.squared.mark(act.activation(sq[1][:, :], b.o[:, 1, :], ACT.Square))
            s.mean_ready.next(act)
            for p, o, n in ps3(0):
                a = act.activation(b.e[:, o:o + n], p, ACT.Sqrt, bias=g.col["eps"], scale=1.0 / 256)
            s.root.mark(a)
            for x in range(2):
                s.r_ready.next(act)
                for p, o, n in ps3(3 - 3 * x):
                    a = act.activation(silu[x][:, o:o + n], p, ACT.Silu)
                s.r_out.mark(a)

        @block.vector
        def _(dve):
            s.root.next(dve)
            dve.reciprocal(b.e[:, :], b.e[:, :])
            dve.drain()
            for x in range(2):
                dve.scalar_tensor_tensor(b.o[:, x, :], b.o[:, x, :], g.col["gn"][:, x:x + 1], b.e[:, :], ALU.mult, ALU.mult)
            dve.drain()
            for x in range(2):
                s.r_out.next(dve)
                s.gated.mark(dve.tensor_tensor(b.o[:, x, :], b.o[:, x, :], silu[x][:, :], ALU.mult))


def split_buffers(g, ctx, name):
    return [ctx.enter_context(g.nc.sbuf_tensor(name + part, [P, KT, TOK], F32R)) for part in ("_high", "_low")]


def program(nc, d, shapes):
    with ExitStack() as ctx:
        g = allocate(nc, ctx)
        load_inputs(g, d)
        for layer in range(2):
            g.layer = layer
            with ExitStack() as mixer:
                m = allocate_mixer(g, mixer, shapes)
                rmsnorm(m, f"mix{layer}", g.col["mix"][:, KT * layer:KT * layer + KT], (m.act,), d.const)
                if layer == 0:
                    rwkv_mix(m, d)
                    with ExitStack() as nsa:
                        nsa_layer_buffers(m, nsa)
                        nsa_project(m, d)
                        nsa_compress(m, d)
                        nsa_prompt(m, d)
                        nsa_sample(m, d)
                else:
                    gla_mix(m, d)
                with ExitStack() as out:
                    ah, al = split_buffers(g, out, f"out{layer}")
                    project_out(g, layer, m.act, ah, al, (d.w_out_even, d.w_out_odd)[layer], (d.rwkv_out, d.gla_out)[layer], (4, 0)[layer])
            with ExitStack() as ffn:
                ah, al = split_buffers(g, ffn, f"ffn{layer}")
                rmsnorm(g, f"ffn{layer}", g.col["ffn"][:, KT * layer:KT * layer + KT], (ah, al))
                feed_forward(g, layer, ah, al, d.wg[layer], d.wu[layer], d.wd[layer])
        store_tokens(g, d)


def store_tokens(g, d):
    with g.nc.Block() as block:
        @block.sync
        def _(sp):
            sp.dma_start(d.y, g.resid[:, :, :]).then_inc(g.tokens_moved, 16)
            sp.dma_start(d.win_rows, d.cache_win_rows[:, 8:512, :]).then_inc(g.tokens_moved, 16)
            sp.wait_ge(g.tokens_moved, 64 + 32)


def pack(inp):
    inp = {k: np.asarray(v) for k, v in inp.items()}
    out = {}

    def weight(w, n):
        a, b = w.shape
        return np.ascontiguousarray(w.reshape(a // P, P, b // n, n).transpose(2, 1, 0, 3))

    def column(v):
        return v.reshape(-1, P).T

    x = np.concatenate([inp["x_prompt"].reshape(NP, D), inp["x_sample"].reshape(NS, D)])
    out["x"] = np.ascontiguousarray(x.T.reshape(KT, P, TOK).transpose(1, 0, 2))
    out["const"] = np.concatenate([v.reshape(P, -1) for v in _constants().values()], axis=1)
    w = inp["w_in_even"][0]
    q = w[:, 0:512].reshape(D, 2, 4, HD).transpose(0, 2, 1, 3).reshape(D, 512)
    kv = w[:, 512:1280].reshape(D, 3, 2, P)
    nsa = np.concatenate([q, kv[:, :, 0].reshape(D, 384), kv[:, :, 1].reshape(D, 384), w[:, 1280:1304]], axis=1)
    out["w_nsa"] = np.ascontiguousarray(nsa.reshape(KT, P, NSAW).transpose(1, 0, 2))
    order = np.concatenate([np.arange(1536, 1792)] + [np.arange(P) + 512 * s + P * j for j in range(4) for s in range(3)])
    out["w_rwkv"] = weight(w[:, 1304:][:, order], P)
    out["qk_gain"] = np.concatenate([np.tile(inp["nsa_qnorm"][0], 8), np.tile(inp["nsa_knorm"][0][:, None, :], (1, 2, 1)).reshape(-1)])
    out["cmp_w1"] = np.ascontiguousarray(inp["cmp_w1"][0].reshape(2, 16, P, P).transpose(2, 0, 1, 3))
    out["cmp_w2"] = np.ascontiguousarray(inp["cmp_w2"][0].transpose(1, 0, 2))
    out["cmp_pe"] = np.ascontiguousarray(inp["cmp_pe"][0].reshape(2, 16, P).transpose(2, 0, 1))
    cache = inp["cache_nsa_kv"][0]
    out["cache_cmp"] = np.ascontiguousarray(cache[:, :, 0:2].reshape(80, 64, 2, 2, 2, HD).transpose(0, 2, 5, 3, 4, 1).reshape(80, P, 4, 64))
    out["cache_slc"] = np.ascontiguousarray(np.concatenate([cache[:, :, 2].reshape(80, P, P).transpose(0, 2, 1), cache[:, :, 3].reshape(80, P, P)], axis=2))
    win = inp["cache_nsa_win"][0].reshape(NB, 4, P, 2, P)
    out["cache_win"] = np.ascontiguousarray(np.concatenate([win[:, :, :, 0].transpose(0, 3, 1, 2), win[:, :, :, 1].transpose(0, 2, 1, 3)], axis=3))
    out["cache_win_rows"] = np.ascontiguousarray(inp["cache_nsa_win"][0].reshape(NB, 512, 2 * P))
    out["pages"] = np.ascontiguousarray(inp["page_table"].reshape(1, NB * 8))
    out["shift"] = np.ascontiguousarray(inp["state_rwkv_shift"][0][:, order].reshape(NB, RT, P).transpose(2, 1, 0))
    out["lora"] = np.concatenate([np.concatenate([inp["rwkv_wB"][0], inp["rwkv_aB"][0]]), inp["rwkv_gB"][0]], axis=1)
    out["srwkv"] = np.ascontiguousarray(inp["state_rwkv"][0].reshape(NB, 4, 2, HD, HD).transpose(1, 2, 4, 0, 3).reshape(4, P, NB, HD))
    wo = inp["w_in_odd"][0]
    out["w_gla_qk"] = weight(wo[:, 0:1024], P)
    out["w_gla_v"] = np.ascontiguousarray(wo[:, 1024:2048].reshape(KT, P, 4, 256).transpose(2, 1, 0, 3))
    out["w_gla_gd"] = np.ascontiguousarray(wo[:, 2048:2064].reshape(KT, P, 16).transpose(1, 0, 2))
    out["w_gla_r"] = weight(wo[:, 2064:3088], P)
    out["gate_up"] = inp["gla_gate_up"][0]
    out["sgla"] = np.ascontiguousarray(inp["state_gla"][0].transpose(1, 2, 0, 3))
    out["w_out_even"] = weight(inp["w_out_even"][0], P)
    out["w_out_odd"] = weight(inp["w_out_odd"][0], P)
    out["wg"] = np.stack([weight(inp["ffn_gate"][i], P) for i in range(2)])
    out["wu"] = np.stack([weight(inp["ffn_up"][i], P) for i in range(2)])
    out["wd"] = np.stack([weight(inp["ffn_down"][i], P) for i in range(2)])
    cols = {"mix": inp["norm_mix"], "ffn": inp["norm_ffn"], "mu": inp["rwkv_mu"][0][order], "w0": inp["rwkv_w0"], "a0": inp["rwkv_a0"],
            "kk": inp["rwkv_kk"], "ka": inp["rwkv_ka"], "rk": inp["rwkv_rk"], "lnw": inp["rwkv_ln_w"], "lnb": inp["rwkv_ln_b"],
            "gb": inp["gla_gate_b"], "gn": inp["gla_norm"], "eps": np.full(P, EPS, np.float32), "gneps": np.full(P, GN_EPS, np.float32)}
    out["param"] = np.concatenate([column(cols[n]) for n, _ in PARAMS], axis=1)
    return {k: np.ascontiguousarray(v) for k, v in out.items()}


SCRATCH = {"gate_rows": (NS, 24), "rwkv_out": (P, 4, TOK), "gla_out": (P, KT, TOK)}
OUTS = {"y": (P, KT, TOK), "kv": (TOK, 768), "win_rows": (NB, 504, 2 * P), "last": (P, RT, 9),
        "rw_p": (4, P, HD), "rw_s": (4, P, NB, HD), "gl_p": (4, P, 256), "gl_s": (4, P, NB, 256)}


def kernel(**inputs):
    import concourse.bacc as _bacc
    from concourse.bass_utils import run_bass_kernel_spmd as _run

    nc = _bacc.Bacc("TRN2", target_bir_lowering=False, num_devices=1)
    arrays = pack(inputs)
    d = {n: nc.dram_tensor(f"in_{n}", a.shape, mybir.dt.from_np(a.dtype), kind="ExternalInput").ap() for n, a in arrays.items()}
    d |= {n: nc.dram_tensor(f"out_{n}", s, F32, kind="ExternalOutput").ap() for n, s in OUTS.items()}
    d |= {n: nc.dram_tensor(f"scratch_{n}", s, F32, kind="Internal").ap() for n, s in SCRATCH.items()}
    program(nc, names(**d), {k: v.shape for k, v in _constants().items()})
    r = _run(nc, [{f"in_{n}": a for n, a in arrays.items()}], core_ids=[0]).results[0]
    o = {n: r[f"out_{n}"] for n in OUTS}
    y = o["y"].transpose(2, 1, 0).reshape(TOK, D)
    k, v = o["kv"][:, 0:384].reshape(TOK, 3, 1, 2, HD), o["kv"][:, 384:768].reshape(TOK, 3, 1, 2, HD)
    kv = np.concatenate([k, v], axis=2)
    rows, win = kv[:, 0:2].reshape(TOK, 4, 2, HD), kv[:, 2]
    win_s = np.concatenate([o["win_rows"].reshape(NB, 504, 2, 2, HD), win[NP:].reshape(NB, SS, 2, 2, HD)], axis=1)
    last = o["last"].transpose(2, 1, 0).reshape(9, RT * P)
    order = np.concatenate([np.arange(1536, 1792)] + [np.arange(P) + 512 * s + P * j for j in range(4) for s in range(3)])
    last = last[:, np.argsort(order)]
    rw_p = o["rw_p"].reshape(4, 2, HD, HD).transpose(0, 1, 3, 2).reshape(1, 1, 8, HD, HD)
    rw_s = o["rw_s"].reshape(4, 2, HD, NB, HD).transpose(3, 0, 1, 4, 2).reshape(1, NB, 8, HD, HD)
    out = (y[:NP].reshape(1, NP, D), y[NP:].reshape(NB, SS, D), rows[:NP].reshape(1, 1, NP, 4, 2, HD),
           rows[NP:].reshape(1, NB, SS, 4, 2, HD), win[NP - 512:NP].reshape(1, 1, 512, 2, 2, HD), win_s[None],
           rw_p, rw_s, last[8:9][None], last[0:8][None], o["gl_p"][None, None], o["gl_s"].transpose(2, 0, 1, 3)[None])
    return tuple(np.ascontiguousarray(a) for a in out)
```

```python
from contextlib import ExitStack

import numpy as np

import concourse.bass as bass
from concourse import mybir

F32 = mybir.dt.float32
F32R = mybir.dt.float32r
I32 = mybir.dt.int32
ALU = mybir.AluOpType
ACT = mybir.ActivationFunctionType
AX = mybir.AxisListType.X
ds = bass.ds

P = 128
D = 1024
KT = D // P
NP = 1024
NB, SS = 8, 8
NS = NB * SS
TOK = NP + NS
HD = 64
FF = 2816
FT = FF // P
PARTS = ((0, 5), (5, 5), (10, 4), (14, 4), (18, 4))
CH = ((0, 384), (384, 384), (768, 320))
NCMP = 63
NSEL = 17
NEG = -1e30
KSETS = 3
QK = 512 + KSETS * P
NSAW = QK + KSETS * P + 24
RT = 14
EPS = 1e-6
GN_EPS = 64e-5


def _constants():
    i = np.arange(P)
    t64, c64 = i[:, None] % 64, np.arange(64)[None, :]
    same8 = (t64 // 8) == (c64 // 8)
    parts = {
        "ident": np.eye(P),
        "blk": (i[:, None] // 64 == i[None, :] // 64) * 1.0,
        "ones": np.ones((P, P)),
        "causal": np.where(i[None, :] <= i[:, None], 0.0, NEG),
        "window": np.where(i[None, :] > i[:, None], 0.0, NEG),
        "cmpmask": np.where(16 * np.arange(NCMP)[None, None, :] + 31 <= (i[:, None] + 128 * np.arange(8)[None, :])[:, :, None], 0.0, NEG),
        "seen": (i[:, None] >= 31) * 1.0,
        "id2": (t64 == c64) * 1.0,
        "below": (c64 < t64) * 1.0,
        "above": (c64 > t64) * 1.0,
        "upto": (c64 >= t64) * 1.0,
        "below8": (c64 < t64) * same8 * 1.0,
        "above8": (c64 > t64) * same8 * 1.0,
        "upto8": (c64 >= t64) * same8 * 1.0,
        "bcol": np.broadcast_to((np.arange(8)[:, None] == c64[0][None, :] // 8) * 1.0, (P, 8, 64)),
        "brow": (t64 // 8 == np.arange(8)[None, :]) * 1.0,
        "smask": np.where(np.arange(8)[None, :] <= i[:, None] % 8, 0.0, NEG),
        "swmask": np.where(np.arange(8)[None, :] > i[:, None] % 8, 0.0, NEG),
        "selmap": ((16 * i[:, None] <= 64 * np.arange(NSEL)[None, :] + 63) & (16 * i[:, None] + 31 >= 64 * np.arange(NSEL)[None, :]) & (i[:, None] < NCMP)) * 1.0,
        "samerow": ((i[:, None] // 32 == i[None, :] // 32) & (i[:, None] % 8 == i[None, :] % 8)) * 1.0,
        "blkid": np.broadcast_to(np.arange(NSEL)[None, :] * 1.0, (P, NSEL)),
        "scan": np.broadcast_to(np.where(np.arange(TOK) < NP, np.arange(TOK) % 64, np.arange(TOK) % 8)[None, :] != 0, (P, TOK)) * 1.0,
    }
    half = 8
    inv = (np.float32(500000.0) ** (-np.arange(half, dtype=np.float32) / np.float32(half))).astype(np.float32)
    pos = np.concatenate([np.arange(NP), 1024 + np.arange(NS) % SS, np.zeros(64)]).astype(np.float32)
    ang = pos[:, None] * inv[None, :]
    rope = np.concatenate([np.cos(ang), np.sin(ang)], axis=1).reshape(9, P, 16).transpose(1, 0, 2)
    parts["rope"] = rope
    return {k: np.ascontiguousarray(v, dtype=np.float32) for k, v in parts.items()}


PARAMS = (("mix", 16), ("ffn", 16), ("mu", 14), ("w0", 4), ("a0", 4), ("kk", 4), ("ka", 4), ("rk", 4),
          ("lnw", 4), ("lnb", 4), ("gb", 4), ("gn", 2), ("eps", 1), ("gneps", 1))


def names(**items):
    return type("Names", (), items)()


class Signal:

    def __init__(self, nc, ctx, name):
        self.sem = ctx.enter_context(nc.semaphore(name))
        self.waited = {}

    def mark(self, instruction):
        instruction.then_inc(self.sem, 1)

    def next(self, engine, n=1):
        who = str(engine.engine)
        self.waited[who] = self.waited.get(who, 0) + n
        engine.wait_ge(self.sem, self.waited[who])


def signals(nc, ctx, prefix, listed):
    return names(**{n: Signal(nc, ctx, prefix + n) for n in listed.split()})


def allocate(nc, ctx):
    sb = lambda name, shape: ctx.enter_context(nc.sbuf_tensor(name, shape, F32))
    sem = lambda n: ctx.enter_context(nc.semaphore(n))
    param = sb("param", [P, sum(n for _, n in PARAMS)])
    col, at = {}, 0
    for name, n in PARAMS:
        col[name] = param[:, at:at + n]
        at += n
    g = names(nc=nc, param=param, col=col, resid=sb("resid", [P, KT, TOK]), mean=sb("mean", [P, P]))
    g.norm_signals = signals(nc, ctx, "norm_", "squared mean_ready root_ready normed rounded")
    g.split_signals = signals(nc, ctx, "split_", "high both")
    g.const_here, g.tokens_moved = sem("const_here"), sem("tokens_moved")
    g.acts_here = [sem(f"acts_here{i}") for i in range(2)]
    g.ff_sems = names(**{n: sem("ff_" + n) for n in (
        "gate_here", "up_here", "down_here0", "down_here1", "gate_hi", "up_hi", "down_hi", "gate_lo", "up_lo", "down_lo",
        "gate_done", "up_done", "down_done", "gate_out", "up_out", "down_out", "hid_ready")})
    g.out_sems = names(**{n: sem("wo_" + n) for n in ("here0", "here1", "hi", "lo", "done", "out")})
    g.ps = ctx.enter_context(nc.psum_tensor("ps", [P, 8, 512], F32))
    return g


def allocate_mixer(g, ctx, shapes):
    sb = lambda name, shape: ctx.enter_context(g.nc.sbuf_tensor(name, shape, F32))
    layer = g.layer
    const = sb(f"const{layer}", [P, sum(int(np.prod(s[1:])) for s in shapes.values())])
    items, at = {}, 0
    for name, s in shapes.items():
        n = int(np.prod(s[1:]))
        v = const[:, at:at + n]
        items[name] = v.rearrange("p (a b) -> p a b", b=s[2]) if len(s) == 3 else v
        at += n
    m = names(nc=g.nc, const=const, col=g.col, resid=g.resid, mean=g.mean, ps=g.ps, norm_signals=g.norm_signals,
              const_here=g.const_here, acts_here=g.acts_here, layer=layer, act=sb(f"act{layer}", [P, KT, TOK]), **items)
    return m


def load_inputs(g, d):
    nc = g.nc
    with nc.Block() as block:
        @block.sync
        def _(sp):
            for c, (o, n) in enumerate(CH):
                sp.dma_start(g.resid[:, :, o:o + n], d.x[:, :, o:o + n]).then_inc(g.tokens_moved, 16)
            sp.dma_start(g.param[:, :], d.param).then_inc(g.tokens_moved, 16)
            sp.wait_ge(g.tokens_moved, 64)

        @block.gpsimd
        def _(pool):
            pool.memset(g.mean[:, :], 1.0 / D)


def rmsnorm(g, name, gain, out, const=None):
    nc = g.nc
    s = g.norm_signals
    pair = len(out) == 2
    with ExitStack() as ctx:
        sq = ctx.enter_context(nc.sbuf_tensor(name + "sq", [P, 2, KT, 384], F32))
        rs = ctx.enter_context(nc.sbuf_tensor(name + "rs", [P, 3, 384], F32))
        normed = ctx.enter_context(nc.sbuf_tensor(name + "normed", [P, KT if pair else 1, 384], F32))
        block = ctx.enter_context(nc.Block())
        if const is not None:
            @block.sync
            def _(sp):
                sp.dma_start(g.const[:, :], const).then_inc(g.const_here, 16)
                sp.wait_ge(g.const_here, 16 * (g.layer + 1))

        @block.scalar
        def _(act):
            def square(c):
                o, n = CH[c]
                s.squared.mark(act.activation(sq[:, c % 2, :, 0:n], g.resid[:, :, o:o + n], ACT.Square))

            square(0)
            square(1)
            for c, (o, n) in enumerate(CH):
                s.mean_ready.next(act)
                s.root_ready.mark(act.activation(rs[:, c, 0:n], g.ps[:, c, 0:n], ACT.Sqrt, bias=g.col["eps"]))
                if c == 0:
                    square(2)
                if pair:
                    s.normed.next(act)
                    s.rounded.mark(act.activation(out[0][:, :, o:o + n], normed[:, :, 0:n], ACT.Copy))

        @block.tensor
        def _(pe):
            for c, (o, n) in enumerate(CH):
                s.squared.next(pe)
                for k in range(KT):
                    mm = pe.matmul(g.ps[:, c, 0:n], g.mean[:, :], sq[:, c % 2, k, 0:n], start=(k == 0), stop=(k == KT - 1))
                s.mean_ready.mark(mm)

        @block.vector
        def _(dve):
            for c, (o, n) in enumerate(CH):
                s.root_ready.next(dve)
                dve.reciprocal(rs[:, c, 0:n], rs[:, c, 0:n])
                dve.drain()
                for k in range(KT):
                    to = out[0][:, k, o:o + n] if not pair else normed[:, k, 0:n]
                    m = dve.scalar_tensor_tensor(to, g.resid[:, k, o:o + n], gain[:, k:k + 1],
                                                 rs[:, c, 0:n], ALU.mult, ALU.mult)
                if pair:
                    s.normed.mark(m)
                    s.rounded.next(dve)
                    dve.tensor_tensor(out[1][:, :, o:o + n], normed[:, :, 0:n], out[0][:, :, o:o + n].bitcast(F32), ALU.subtract)


def products(pe, g, bank, hi, lo, k, xh, xl, kx, first, last):
    passes = ((hi, xh), (lo, xh), (hi, xl))
    for i, (w, x) in enumerate(passes):
        for c, (o, n) in enumerate(CH):
            mm = pe.matmul(g.ps[:, bank + c, 0:n], w[:, k, :], x[:, kx, o:o + n],
                           start=(first and i == 0), stop=(last and i == 2))
    return mm


def feed_forward(g, layer, ah, al, w_gate, w_up, w_down):
    nc = g.nc
    name = f"ff{layer}_"
    F0, D0 = layer * FT, layer * len(PARTS) * KT
    s = g.ff_sems
    with ExitStack() as ctx:
        sb = lambda n, shape, dt=F32: ctx.enter_context(nc.sbuf_tensor(name + n, shape, dt))
        NF = PARTS[0][1]
        wg, wu = sb("wg", [P, KT, P]), sb("wu", [P, KT, P])
        gh, gl, uh, ul = (sb(n, [P, KT, P], F32R) for n in ("gh", "gl", "uh", "ul"))
        wd = [sb(f"wd{i}", [P, NF, P]) for i in range(2)]
        dh = [sb(f"dh{i}", [P, NF, P], F32R) for i in range(2)]
        dl = [sb(f"dl{i}", [P, NF, P], F32R) for i in range(2)]
        down_here = (s.down_here0, s.down_here1)
        silu, prod = sb("silu", [P, TOK]), sb("prod", [P, TOK])
        hh, hl = sb("hh", [P, NF, TOK], F32R), sb("hl", [P, NF, TOK], F32R)
        flat = lambda x: x.rearrange("p a n -> p (a n)")
        block = ctx.enter_context(nc.Block())

        @block.sync
        def _(sp):
            sp.dma_start(wg[:, :, :], w_gate[0]).then_inc(s.gate_here, 16)
            sp.dma_start(wu[:, :, :], w_up[0]).then_inc(s.up_here, 16)
            with sp.Fori(1, FT) as i:
                sp.wait_ge(s.gate_lo, i + F0)
                sp.dma_start(wg[:, :, :], w_gate[ds(i, 1)].rearrange("a p k n -> (a p) k n")).then_inc(s.gate_here, 16)
                sp.wait_ge(s.up_lo, i + F0)
                sp.dma_start(wu[:, :, :], w_up[ds(i, 1)].rearrange("a p k n -> (a p) k n")).then_inc(s.up_here, 16)

        @block.gpsimd
        def _(pool):
            def low_gate_up(f):
                pool.wait_ge(s.gate_hi, f + 1)
                pool.tensor_tensor(gl[:, :, :], wg[:, :, :], gh[:, :, :].bitcast(F32), ALU.subtract).then_inc(s.gate_lo, 1)
                pool.wait_ge(s.up_hi, f + 1)
                pool.tensor_tensor(ul[:, :, :], wu[:, :, :], uh[:, :, :].bitcast(F32), ALU.subtract).then_inc(s.up_lo, 1)

            def low_down(n, t, nf):
                pool.wait_ge(s.down_hi, n + 1)
                pool.tensor_tensor(dl[t][:, 0:nf, :], wd[t][:, 0:nf, :], dh[t][:, 0:nf, :].bitcast(F32), ALU.subtract).then_inc(s.down_lo, 1)

            for part, (f0, nf) in enumerate(PARTS):
                n0 = D0 + part * KT
                for t in range(2):
                    if n0 > 0:
                        pool.wait_ge(s.down_lo, n0)
                    pool.dma_start(wd[t][:, 0:nf, :], w_down[t, :, f0:f0 + nf, :]).then_inc(down_here[t], 16)
                if part == 0:
                    low_gate_up(F0)
                for t in range(2):
                    low_down(n0 + t, t, nf)
                with pool.Fori(0, nf - (part == len(PARTS) - 1)) as i:
                    low_gate_up(i + F0 + f0 + 1)
                with pool.Fori(1, KT // 2) as i:
                    for t in range(2):
                        pool.wait_ge(s.down_lo, 2 * i + n0 + t - 1)
                        pool.dma_start(wd[t][:, 0:nf, :], w_down[ds(2 * i + t, 1), :, f0:f0 + nf, :]
                                       .rearrange("a p k n -> (a p) k n")).then_inc(down_here[t], 16)
                    for t in range(2):
                        low_down(2 * i + n0 + t, t, nf)

        @block.tensor
        def _(pe):
            for part, (f0, nf) in enumerate(PARTS):
                n0 = D0 + part * KT
                pe.wait_ge(s.down_out, n0 + 2)
                with pe.Fori(0, nf) as i:
                    f = i + F0 + f0
                    pe.wait_ge(s.gate_lo, f + 1)
                    pe.wait_ge(s.gate_out, f + 1)
                    for k in range(KT):
                        mm = products(pe, g, 0, gh, gl, k, ah, al, k, k == 0, k == KT - 1)
                    mm.then_inc(s.gate_done, 1)
                    pe.wait_ge(s.up_lo, f + 1)
                    pe.wait_ge(s.up_out, f + 1)
                    for k in range(KT):
                        mm = products(pe, g, 3, uh, ul, k, ah, al, k, k == 0, k == KT - 1)
                    mm.then_inc(s.up_done, 1)
                pe.wait_ge(s.hid_ready, F0 + f0 + nf)
                with pe.Fori(0, KT // 2) as i:
                    for t in range(2):
                        n = 2 * i + n0 + t
                        pe.wait_ge(s.down_lo, n + 1)
                        pe.wait_ge(s.down_out, n + 1)
                        for k in range(nf):
                            mm = products(pe, g, 3 * t, dh[t], dl[t], k, hh, hl, k, k == 0, k == nf - 1)
                        mm.then_inc(s.down_done, 1)

        @block.scalar
        def _(act):
            def high_gate(f):
                act.wait_ge(s.gate_here, 16 * (f + 1))
                act.activation(gh[:, :, :], wg[:, :, :], ACT.Copy).then_inc(s.gate_hi, 1)

            def high_up(f):
                act.wait_ge(s.up_here, 16 * (f + 1))
                act.activation(uh[:, :, :], wu[:, :, :], ACT.Copy).then_inc(s.up_hi, 1)

            def high_down(n, t, nf, here):
                act.wait_ge(down_here[t], 16 * here)
                act.activation(dh[t][:, 0:nf, :], wd[t][:, 0:nf, :], ACT.Copy).then_inc(s.down_hi, 1)

            def swish(f):
                act.wait_ge(s.gate_done, f + 1)
                act.wait_ge(s.up_out, f + 1)
                for c, (o, n) in enumerate(CH):
                    a = act.activation(silu[:, o:o + n], g.ps[:, c, 0:n], ACT.Silu)
                a.then_inc(s.gate_out, 1)

            if layer == 0:
                act.sem_inc(s.gate_out, 1)
            high_gate(F0)
            high_up(F0)
            for part, (f0, nf) in enumerate(PARTS):
                n0 = D0 + part * KT
                if n0 > 0:
                    act.wait_ge(s.down_done, n0)
                for t in range(2):
                    high_down(n0 + t, t, nf, n0 // 2 + 1)
                last = part == len(PARTS) - 1
                with act.Fori(0, nf - last) as i:
                    f = i + F0 + f0
                    swish(f)
                    high_gate(f + 1)
                    act.wait_ge(s.up_done, f + 1)
                    high_up(f + 1)
                if last:
                    swish(F0 + FT - 1)
                with act.Fori(1, KT // 2) as i:
                    for t in range(2):
                        act.wait_ge(s.down_done, 2 * i + n0 + t - 1)
                        high_down(2 * i + n0 + t, t, nf, i + n0 // 2 + 1)

        @block.vector
        def _(dve):
            if layer == 0:
                dve.sem_inc(s.up_out, 1)
                dve.sem_inc(s.down_out, 2)
            for part, (f0, nf) in enumerate(PARTS):
                n0 = D0 + part * KT
                with dve.Fori(0, nf) as i:
                    f = i + F0 + f0
                    dve.wait_ge(s.gate_out, f + 2)
                    dve.wait_ge(s.up_done, f + 1)
                    for c, (o, n) in enumerate(CH):
                        m = dve.tensor_tensor(prod[:, o:o + n], silu[:, o:o + n], g.ps[:, 3 + c, 0:n], ALU.mult)
                    m.then_inc(s.up_out, 1)
                    dve.drain()
                    dve.tensor_copy(flat(hh[:, ds(i, 1), :]), prod[:, :])
                    dve.drain()
                    dve.tensor_tensor(flat(hl[:, ds(i, 1), :]), prod[:, :], flat(hh[:, ds(i, 1), :].bitcast(F32)), ALU.subtract)\
                       .then_inc(s.hid_ready, 1)
                    dve.drain()
                with dve.Fori(0, KT // 2) as i:
                    for t in range(2):
                        dve.wait_ge(s.down_done, 2 * i + n0 + t + 1)
                        for c, (o, n) in enumerate(CH):
                            r = flat(g.resid[:, ds(2 * i + t, 1), o:o + n])
                            m = dve.tensor_tensor(r, r, g.ps[:, 3 * t + c, 0:n], ALU.add)
                        m.then_inc(s.down_out, 1)


def project_out(g, layer, act_in, ah, al, w, waiting, first):
    nc = g.nc
    T0 = layer * KT
    name = f"out{layer}_"
    s = g.out_sems
    here = (s.here0, s.here1)
    per = (KT - first) // 2
    starts = list(range(first, KT, per))
    split = g.split_signals
    with ExitStack() as ctx:
        wo = [ctx.enter_context(nc.sbuf_tensor(name + f"w{i}", [P, KT, P], F32)) for i in range(2)]
        oh = [ctx.enter_context(nc.sbuf_tensor(name + f"h{i}", [P, KT, P], F32R)) for i in range(2)]
        ol = [ctx.enter_context(nc.sbuf_tensor(name + f"l{i}", [P, KT, P], F32R)) for i in range(2)]
        block = ctx.enter_context(nc.Block())

        @block.sync
        def _(sp):
            for part, k in enumerate(starts):
                sp.dma_start(act_in[:, k:k + per, :], waiting[:, k - first:k - first + per, :]).then_inc(g.acts_here[part], 16)
            for t in range(2):
                sp.dma_start(wo[t][:, :, :], w[t]).then_inc(here[t], 16)
            with sp.Fori(1, KT // 2) as i:
                for t in range(2):
                    sp.wait_ge(s.lo, 2 * i + (T0 + t - 1))
                    sp.dma_start(wo[t][:, :, :], w[ds(2 * i + t, 1)].rearrange("a p k n -> (a p) k n")).then_inc(here[t], 16)

        @block.gpsimd
        def _(pool):
            with pool.Fori(0, KT // 2) as i:
                for t in range(2):
                    pool.wait_ge(s.hi, 2 * i + T0 + t + 1)
                    pool.tensor_tensor(ol[t][:, :, :], wo[t][:, :, :], oh[t][:, :, :].bitcast(F32), ALU.subtract).then_inc(s.lo, 1)

        @block.tensor
        def _(pe):
            for t in range(2):
                pe.wait_ge(s.lo, T0 + t + 1)
                pe.wait_ge(s.out, T0 + t + 1)
                for k in range(KT):
                    if t == 0:
                        split.both.next(pe)
                    mm = products(pe, g, 3 * t, oh[t], ol[t], k, ah, al, k, k == 0, k == KT - 1)
                mm.then_inc(s.done, 1)
            with pe.Fori(1, KT // 2) as i:
                for t in range(2):
                    pe.wait_ge(s.lo, 2 * i + T0 + t + 1)
                    pe.wait_ge(s.out, 2 * i + T0 + t + 1)
                    for k in range(KT):
                        mm = products(pe, g, 3 * t, oh[t], ol[t], k, ah, al, k, k == 0, k == KT - 1)
                    mm.then_inc(s.done, 1)

        @block.scalar
        def _(act):
            for t in range(2):
                act.wait_ge(here[t], 16 * (T0 // 2 + 1))
                act.activation(oh[t][:, :, :], wo[t][:, :, :], ACT.Copy).then_inc(s.hi, 1)
            for k in range(KT):
                if k in starts:
                    act.wait_ge(g.acts_here[starts.index(k)], 16 * (layer + 1))
                split.high.mark(act.activation(ah[:, k, :], act_in[:, k, :], ACT.Copy))
            with act.Fori(1, KT // 2) as i:
                for t in range(2):
                    act.wait_ge(here[t], 16 * (i + T0 // 2 + 1))
                    act.wait_ge(s.done, 2 * i + (T0 + t - 1))
                    act.activation(oh[t][:, :, :], wo[t][:, :, :], ACT.Copy).then_inc(s.hi, 1)

        @block.vector
        def _(dve):
            if layer == 0:
                dve.sem_inc(s.out, 2)
            for k in range(KT):
                split.high.next(dve)
                split.both.mark(dve.tensor_tensor(al[:, k, :], act_in[:, k, :], ah[:, k, :].bitcast(F32), ALU.subtract))
            with dve.Fori(0, KT // 2) as i:
                for t in range(2):
                    dve.wait_ge(s.done, 2 * i + T0 + t + 1)
                    for c, (o, n) in enumerate(CH):
                        r = g.resid[:, ds(2 * i + t, 1), o:o + n].rearrange("p a n -> p (a n)")
                        m = dve.tensor_tensor(r, r, g.ps[:, 3 * t + c, 0:n], ALU.add)
                    m.then_inc(s.out, 1)


def nsa_project(g, d):
    nc = g.nc
    tiles = [(t, min(P, TOK - t * P)) for t in range(9)]
    H = QK // HD
    with ExitStack() as ctx:
        sem = lambda s: ctx.enter_context(nc.semaphore("np_" + s))
        sb = lambda s, shape: ctx.enter_context(nc.sbuf_tensor("np_" + s, shape, F32))
        w = sb("w", [P, KT, NSAW])
        gain = sb("gain", [P, QK])
        sq = sb("sq", [P, QK])
        qk = [sb("qk0", [P, QK]), sb("qk1", [P, QK])]
        rn = sb("rn", [P, 2, H])
        rot = sb("rot", [P, 4, H, 8])
        w_here = [sem(f"w_here{i}") for i in range(2)]
        product, squared, summed, root, scaled = sem("product"), sem("squared"), sem("summed"), sem("root"), sem("scaled")
        freed_a, freed_v = sem("freed_a"), sem("freed_v")
        normed, turned, moved, stored = sem("normed"), sem("turned"), sem("moved"), [sem("stored0"), sem("stored1")]
        block = ctx.enter_context(nc.Block())

        @block.sync
        def _(sp):
            for i in range(2):
                sp.dma_start(w[:, 4 * i:4 * i + 4, :], d.w_nsa[:, 4 * i:4 * i + 4, :]).then_inc(w_here[i], 16)
            sp.dma_start(gain[:, :], d.qk_gain.partition_broadcast(P)).then_inc(w_here[0], 16)
            for t, R in tiles:
                sp.wait_ge(normed, t + 1)
                sp.dma_start(d.kv[t * P:t * P + R, 0:384], qk[t % 2][0:R, 512:QK]).then_inc(stored[t % 2], 16)
                sp.wait_ge(freed_v, t + 1)
                sp.dma_start(d.kv[t * P:t * P + R, 384:768], g.vtok[0:R, t, :]).then_inc(stored[t % 2], 16)
            sp.wait_ge(stored[0], 5 * 32)
            sp.wait_ge(stored[1], 4 * 32)

        @block.tensor
        def _(pe):
            def project(t, R):
                b = 3 * (t % 2)
                if t >= 2:
                    pe.wait_ge(scaled, t - 1)
                    pe.wait_ge(freed_v, t - 1)
                for k in range(KT):
                    x = g.act[:, k, t * P:t * P + R]
                    if t == 0 and k % 4 == 0:
                        pe.wait_ge(w_here[k // 4], 32 if k == 0 else 16)
                    for j, (o, n) in enumerate(((0, 512), (512, 384), (QK, 408))):
                        mm = pe.matmul(g.ps[0:R, b + j, 0:n], x, w[:, k, o:o + n], start=(k == 0), stop=(k == KT - 1))
                mm.then_inc(product, 1)

            def turn(t, R):
                pe.wait_ge(normed, t + 1)
                if t >= 1:
                    pe.wait_ge(moved, 2 * t)
                for j in range(7):
                    mm = pe.transpose(g.ps[:, 6 + j // 4, (j % 4) * P:(j % 4) * P + R], qk[t % 2][0:R, j * P:j * P + P],
                                      g.ident[0:R, 0:R])
                mm.then_inc(turned, 1)

            project(*tiles[0])
            for t, R in tiles:
                if t + 1 < 9:
                    project(*tiles[t + 1])
                turn(t, R)

        @block.scalar
        def _(act):
            def move(t, R):
                act.wait_ge(turned, t + 1)
                act.activation(g.qT[:, :, t * P:t * P + R], g.ps[:, 6, :].rearrange("p (a b) -> p a b", b=P)[:, :, 0:R], ACT.Copy)\
                   .then_inc(moved, 1)

            for t, R in tiles:
                b = 3 * (t % 2)
                act.wait_ge(product, t + 1)
                if t >= 1:
                    act.wait_ge(summed, t)
                act.activation(sq[0:R, 0:512], g.ps[0:R, b, 0:512], ACT.Square)
                act.activation(sq[0:R, 512:QK], g.ps[0:R, b + 1, 0:384], ACT.Square).then_inc(squared, 1)
                act.activation(g.vtok[0:R, t, :], g.ps[0:R, b + 2, 0:384], ACT.Copy)
                act.activation(g.gates[0:R, t, :], g.ps[0:R, b + 2, 384:408], ACT.Copy).then_inc(freed_v, 1)
                act.wait_ge(summed, t + 1)
                if t >= 1:
                    act.wait_ge(scaled, t)
                act.activation(rn[0:R, 0, :], rn[0:R, 1, :], ACT.Sqrt, bias=g.col["eps"][0:R, :], scale=1.0 / HD).then_inc(root, 1)
                if t >= 1:
                    move(t - 1, P)
            move(8, NS)
            act.drain()
            act.activation(g.gates[:, 0:8, :], g.gates[:, 0:8, :], ACT.Sigmoid)
            act.activation(g.gates[0:NS, 8, :], g.gates[0:NS, 8, :], ACT.Sigmoid)

        @block.vector
        def _(dve):
            def move(t, R):
                dve.wait_ge(turned, t + 1)
                dve.tensor_copy(g.kT[:, :, t * P:t * P + R], g.ps[:, 7, 0:384].rearrange("p (a b) -> p a b", b=P)[:, :, 0:R])\
                   .then_inc(moved, 1)

            for t, R in tiles:
                b = 3 * (t % 2)
                x = qk[t % 2]
                v = x[0:R, :].rearrange("p (h c) -> p h c", c=HD)
                dve.wait_ge(squared, t + 1)
                if t >= 1:
                    dve.wait_ge(root, t)
                dve.tensor_reduce(rn[0:R, 1, :], sq[0:R, :].rearrange("p (h c) -> p h c", c=HD), AX, ALU.add).then_inc(summed, 1)
                if t == 0:
                    dve.wait_ge(w_here[0], 32)
                if t >= 2:
                    dve.wait_ge(turned, t - 1)
                    dve.wait_ge(stored[t % 2], 32 * (t // 2))
                dve.tensor_tensor(x[0:R, 0:512], g.ps[0:R, b, 0:512], gain[0:R, 0:512], ALU.mult)
                dve.tensor_tensor(x[0:R, 512:QK], g.ps[0:R, b + 1, 0:384], gain[0:R, 512:QK], ALU.mult)
                dve.wait_ge(root, t + 1)
                dve.reciprocal(rn[0:R, 0, :], rn[0:R, 0, :])
                dve.drain()
                dve.tensor_tensor(v, v, rn[0:R, 0, :].unsqueeze(2).to_broadcast([R, H, HD]), ALU.mult).then_inc(scaled, 1)
                dve.drain()
                cos = g.rope[0:R, t, 0:8].unsqueeze(1).to_broadcast([R, H, 8])
                sin = g.rope[0:R, t, 8:16].unsqueeze(1).to_broadcast([R, H, 8])
                dve.tensor_tensor(rot[0:R, 0], v[:, :, 0:8], cos, ALU.mult)
                dve.tensor_tensor(rot[0:R, 1], v[:, :, 8:16], sin, ALU.mult)
                dve.tensor_tensor(rot[0:R, 2], v[:, :, 8:16], cos, ALU.mult)
                dve.tensor_tensor(rot[0:R, 3], v[:, :, 0:8], sin, ALU.mult)
                dve.drain()
                dve.tensor_tensor(v[:, :, 0:8], rot[0:R, 0], rot[0:R, 1], ALU.subtract)
                dve.tensor_tensor(v[:, :, 8:16], rot[0:R, 2], rot[0:R, 3], ALU.add).then_inc(normed, 1)
                dve.drain()
                if t >= 1:
                    move(t - 1, P)
            move(8, NS)


def nsa_compress(g, d):
    nc = g.nc
    with ExitStack() as ctx:
        sem = lambda s: ctx.enter_context(nc.semaphore("nc_" + s))
        sb = lambda s, shape: ctx.enter_context(nc.sbuf_tensor("nc_" + s, shape, F32))
        past = [sb(f"past{i}", [P, NB, 512]) for i in range(2)]
        rows = sb("rows", [P, 4, 4, P])
        pairs = sb("pairs", [P, 4, 512])
        w1 = sb("w1", [P, 2, 16, P])
        w2 = sb("w2", [P, 2, HD])
        pe_in = sb("pe", [P, 2, 16])
        bias = sb("bias", [P, 2])
        hid = sb("hid", [P, 2, NB + 2, NCMP])
        pt = ctx.enter_context(nc.sbuf_tensor("nc_pages", [1, NB * 8], I32))
        w_here, rows_here, pt_here = sem("w_here"), sem("rows_here"), sem("pt_here")
        past_here = [[sem(f"past_here{of}{i}") for i in range(2)] for of in range(2)]
        turned, moved, biased, bias_ready = sem("turned"), sem("moved"), sem("biased"), sem("bias_ready")
        h_done, h_out, c_done, c_out = sem("h_done"), sem("h_out"), sem("c_done"), sem("c_out")
        block = ctx.enter_context(nc.Block())

        def pages(eng, of):
            for s in range(4):
                if s >= 2:
                    eng.wait_ge(h_done, s - 1)
                for b in (2 * of, 2 * of + 1):
                    for i in range(8):
                        at = (4 * (s % 2) + b) * 8 + i
                        page = eng.value_load(pt[0:1, at:at + 1], min_val=0, max_val=79)
                        eng.dma_start(past[s % 2][:, 2 * b:2 * b + 2, i * 64:(i + 1) * 64],
                                      d.cache_cmp[ds(page, 1), :, 2 * (s // 2):2 * (s // 2) + 2, :].rearrange("a p g n -> (a p) g n"))\
                           .then_inc(past_here[of][s % 2], 16)

        @block.sync
        def _(sp):
            sp.dma_start(pt[:, :], d.pages).then_inc(pt_here, 16)
            for i in range(4):
                src = d.kv[i * 256:(i + 1) * 256, :].rearrange("(p e) c -> p e c", e=2)
                for s in range(4):
                    at = 384 * (s // 2) + 64 * (s % 2)
                    sp.dma_start(rows[:, i, s, :].rearrange("p (e c) -> p e c", e=2), src[:, :, at:at + 64]).then_inc(rows_here, 16)
            sp.dma_start(w1[:, :, :, :], d.cmp_w1).then_inc(w_here, 16)
            sp.dma_start(w2[:, :, :], d.cmp_w2).then_inc(w_here, 16)
            sp.dma_start(pe_in[:, :, :], d.cmp_pe).then_inc(w_here, 16)
            sp.wait_ge(pt_here, 16)
            pages(sp, 0)

        @block.gpsimd
        def _(pool):
            pool.wait_ge(pt_here, 16)
            pages(pool, 1)

        @block.tensor
        def _(pe):
            pe.wait_ge(w_here, 48)
            for s in range(2):
                for l in range(16):
                    mm = pe.matmul(g.ps[:, 4, s:s + 1], w1[:, s, l, :], pe_in[:, s, l:l + 1], start=(l == 0), stop=(l == 15))
            mm.then_inc(biased, 1)
            pe.wait_ge(rows_here, 16 * 16)
            for s in range(4):
                for i in range(4):
                    mm = pe.transpose(g.ps[:, s, i * P:(i + 1) * P], rows[:, i, s, :], g.ident)
                mm.then_inc(turned, 1)
            pe.wait_ge(moved, 4)

            def hidden(s):
                for of in range(2):
                    pe.wait_ge(past_here[of][s % 2], 16 * 16 * (s // 2 + 1))
                if s >= 2:
                    pe.wait_ge(h_out, s - 1)
                b = 2 * (s % 2)
                for l in range(16):
                    w = w1[:, s // 2, l, :]
                    mm = pe.matmul(g.ps[:, b, 0:504].rearrange("p (a n) -> p a n", n=NCMP), w, past[s % 2][:, :, l:l + 497:8],
                                   start=(l == 0), stop=(l == 15))
                    if s % 2 == 0:
                        mm = pe.matmul(g.ps[:, b + 1, 0:2 * NCMP].rearrange("p (a n) -> p a n", n=NCMP), w, pairs[:, s:s + 2, l:l + 497:8],
                                       start=(l == 0), stop=(l == 15))
                mm.then_inc(h_done, 1)

            def compressed(s):
                pe.wait_ge(h_out, s + 1)
                prompt = s % 2 == 0
                if s == 0:
                    pe.wait_ge(bias_ready, 1)
                if s < 2:
                    for gr in range(2):
                        q = slice(64 * gr, 64 * gr + 64)
                        mm = pe.matmul(g.ps[q, 6, 0:252].rearrange("p (a n) -> p a n", n=NCMP), w2[:, 0, :], hid[:, s % 2, gr:8:2, :], start=True, stop=True)
                        if prompt:
                            mm = pe.matmul(g.ps[q, 7, 0:NCMP], w2[:, 0, :], hid[:, s % 2, 8 + gr, :], start=True, stop=True)
                else:
                    for b in range(10 if prompt else 8):
                        mm = pe.matmul(g.ps[0:NCMP, 4 + b // 8, 64 * (b % 8):64 * (b % 8) + 64], hid[:, s % 2, b, :], w2[:, 1, :],
                                       start=True, stop=True)
                mm.then_inc(c_done, 1)

            hidden(0)
            for s in range(4):
                if s + 1 < 4:
                    hidden(s + 1)
                if s >= 1:
                    pe.wait_ge(c_out, s)
                compressed(s)

        @block.scalar
        def _(act):
            act.wait_ge(biased, 1)
            act.activation(bias[:, :], g.ps[:, 4, 0:2], ACT.Copy).then_inc(bias_ready, 1)
            act.wait_ge(bias_ready, 1)
            for s in range(4):
                act.wait_ge(h_done, s + 1)
                if s >= 2:
                    act.wait_ge(c_done, s - 1)
                b = 2 * (s % 2)
                h = hid[:, s % 2, :, :].rearrange("p a n -> p (a n)")
                a = act.activation(h[:, 0:504], g.ps[:, b, 0:504], ACT.Gelu_apprx_tanh, bias=bias[:, s // 2:s // 2 + 1])
                if s % 2 == 0:
                    a = act.activation(h[:, 504:630], g.ps[:, b + 1, 0:126], ACT.Gelu_apprx_tanh, bias=bias[:, s // 2:s // 2 + 1])
                a.then_inc(h_out, 1)

        @block.vector
        def _(dve):
            for s in range(4):
                dve.wait_ge(turned, s + 1)
                dve.tensor_copy(pairs[:, s, :], g.ps[:, s, :]).then_inc(moved, 1)
            for s in range(4):
                dve.wait_ge(c_done, s + 1)
                half = slice(4 * (s % 2), 4 * (s % 2) + 4)
                if s < 2:
                    m = dve.tensor_copy(g.kcT[:, half, :], g.ps[:, 6, 0:252].rearrange("p (a n) -> p a n", n=NCMP))
                    if s == 0:
                        m = dve.tensor_copy(g.kcT[:, 8, :], g.ps[:, 7, 0:NCMP])
                else:
                    m = dve.tensor_copy(g.vc[0:NCMP, half, :, :], g.ps[0:NCMP, 4, :].rearrange("p (a x n) -> p a x n", x=2, n=HD))
                    if s == 2:
                        m = dve.tensor_copy(g.vc[0:NCMP, 8, :, :], g.ps[0:NCMP, 5, 0:P].rearrange("p (x n) -> p x n", n=HD))
                m.then_inc(c_out, 1)


def sample_buffers(g, ctx):
    nc = g.nc
    sb = lambda s, shape, dt=F32: ctx.enter_context(nc.sbuf_tensor("ns_" + s, shape, dt))
    g.past = [sb(f"past{i}", [P, 8, 2 * P]) for i in range(2)]
    g.win = [sb(f"win{i}", [P, 4, 2 * P]) for i in range(2)]
    g.pt = sb("pages", [1, NB * 8], I32)
    g.past_here = [ctx.enter_context(nc.semaphore(f"ns_past_here{i}")) for i in range(2)]
    g.newv = sb("newv", [SS, NB, 2 * P])
    g.gate = sb("gate", [P, 4, 3])
    g.small_here, g.gates_out = (ctx.enter_context(nc.semaphore("ns_" + n)) for n in ("small_here", "gates_out"))
    g.pt_here = ctx.enter_context(nc.semaphore("ns_pt_here"))


def load_past(g, d, sp, b):
    for i in range(8):
        page = sp.value_load(g.pt[0:1, b * 8 + i:b * 8 + i + 1], min_val=0, max_val=79)
        sp.dma_start(g.past[b % 2][:, i, :], d.cache_slc[ds(page, 1), :, :].rearrange("a p n -> (a p) n")).then_inc(g.past_here[b % 2], 16)
    sp.dma_start(g.win[b % 2][:, :, :], d.cache_win[b]).then_inc(g.past_here[b % 2], 16)


def nsa_prompt(g, d):
    nc = g.nc
    items = [(t, h, part) for t in range(8) for h in range(8) for part in range(2)]

    def keys(t, part):
        return list(range(t + 1)) if part == 0 else list(range(max(0, t - 4), t + 1))

    def size(i):
        return len(keys(*items[i][::2])) + items[i][2]

    steps, rows_step = [], {}
    for i, (t, h, part) in enumerate(items):
        steps += [(i, a, min(4, size(i) - a)) for a in range(0, size(i), 4)]
        if (h == 1 and part == 0 and t >= 1) or i == len(items) - 1:
            rows_step[t - 1 if h == 1 else t] = len(steps)
            steps.append((i, size(i), 0))
    made = np.cumsum([n > 0 for _, _, n in steps]).tolist()
    finished = {e: t for t, e in rows_step.items()}.get
    past = [sum(1 for s in steps if s[0] < i) for i in range(len(items) + 1)]
    with ExitStack() as ctx:
        sem = lambda s: ctx.enter_context(nc.semaphore("na_" + s))
        sb = lambda s, shape: ctx.enter_context(nc.sbuf_tensor("na_" + s, shape, F32))
        prob = sb("prob", [P, 2, 1024])
        probT = sb("probT", [P, 2, 512])
        top = sb("top", [P, 2, 2])
        total = sb("total", [P, 4, 2])
        weight = sb("weight", [P, 2, 4])
        o = sb("o", [P, 2, 512])
        scored, maxed, expd, turned, moved = sem("scored"), sem("maxed"), sem("expd"), sem("turned"), sem("moved")
        used, mixed = sem("used"), sem("mixed")
        block = ctx.enter_context(nc.Block())

        @block.sync
        def _(sp):
            sp.dma_start(g.pt[:, :], d.pages).then_inc(g.pt_here, 16)
            sp.wait_ge(g.pt_here, 16)
            for b in range(2):
                load_past(g, d, sp, b)
            for b in range(2):
                sp.wait_ge(g.past_here[b], 9 * 16)

        @block.gpsimd
        def _(pool):
            pool.dma_start(g.newv[:, :, 0:2 * P], d.kv[NP:TOK, 512:768].rearrange("(b q) c -> q b c", q=SS)).then_inc(g.small_here, 16)
            pool.dma_start(d.gate_rows, g.gates[0:NS, 8, :]).then_inc(g.gates_out, 16)
            pool.wait_ge(g.gates_out, 16)
            for i in range(4):
                for b2 in range(2):
                    for h in range(8):
                        r0 = 64 * b2 + 8 * h
                        pool.dma_start(g.gate[r0:r0 + 8, i, :], d.gate_rows[(2 * i + b2) * 8:(2 * i + b2) * 8 + 8, 3 * h:3 * h + 3])\
                          .then_inc(g.small_here, 16)
            pool.wait_ge(g.small_here, 65 * 16)

        @block.tensor
        def _(pe):
            def scores(i):
                t, h, part = items[i]
                q0 = 64 * (h // 4)
                q = g.qT[q0:q0 + 64, h % 4, t * P:t * P + P]
                b = 2 * (i % 2)
                if i >= 2:
                    pe.wait_ge(expd, i - 1)
                ks = keys(t, part)
                kset = 1 + part
                lo, n = ks[0] * P, len(ks) * P
                masks = {len(ks) - 1: g.causal}
                if part == 1 and t >= 4:
                    masks[0] = g.window
                for a in range(0, n, 512):
                    m = min(512, n - a)
                    inside = [j for j in masks if a <= j * P < a + m]
                    mm = pe.matmul(g.ps[:, b + a // 512, 0:m], q, g.kT[q0:q0 + 64, kset, lo + a:lo + a + m],
                                   start=True, stop=not inside)
                    for j in inside:
                        mm = pe.matmul(g.ps[:, b + a // 512, j * P - a:j * P - a + P], g.ident, masks[j], start=False,
                                       stop=(j == inside[-1]))
                if part == 1:
                    out = g.ps[:, b + 1, 256:256 + NCMP]
                    pe.matmul(out, q, g.kcT[q0:q0 + 64, 8, :], start=True, stop=False, skip_group_check=True)
                    mm = pe.matmul(out, g.ident, g.cmpmask[:, t, :], start=False, stop=True, skip_group_check=True)
                mm.then_inc(scored, 1)

            def turn(e):
                i, a, n = steps[e]
                ks = keys(*items[i][::2])
                if a == 0:
                    pe.wait_ge(expd, i + 1)
                if e >= 2:
                    pe.wait_ge(moved, e - 1)
                if n == 0:
                    t = finished(e)
                    pe.wait_ge(mixed, 8 * (t + 1))
                    for j in range(4):
                        mm = pe.transpose(g.ps[:, 4 + e % 2, j * P:j * P + P], o[:, t % 2, j * P:j * P + P], g.ident)
                for j in range(a, a + n):
                    if j < len(ks):
                        mm = pe.transpose(g.ps[:, 4 + e % 2, (j - a) * P:(j - a) * P + P], prob[:, i % 2, j * P:j * P + P], g.ident)
                    else:
                        mm = pe.transpose(g.ps[0:NCMP, 4 + e % 2, (j - a) * P:(j - a) * P + P], prob[:, i % 2, 768:768 + NCMP], g.ident)
                mm.then_inc(turned, 1)

            def values(e):
                i, a, n = steps[e]
                t, h, part = items[i]
                ks = keys(t, part)
                out = g.ps[:, 6 + i // 2 % 2, :]
                col = lambda j: 64 * j
                if n == 0:
                    return
                if a == 0 and part == 0 and i >= 4:
                    pe.wait_ge(mixed, i // 2 - 1)
                pe.wait_ge(moved, e + 1)
                for j in range(a, a + n):
                    if j < len(ks):
                        v = g.vtok[:, ks[j], (1 + part) * P + 64 * (h // 4):(1 + part) * P + 64 * (h // 4) + 64]
                        mm = pe.matmul(out[:, col(part):col(part) + 64], probT[:, e % 2, (j - a) * P:(j - a) * P + P], v,
                                       start=(j == 0), stop=(j == len(ks) - 1), skip_group_check=True)
                    else:
                        mm = pe.matmul(out[:, col(2):col(2) + 64], probT[0:NCMP, e % 2, (j - a) * P:(j - a) * P + P],
                                       g.vc[0:NCMP, 8, h // 4, :], start=True, stop=True, skip_group_check=True)
                mm.then_inc(used, 1)

            scores(0)
            scores(1)
            turn(0)
            scores(2)
            for e, (i, a, n) in enumerate(steps):
                if e + 2 < len(steps):
                    turn(e + 1)
                values(e)
                if e + 1 == past[i + 1] and i + 3 < len(items):
                    scores(i + 3)
            turn(len(steps) - 1)

        @block.scalar
        def _(act):
            for i, (t, h, part) in enumerate(items):
                n = len(keys(t, part)) * P
                b = 2 * (i % 2)
                act.wait_ge(maxed, i + 1)
                if i >= 2:
                    act.wait_ge(turned, past[i - 1])
                if i >= 4:
                    act.wait_ge(mixed, i // 2 - 1)
                tot = total[:, 2 * (i // 2 % 2):2 * (i // 2 % 2) + 2, :]
                s = g.ps[:, b:b + 2, :].rearrange("p a n -> p (a n)")[:, 0:n]
                a = act.activation(prob[:, i % 2, 0:n], s, ACT.Exp, bias=top[:, i % 2, 0:1], scale=0.125, accum_out=tot[:, 0, part:part + 1])
                if part == 1:
                    a = act.activation(prob[:, 1, 768:768 + NCMP], g.ps[:, b + 1, 256:256 + NCMP], ACT.Exp, bias=top[:, i % 2, 1:2], scale=0.125,
                                       accum_out=tot[:, 1, 0:1])
                a.then_inc(expd, 1)

        @block.vector
        def _(dve):
            def maxima(i):
                t, h, part = items[i]
                n = len(keys(t, part)) * P
                b = 2 * (i % 2)
                dve.wait_ge(scored, i + 1)
                if i >= 2:
                    dve.wait_ge(expd, i - 1)
                s = g.ps[:, b:b + 2, :].rearrange("p a n -> p (a n)")[:, 0:n]
                dve.tensor_reduce(top[:, i % 2, 0:1], s, AX, ALU.max)
                if part == 1:
                    dve.tensor_reduce(top[:, i % 2, 1:2], g.ps[:, b + 1, 256:256 + NCMP], AX, ALU.max)
                dve.drain()
                dve.tensor_scalar(top[:, i % 2, 0:1 + part], top[:, i % 2, 0:1 + part], -0.125, None, ALU.mult).then_inc(maxed, 1)

            def move(e):
                i, a, n = steps[e]
                dve.wait_ge(turned, e + 1)
                if e >= 2:
                    dve.wait_ge(used, made[e - 2])
                if n == 0:
                    t = finished(e)
                    dve.tensor_copy(g.act[:, 0:4, t * P:t * P + P], g.ps[:, 4 + e % 2, :].rearrange("p (a b) -> p a b", b=P)).then_inc(moved, 1)
                    return
                whole = n - (items[i][2] == 1 and a + n == size(i))
                m = None
                if whole:
                    m = dve.tensor_copy(probT[:, e % 2, 0:whole * P], g.ps[:, 4 + e % 2, 0:whole * P])
                if whole < n:
                    m = dve.tensor_copy(probT[0:NCMP, e % 2, whole * P:n * P], g.ps[0:NCMP, 4 + e % 2, whole * P:n * P])
                m.then_inc(moved, 1)

            def mix(i):
                t, h, _ = items[i]
                u = i // 2 % 2
                dve.wait_ge(expd, i + 1)
                dve.reciprocal(weight[:, u, 0:2], total[:, 2 * u, :])
                dve.reciprocal(weight[:, u, 2:3], total[:, 2 * u + 1, 0:1])
                dve.drain()
                dve.tensor_tensor(weight[:, u, 0:2], weight[:, u, 0:2], g.gates[:, t, 3 * h + 1:3 * h + 3], ALU.mult)
                if t == 0:
                    dve.scalar_tensor_tensor(weight[:, u, 2:3], weight[:, u, 2:3], g.seen, g.gates[:, t, 3 * h:3 * h + 1], ALU.mult, ALU.mult)
                else:
                    dve.tensor_tensor(weight[:, u, 2:3], weight[:, u, 2:3], g.gates[:, t, 3 * h:3 * h + 1], ALU.mult)
                dve.wait_ge(used, made[past[i + 1] - 1])
                if h == 0 and t >= 2:
                    dve.wait_ge(turned, rows_step[t - 2] + 1)
                dve.drain()
                out = o[:, t % 2, 64 * h:64 * h + 64]
                for j in range(3):
                    s = g.ps[:, 6 + u, 64 * j:64 * j + 64]
                    if j == 0:
                        m = dve.tensor_scalar(out, s, weight[:, u, 0:1], None, ALU.mult)
                    else:
                        dve.drain()
                        m = dve.scalar_tensor_tensor(out, s, weight[:, u, j:j + 1], out, ALU.mult, ALU.add)
                m.then_inc(mixed, 1)

            maxima(0)
            maxima(1)
            for e, (i, a, n) in enumerate(steps):
                if e == len(steps) - 1:
                    mix(len(items) - 1)
                move(e)
                t, h, part = items[i]
                if a == 0 and i >= 1:
                    if i + 1 < len(items):
                        maxima(i + 1)
                    if part == 0:
                        mix(i - 1)


def nsa_sample(g, d):
    nc = g.nc
    with ExitStack() as ctx:
        sem = lambda s: ctx.enter_context(nc.semaphore("ns_" + s))
        sb = lambda s, shape: ctx.enter_context(nc.sbuf_tensor("ns_" + s, shape, F32))
        past, win, past_here = g.past, g.win, g.past_here
        newv, gate = g.newv, g.gate
        qs = sb("qs", [P, NB, 32])
        prob = sb("prob", [P, 1536 + 80])
        probT = sb("probT", [P, 15, P])
        top = sb("top", [P, 3])
        total = sb("total", [P, 3])
        weight = sb("weight", [P, 3])
        imp = sb("imp", [P, 4, NSEL])
        least = sb("least", [P, 2])
        o = sb("o", [P, HD])
        oT = sb("oT", [HD, P])
        queries = sem("queries")
        scored, maxed, cmp_exp, cmp_norm, cmp_turned, cmp_moved = (sem(s) for s in
            ("scored", "maxed", "cmp_exp", "cmp_norm", "cmp_turned", "cmp_moved"))
        imp_row, imp_moved, imp_sum, dropped, expd = (sem(s) for s in ("imp_row", "imp_moved", "imp_sum", "dropped", "expd"))
        turned, moved, summed, mixed, o_turned, o_out = (sem(s) for s in ("turned", "moved", "summed", "mixed", "o_turned", "o_out"))
        block = ctx.enter_context(nc.Block())

        @block.sync
        def _(sp):
            for b in range(2, NB):
                sp.wait_ge(summed, b // 2)
                load_past(g, d, sp, b)

        @block.tensor
        def _(pe):
            def combos(i):
                for j in range(4):
                    b, gr = 2 * i + j // 2, j % 2
                    yield j, b, gr, qs[64 * gr:64 * gr + 64, b, :]

            pe.wait_ge(queries, 1)
            for i in range(4):
                for j, b, gr, q in combos(i):
                    if gr == 0:
                        pe.wait_ge(past_here[b % 2], 9 * 16 * (i + 1))
                    if i >= 1 and j == 0:
                        pe.wait_ge(expd, i)
                    rows = slice(32 * j, 32 * j + 32)
                    f = slice(64 * gr, 64 * gr + 64)
                    new = slice(NP + 8 * b, NP + 8 * b + 8)
                    for half in range(2):
                        pe.matmul(g.ps[rows, half, :].rearrange("p (a n) -> p a n", n=P), q, past[b % 2][f, 4 * half:4 * half + 4, 0:P],
                                  start=True, stop=True)
                    pe.matmul(g.ps[rows, 2, :].rearrange("p (a n) -> p a n", n=P), q, win[b % 2][f, :, 0:P], start=True, stop=True)
                    pe.matmul(g.ps[rows, 3, 0:8], q, g.kT[f, 1, new], start=True, stop=True, skip_group_check=True)
                    pe.matmul(g.ps[rows, 3, 8:16], q, g.kT[f, 2, new], start=True, stop=True, skip_group_check=True)
                    mm = pe.matmul(g.ps[rows, 3, 16:16 + NCMP], q, g.kcT[f, b, :], start=True, stop=True, skip_group_check=True)
                mm.then_inc(scored, 1)
                pe.wait_ge(cmp_norm, i + 1)
                if i >= 1:
                    pe.wait_ge(o_out, i)
                pe.transpose(g.ps[0:NCMP, 4, 0:P], prob[:, 1536 + 16:1536 + 16 + NCMP], g.ident).then_inc(cmp_turned, 1)
                pe.wait_ge(cmp_moved, i + 1)
                pe.matmul(g.ps[:, 5, 0:NSEL], probT[0:NCMP, 14, :], g.selmap[0:NCMP, :], start=True, stop=True).then_inc(imp_row, 1)
                pe.wait_ge(imp_moved, i + 1)
                pe.matmul(g.ps[:, 5, 64:64 + NSEL], g.samerow, imp[:, 0, :], start=True, stop=True, skip_group_check=True).then_inc(imp_sum, 1)
                pe.wait_ge(expd, i + 1)
                for a in range(14):
                    if a < 12:
                        mm = pe.transpose(g.ps[:, 4 + a // 4, (a % 4) * P:(a % 4) * P + P], prob[:, a * P:a * P + P], g.ident)
                    else:
                        c = 1536 + 8 * (a - 12)
                        mm = pe.transpose(g.ps[0:8, 7, (a - 12) * P:(a - 12) * P + P], prob[:, c:c + 8], g.ident)
                    if a == 11:
                        mm.then_inc(turned, 1)
                mm.then_inc(turned, 1)
                pe.wait_ge(moved, i + 1)
                for j, b, gr, q in combos(i):
                    rows = slice(32 * j, 32 * j + 32)
                    f = slice(64 * gr, 64 * gr + 64)
                    fv = slice(P + 64 * gr, P + 64 * gr + 64)
                    for a in range(8):
                        pe.matmul(g.ps[rows, 4, 0:64], probT[:, a, rows], past[b % 2][:, a, fv], start=(a == 0), stop=False)
                    pe.matmul(g.ps[rows, 4, 0:64], probT[0:8, 12, rows], newv[:, b, f], start=False, stop=True)
                    for a in range(4):
                        pe.matmul(g.ps[rows, 5, 0:64], probT[:, 8 + a, rows], win[b % 2][:, a, fv], start=(a == 0), stop=False)
                    pe.matmul(g.ps[rows, 5, 0:64], probT[0:8, 13, rows], newv[:, b, fv], start=False, stop=True)
                    mm = pe.matmul(g.ps[rows, 6, 0:64], probT[0:NCMP, 14, rows], g.vc[0:NCMP, b, gr, :], start=True, stop=True)
                mm.then_inc(summed, 1)
                pe.wait_ge(mixed, i + 1)
                pe.transpose(g.ps[0:64, 7, 256:256 + P], o[:, :], g.ident).then_inc(o_turned, 1)

        @block.scalar
        def _(act):
            for i in range(4):
                act.wait_ge(maxed, i + 1)
                act.activation(prob[:, 1552:1552 + NCMP], g.ps[:, 3, 16:16 + NCMP], ACT.Exp, bias=top[:, 2:3], scale=0.125,
                               accum_out=total[:, 2:3]).then_inc(cmp_exp, 1)
                act.wait_ge(dropped, i + 1)
                act.activation(prob[:, 0:1024], g.ps[:, 0:2, :].rearrange("p a n -> p (a n)"), ACT.Exp, bias=top[:, 0:1], scale=0.125)
                act.activation(prob[:, 1024:1536], g.ps[:, 2, :], ACT.Exp, bias=top[:, 1:2], scale=0.125)
                act.activation(prob[:, 1536:1544], g.ps[:, 3, 0:8], ACT.Exp, bias=top[:, 0:1], scale=0.125)
                act.activation(prob[:, 1544:1552], g.ps[:, 3, 8:16], ACT.Exp, bias=top[:, 1:2], scale=0.125).then_inc(expd, 1)

        @block.vector
        def _(dve):
            part = sb("part", [P, 4])
            dve.tensor_copy(qs[:, :, :].rearrange("p b (r q) -> p b r q", q=8),
                            g.qT[:, :, NP:TOK].rearrange("p r (b q) -> p b r q", q=8)).then_inc(queries, 1)
            for i in range(4):
                dve.wait_ge(scored, i + 1)
                dve.tensor_tensor(g.ps[:, 3, 0:8], g.ps[:, 3, 0:8], g.smask, ALU.add)
                dve.tensor_tensor(g.ps[:, 3, 8:16], g.ps[:, 3, 8:16], g.smask, ALU.add)
                dve.tensor_tensor(g.ps[:, 2, 0:8], g.ps[:, 2, 0:8], g.swmask, ALU.add)
                dve.tensor_reduce(top[:, 2:3], g.ps[:, 3, 16:16 + NCMP], AX, ALU.max)
                dve.drain()
                dve.tensor_reduce(part[:, 0:1], g.ps[:, 2, :], AX, ALU.max)
                dve.tensor_reduce(part[:, 1:2], g.ps[:, 3, 8:16], AX, ALU.max)
                dve.drain()
                dve.tensor_tensor(top[:, 1:2], part[:, 0:1], part[:, 1:2], ALU.max)
                dve.drain()
                dve.tensor_scalar(top[:, 1:3], top[:, 1:3], -0.125, None, ALU.mult).then_inc(maxed, 1)
                dve.wait_ge(cmp_exp, i + 1)
                dve.reciprocal(weight[:, 2:3], total[:, 2:3])
                dve.drain()
                c = prob[:, 1552:1552 + NCMP]
                dve.tensor_scalar(c, c, weight[:, 2:3], None, ALU.mult).then_inc(cmp_norm, 1)
                dve.wait_ge(cmp_turned, i + 1)
                dve.tensor_copy(probT[0:NCMP, 14, :], g.ps[0:NCMP, 4, 0:P]).then_inc(cmp_moved, 1)
                dve.wait_ge(imp_row, i + 1)
                dve.tensor_copy(imp[:, 0, :], g.ps[:, 5, 0:NSEL]).then_inc(imp_moved, 1)
                dve.wait_ge(imp_sum, i + 1)
                dve.tensor_copy(imp[:, 1, :], g.ps[:, 5, 64:64 + NSEL])
                dve.drain()
                dve.tensor_reduce(least[:, 0:1], imp[:, 1, 1:15], AX, ALU.min)
                dve.drain()
                dve.scalar_tensor_tensor(imp[:, 2, 1:15], imp[:, 1, 1:15], least[:, 0:1], g.blkid[:, 1:15], ALU.is_equal, ALU.mult)
                dve.drain()
                dve.tensor_reduce(least[:, 1:2], imp[:, 2, 1:15], AX, ALU.max)
                dve.drain()
                dve.tensor_scalar(imp[:, 3, 0:16], g.blkid[:, 0:16], least[:, 1:2], NEG, ALU.is_equal, ALU.mult)
                dve.drain()
                s = g.ps[:, 0:2, :].rearrange("p a (m n) -> p (a m) n", n=64)
                dve.tensor_tensor(s, s, imp[:, 3, 0:16].unsqueeze(2).to_broadcast([P, 16, 64]), ALU.add)
                dve.drain()
                dve.tensor_reduce(part[:, 0:1], g.ps[:, 0:2, :].rearrange("p a n -> p (a n)"), AX, ALU.max)
                dve.tensor_reduce(part[:, 1:2], g.ps[:, 3, 0:8], AX, ALU.max)
                dve.drain()
                dve.tensor_tensor(top[:, 0:1], part[:, 0:1], part[:, 1:2], ALU.max)
                dve.drain()
                dve.tensor_scalar(top[:, 0:1], top[:, 0:1], -0.125, None, ALU.mult).then_inc(dropped, 1)
                dve.wait_ge(expd, i + 1)
                dve.tensor_reduce(part[:, 0:1], prob[:, 0:1024], AX, ALU.add)
                dve.tensor_reduce(part[:, 1:2], prob[:, 1024:1536], AX, ALU.add)
                dve.tensor_reduce(part[:, 2:4], prob[:, 1536:1552].rearrange("p (a b) -> p a b", b=8), AX, ALU.add)
                dve.drain()
                dve.tensor_tensor(total[:, 0:2], part[:, 0:2], part[:, 2:4], ALU.add)
                dve.drain()
                dve.reciprocal(weight[:, 0:2], total[:, 0:2])
                dve.wait_ge(turned, 2 * i + 1)
                dve.tensor_copy(probT[:, 0:12, :], g.ps[:, 4:7, :].rearrange("p a (b n) -> p (a b) n", n=P))
                dve.wait_ge(turned, 2 * i + 2)
                dve.tensor_copy(probT[0:8, 12:14, :], g.ps[0:8, 7, 0:256].rearrange("p (b n) -> p b n", n=P)).then_inc(moved, 1)
                dve.drain()
                dve.tensor_tensor(weight[:, 0:2], weight[:, 0:2], gate[:, i, 1:3], ALU.mult)
                dve.wait_ge(summed, i + 1)
                dve.drain()
                dve.tensor_scalar(o[:, :], g.ps[:, 4, 0:64], weight[:, 0:1], None, ALU.mult)
                dve.drain()
                dve.scalar_tensor_tensor(o[:, :], g.ps[:, 5, 0:64], weight[:, 1:2], o[:, :], ALU.mult, ALU.add)
                dve.drain()
                dve.scalar_tensor_tensor(o[:, :], g.ps[:, 6, 0:64], gate[:, i, 0:1], o[:, :], ALU.mult, ALU.add).then_inc(mixed, 1)
                dve.wait_ge(o_turned, i + 1)
                for gr in range(2):
                    for r in range(4):
                        h = 4 * gr + r
                        src = g.ps[0:64, 7, 256:256 + P].rearrange("p (b s) -> p b s", b=2)[:, :, 8 * h:8 * h + 8]
                        dst = g.act[64 * (h % 2):64 * (h % 2) + 64, h // 2, NP + 16 * i:NP + 16 * i + 16].rearrange("p (b s) -> p b s", b=2)
                        m = dve.tensor_copy(dst, src)
                m.then_inc(o_out, 1)


def nsa_layer_buffers(g, ctx):
    sb = lambda name, shape: ctx.enter_context(g.nc.sbuf_tensor(name, shape, F32))
    g.qT = sb("qT", [P, 4, TOK])
    g.kT = sb("kT", [P, KSETS, TOK])
    g.vtok = sb("vtok", [P, 9, KSETS * P])
    g.gates = sb("gates", [P, 9, 24])
    g.kcT = sb("kcT", [P, 9, NCMP])
    g.vc = sb("vc", [P, 9, 2, HD])


RWKV_GROUPS = [(0, 4), (4, 4), (8, 4), (12, 4), (16, 1)]


def rwkv_mix(g, d):
    nc = g.nc
    with ExitStack() as ctx:
        sb = lambda s, shape: ctx.enter_context(nc.sbuf_tensor("rw_" + s, shape, F32))
        two = lambda s, shape: [sb(f"{s}{i}", shape) for i in range(2)]
        b = names(
            w=[sb("w0", [P, KT, P]), sb("w1", [P, KT, P])],
            lora=sb("lora", [P, 2, TOK]),
            lw=sb("lw", [P, 2, 512]),
            shift=sb("shift", [P, RT, NB]), last=sb("last", [P, RT, 9]),
            raw=sb("raw", [P, TOK]),
            r=sb("r", [P, TOK]), k=sb("k", [P, TOK]), v=sb("v", [P, TOK]),
            ar=sb("ar", [P, 17, 2, 64]),
            bt=sb("bt", [P, TOK]), kt=sb("kt", [P, TOK]), cum=sb("cum", [P, TOK]),
            lw_=sb("logw", [P, TOK]), a=sb("a", [P, TOK]), e=sb("e", [P, TOK]), kk=sb("kkn", [P, TOK]),
            bonus=sb("bonus", [P, TOK]), y=sb("y", [P, TOK]),
            endp=sb("endp", [P, 16 + NB]),
            tok=two("tok", [P, 4, 4, 64]),
            tri=two("tri", [P, 4, 4, 64]),
            up=two("up", [P, 4, 2, 64]),
            wg=two("wg", [P, 4, 2, 64]),
            low=sb("low", [P, 4, 64]),
            u=sb("u", [P, 64]), kept=sb("kept", [P, 64]), st=sb("st", [P, 64]), st8=sb("st8", [P, NB, 64]),
            m8=sb("m8", [P, 3, NB, 64]),
        )
        s = signals(nc, ctx, "rw_", "product raw_ready mixed_in za_ready kk_squared kk_summed kk_root "
                    "log_ready a_ready decay decay_read bonus_in bonus_sum scored masked tokens powers "
                    "wg_ready wg_out u_ready u_out y_ready y_out s_ready s_out m8_s centered mean_ready sq_ready var_ready var_root gated")
        w_here = [ctx.enter_context(nc.semaphore("rw_w_here0")), ctx.enter_context(nc.semaphore("rw_w_here1"))]
        small, st_here, stored = (ctx.enter_context(nc.semaphore("rw_" + n)) for n in ("small", "st_here", "stored"))
        for j in range(4):
            rwkv_features(g, d, b, s, range(2 + 3 * j if j else 0, 5 + 3 * j), w_here, small)
            rwkv_prepare(g, d, b, s, j, st_here)
            rwkv_chunks(g, d, b, s, j, st_here, stored)
            rwkv_finish(g, d, b, s, j, stored)
        with ExitStack() as c2:
            block = c2.enter_context(nc.Block())

            @block.sync
            def _(sp):
                sp.dma_start(d.last, b.last[:, :, :]).then_inc(small, 16)
                sp.wait_ge(small, 48)


def rwkv_features(g, d, b, s, tiles, w_here, small):
    nc = g.nc
    raws = (b.raw, b.y)
    with nc.Block() as block:
        @block.sync
        def _(sp):
            if tiles[0] == 0:
                for i in range(2):
                    sp.dma_start(b.w[i][:, :, :], d.w_rwkv[i]).then_inc(w_here[i], 16)
                sp.dma_start(b.lw[:, :, :].rearrange("p a n -> p (a n)"), d.lora).then_inc(small, 16)
                sp.dma_start(b.shift[:, :, :], d.shift).then_inc(small, 16)
            for i in tiles:
                s.product.next(sp)
                if i + 2 < RT:
                    sp.dma_start(b.w[i % 2][:, :, :], d.w_rwkv[i + 2]).then_inc(w_here[i % 2], 16)

        @block.tensor
        def _(pe):
            for x, i in enumerate(tiles):
                pe.wait_ge(w_here[i % 2], 16 * (i // 2 + 1))
                if x >= 2:
                    s.raw_ready.next(pe)
                for k in range(KT):
                    for c, (o, n) in enumerate(CH):
                        mm = pe.matmul(g.ps[:, 3 * (x % 2) + c, 0:n], b.w[i % 2][:, k, :], g.act[:, k, o:o + n], start=(k == 0), stop=(k == KT - 1))
                s.product.mark(mm)
            s.raw_ready.next(pe, 2)

        @block.scalar
        def _(act):
            seen = 0
            for x, i in enumerate(tiles):
                s.product.next(act)
                if x >= 2 and seen < x - 1:
                    s.mixed_in.next(act, x - 1 - seen)
                    seen = x - 1
                for c, (o, n) in enumerate(CH):
                    a = act.activation(raws[x % 2][:, o:o + n], g.ps[:, 3 * (x % 2) + c, 0:n], ACT.Copy)
                s.raw_ready.mark(a)
                if i < 2:
                    s.mixed_in.next(act)
                    seen = x + 1
                    if i == 0:
                        act.activation(b.lora[0:64, 0, :], b.lora[0:64, 0, :], ACT.Tanh)
                    else:
                        act.activation(b.lora[:, 1, :], b.lora[:, 1, :], ACT.Sigmoid)
            s.mixed_in.next(act, len(tiles) - seen)

        @block.vector
        def _(dve):
            for n, i in enumerate(tiles):
                out = b.lora[:, i, :] if i < 2 else (b.r, b.k, b.v)[(i - 2) % 3][:, :]
                t = (b.cum, b.e)[n % 2]
                x = raws[n % 2]
                s.raw_ready.next(dve)
                if i == 0:
                    dve.wait_ge(small, 32)
                x8 = x[:, NP:TOK].rearrange("p (b q) -> p b q", q=SS)
                t8 = t[:, NP:TOK].rearrange("p (b q) -> p b q", q=SS)
                dve.tensor_tensor(t[:, 1:NP], x[:, 0:NP - 1], x[:, 1:NP], ALU.subtract)
                dve.tensor_scalar(t[:, 0:1], x[:, 0:1], -1.0, None, ALU.mult)
                dve.tensor_tensor(t8[:, :, 1:8], x8[:, :, 0:7], x8[:, :, 1:8], ALU.subtract)
                dve.tensor_tensor(t8[:, :, 0:1], b.shift[:, i, :].unsqueeze(2), x8[:, :, 0:1], ALU.subtract)
                dve.tensor_copy(b.last[:, i, 0:8].unsqueeze(2), x8[:, :, 7:8])
                dve.tensor_copy(b.last[:, i, 8:9], x[:, NP - 1:NP])
                dve.drain()
                s.mixed_in.mark(dve.scalar_tensor_tensor(out, t[:, :], g.col["mu"][:, i:i + 1], x[:, :], ALU.mult, ALU.add))


def rwkv_prepare(g, d, b, s, j, st_here):
    nc = g.nc
    col = lambda name: g.col[name][:, j:j + 1]
    pj = slice(P * j, P * j + P)
    ps3 = lambda first: [(g.ps[:, first + c, 0:n], o, n) for c, (o, n) in enumerate(CH)]
    with nc.Block() as block:
        @block.sync
        def _(sp):
            sp.dma_start(b.st8[:, :, :], d.srwkv[j]).then_inc(st_here, 16)

        @block.tensor
        def _(pe):
            for p, o, n in ps3(0):
                pe.matmul(p, b.lw[0:64, 0, pj], b.lora[0:64, 0, o:o + n], start=True, stop=True)
            for p, o, n in ps3(3):
                mm = pe.matmul(p, b.lw[64:P, 0, pj], b.lora[64:P, 0, o:o + n], start=True, stop=True)
            s.za_ready.mark(mm)
            s.kk_squared.next(pe)
            s.a_ready.next(pe)
            for p, o, n in ps3(0):
                mm = pe.matmul(p, g.blk, b.e[:, o:o + n], start=True, stop=True)
            s.kk_summed.mark(mm)
            s.bonus_in.next(pe)
            for p, o, n in ps3(3):
                mm = pe.matmul(p, g.blk, b.y[:, o:o + n], start=True, stop=True)
            s.bonus_sum.mark(mm)

        @block.scalar
        def _(act):
            s.za_ready.next(act)
            for p, o, n in ps3(0):
                a = act.activation(b.lw_[:, o:o + n], p, ACT.Sigmoid, bias=col("w0"))
            s.log_ready.mark(a)
            for p, o, n in ps3(3):
                a = act.activation(b.a[:, o:o + n], p, ACT.Sigmoid, bias=col("a0"))
            s.a_ready.mark(a)
            s.kk_root.next(act)
            s.sq_ready.mark(act.activation(b.e[:, :], b.e[:, :], ACT.Sqrt))
            s.decay_read.next(act)
            s.decay.mark(act.activation(b.e[:, :], b.e[:, :], ACT.Exp))
            s.decay_read.next(act)
            s.decay.mark(act.activation(b.e[:, :], b.cum[:, :], ACT.Exp, scale=-1.0))
            s.decay_read.next(act)
            s.decay.mark(act.activation(b.e[:, :], b.cum[:, :], ACT.Exp))

        @block.vector
        def _(dve):
            ar = lambda which: (b.ar[:, :, which, :])
            chunked = lambda x: x.rearrange("p (c t) -> p c t", t=64)
            dve.tensor_scalar(b.kk[:, :], b.k[:, :], col("kk"), None, ALU.mult)
            dve.drain()
            s.log_ready.next(dve)
            s.kk_squared.mark(dve.tensor_tensor(b.e[:, :], b.kk[:, :], b.kk[:, :], ALU.mult))
            dve.tensor_scalar(b.lw_[:, :], b.lw_[:, :], -float(np.exp(-0.5)), None, ALU.mult)
            dve.drain()
            dve.tensor_tensor_scan(b.cum[:, :], g.scan, b.lw_[:, :], 0.0, ALU.mult, ALU.add)
            s.kk_summed.next(dve)
            for p, o, n in ps3(0):
                m = dve.tensor_scalar(b.e[:, o:o + n], p, 1e-24, None, ALU.max)
            s.kk_root.mark(m)
            dve.tensor_scalar(b.raw[:, :], b.a[:, :], 1.0, col("ka"), ALU.subtract, ALU.mult)
            dve.drain()
            dve.scalar_tensor_tensor(b.k[:, :], b.raw[:, :], 1.0, b.k[:, :], ALU.add, ALU.mult)
            dve.drain()
            s.bonus_in.mark(dve.scalar_tensor_tensor(b.y[:, :], b.k[:, :], col("rk"), b.r[:, :], ALU.mult, ALU.mult))
            s.sq_ready.next(dve)
            dve.reciprocal(b.e[:, :], b.e[:, :])
            dve.drain()
            dve.tensor_tensor(b.kk[:, :], b.kk[:, :], b.e[:, :], ALU.mult)
            dve.drain()
            s.decay_read.mark(dve.tensor_tensor(b.e[:, :], b.cum[:, :], b.lw_[:, :], ALU.subtract))
            s.bonus_sum.next(dve)
            for p, o, n in ps3(3):
                dve.tensor_tensor(b.bonus[:, o:o + n], p, b.v[:, o:o + n], ALU.mult)
            s.decay.next(dve)
            s.decay_read.mark(dve.scalar_tensor_tensor(ar(0), chunked(b.kk[:, :]), -1.0, chunked(b.e[:, :]), ALU.mult, ALU.mult))
            dve.tensor_tensor(b.kk[:, :], b.kk[:, :], b.a[:, :], ALU.mult)
            s.decay.next(dve)
            dve.drain()
            dve.tensor_tensor(b.bt[:, :], b.kk[:, :], b.e[:, :], ALU.mult)
            s.decay_read.mark(dve.tensor_tensor(b.kt[:, :], b.k[:, :], b.e[:, :], ALU.mult))
            s.decay.next(dve)
            dve.tensor_tensor(ar(1), chunked(b.r[:, :]), chunked(b.e[:, :]), ALU.mult)
            dve.tensor_copy(b.endp[:, 0:16].unsqueeze(2), chunked(b.e[:, 0:NP])[:, :, 63:64])
            dve.tensor_copy(b.endp[:, 16:24].unsqueeze(2), b.e[:, NP:TOK].rearrange("p (b q) -> p b q", q=SS)[:, :, 7:8])


def rwkv_chunks(g, d, b, s, j, st_here, stored):
    nc = g.nc
    halves = [slice(0, 64), slice(64, P)]
    GR = len(RWKV_GROUPS)
    with nc.Block() as block:
        @block.tensor
        def _(pe):
            def scores(i):
                c0, n = RWKV_GROUPS[i]
                for c in range(n):
                    t = slice(64 * (c0 + c), 64 * (c0 + c) + 64)
                    for h in halves:
                        at, art = b.ar[h, c0 + c, 0, :], b.ar[h, c0 + c, :, :].rearrange("p a t -> p (a t)")
                        tri = g.ps[h, c // 2, 256 * (c % 2):256 * (c % 2) + 256]
                        pe.matmul(tri[:, 0:P], b.bt[h, t], art, start=True, stop=True)
                        pe.matmul(tri[:, P:2 * P], b.kt[h, t], art, start=True, stop=True)
                        pe.matmul(g.ps[h, 2, 64 * c:64 * c + 64], at, b.bt[h, t], start=True, stop=True)
                        for x, src in enumerate((at, b.bt[h, t], b.kt[h, t], b.v[h, t])):
                            o = 256 * (c % 2) + 64 * x
                            mm = pe.matmul(g.ps[h, 3 + c // 2, o:o + 64], src, g.id2[h, :], start=True, stop=True)
                s.scored.mark(mm)

            def inverse(i, level):
                n = RWKV_GROUPS[i][1]
                up_, tok, tri = b.up[i % 2], b.tok[i % 2], b.tri[i % 2]
                if level > 6:
                    return
                s.masked.next(pe)
                if level == 6:
                    s.tokens.next(pe)
                for c in range(n):
                    for h in halves:
                        if level == 6:
                            pe.matmul(g.ps[h, 5, P * c:P * c + 64], tok[h, c, 0, :], up_[h, c, 1, :], start=True, stop=True)
                            mm = pe.matmul(g.ps[h, 5, P * c + 64:P * c + P], tri[h, c, 2, :], tok[h, c, 3, :], start=True, stop=True)
                            continue
                        x0, x1 = (0, 1) if level == 0 else (1, 2) if level == 5 else (0, 2)
                        low, up = b.low[h, c, :], up_[h, c, x0:x1, :].rearrange("p a t -> p (a t)")
                        mm = pe.matmul(g.ps[h, 5, P * c + 64 * x0:P * c + 64 * x1], low, up, start=True, stop=True)
                        if level < 5:
                            mm = pe.matmul(g.ps[h, 6, 64 * c:64 * c + 64], up_[h, c, 0, :], low, start=True, stop=True)
                (s.wg_ready if level == 6 else s.powers).mark(mm)

            def through(i, c):
                sampled = i == GR - 1
                if c == 0:
                    s.wg_out.next(pe)
                else:
                    s.s_out.next(pe)
                for h in halves:
                    pu = g.ps[h, 7, 0:64]
                    pe.matmul(pu, b.up[i % 2][h, c, 1, :], b.wg[i % 2][h, c, 1, :], start=True, stop=False)
                    if sampled:
                        for q in range(NB):
                            mm = pe.matmul(pu, b.m8[h, 0, q, :], b.st8[h, q, :], start=False, stop=(q == NB - 1))
                    else:
                        mm = pe.matmul(pu, b.wg[i % 2][h, c, 0, :], b.st[h, :], start=False, stop=True)
                s.u_ready.mark(mm)

            def update(i, c):
                c0, n = RWKV_GROUPS[i]
                sampled = i == GR - 1
                tok, tri = b.tok[i % 2], b.tri[i % 2]
                s.u_out.next(pe)
                for h in halves:
                    if sampled:
                        for q in range(NB):
                            ps = g.ps[h, 2, 64 * q:64 * q + 64]
                            pe.matmul(ps, b.m8[h, 2, q, :], b.u[h, :], start=True, stop=False)
                            pe.matmul(ps, b.m8[h, 1, q, :], tok[h, c, 3, :], start=False, stop=False)
                            mm = pe.matmul(ps, g.id2[h, :], b.st8[h, q, :], start=False, stop=True)
                    else:
                        ps = g.ps[h, 7, 64:P]
                        pe.matmul(ps, tok[h, c, 1, :], b.u[h, :], start=True, stop=False)
                        mm = pe.matmul(ps, tok[h, c, 2, :], tok[h, c, 3, :], start=False, stop=True)
                s.s_ready.mark(mm)
                if sampled:
                    s.m8_s.next(pe)
                for h in halves:
                    py = g.ps[h, 7, 256 + 64 * c:256 + 64 * c + 64]
                    pe.matmul(py, b.u[h, :], tri[h, c, 1, :], start=True, stop=False)
                    pe.matmul(py, tok[h, c, 3, :], tri[h, c, 3, :], start=False, stop=False)
                    if sampled:
                        for q in range(NB):
                            mm = pe.matmul(py, b.st8[h, q, :], b.m8[h, 1, q, :], start=False, stop=(q == NB - 1))
                    else:
                        mm = pe.matmul(py, b.st[h, :], b.ar[h, c0 + c, 1, :], start=False, stop=True)
                s.y_ready.mark(mm)

            scores(0)
            for level in range(7):
                inverse(0, level)
            for i, (c0, n) in enumerate(RWKV_GROUPS):
                if i + 1 < GR:
                    scores(i + 1)
                for c in range(n):
                    through(i, c)
                    if i + 1 < GR:
                        inverse(i + 1, 2 * c)
                    update(i, c)
                    if i + 1 < GR:
                        inverse(i + 1, 2 * c + 1)
                s.s_out.next(pe)
                s.y_out.next(pe)

        @block.scalar
        def _(act):
            def tokens(i):
                n = RWKV_GROUPS[i][1]
                s.scored.next(act)
                for q in range(0, n, 2):
                    m = min(2, n - q)
                    a = act.activation(b.tok[i % 2][:, q:q + m, :, :].rearrange("p a x t -> p (a x t)"), g.ps[:, 3 + q // 2, 0:256 * m], ACT.Copy)
                s.tokens.mark(a)

            tokens(0)
            for i, (c0, n) in enumerate(RWKV_GROUPS):
                if i + 1 < GR:
                    tokens(i + 1)
                s.s_out.next(act, n)
                s.y_out.mark(act.activation(b.y[:, 64 * c0:64 * (c0 + n)], g.ps[:, 7, 256:256 + 64 * n], ACT.Copy))

        @block.vector
        def _(dve):
            def masks(i):
                n = RWKV_GROUPS[i][1]
                above, upto, below = (g.above8, g.upto8, g.below8) if i == GR - 1 else (g.above, g.upto, g.below)
                over = lambda m: m.unsqueeze(1).to_broadcast([P, n, 64])
                to, up_ = b.tri[i % 2], b.up[i % 2]
                s.scored.next(dve)
                tri = g.ps[:, 0:2, :].rearrange("p a (c x t) -> p (a c) x t", x=4, t=64)[:, 0:n]
                dve.tensor_tensor(up_[:, 0:n, 0, :], tri[:, :, 0, :], over(above), ALU.mult)
                dve.drain()
                dve.tensor_tensor(up_[:, 0:n, 1, :], up_[:, 0:n, 0, :], over(g.id2), ALU.add)
                dve.tensor_tensor(b.low[:, 0:n, :], g.ps[:, 2, 0:64 * n].rearrange("p (c t) -> p c t", t=64), over(below), ALU.mult)
                for x, m in ((1, upto), (2, above), (3, upto)):
                    last = dve.tensor_tensor(to[:, 0:n, x, :], tri[:, :, x, :], over(m), ALU.mult)
                s.masked.mark(last)

            def inverse(i, level):
                n = RWKV_GROUPS[i][1]
                up_, tok, wg = b.up[i % 2], b.tok[i % 2], b.wg[i % 2]
                if level > 6:
                    return
                if level < 6:
                    s.powers.next(dve)
                    up = g.ps[:, 5, 0:P * n].rearrange("p (c x t) -> p c x t", x=2, t=64)
                    if level > 0:
                        m = dve.tensor_tensor(up_[:, 0:n, 1, :], up_[:, 0:n, 1, :], up[:, :, 1, :], ALU.add)
                    if level < 5:
                        dve.tensor_copy(up_[:, 0:n, 0, :], up[:, :, 0, :])
                        m = dve.tensor_copy(b.low[:, 0:n, :], g.ps[:, 6, 0:64 * n].rearrange("p (c t) -> p c t", t=64))
                    s.masked.mark(m)
                    return
                s.wg_ready.next(dve)
                m = dve.tensor_copy(wg[:, 0:n, :, :].rearrange("p c x t -> p (c x t)"), g.ps[:, 5, 0:P * n])
                if i == GR - 1:
                    dve.drain()
                    eight = lambda x: x.unsqueeze(1).to_broadcast([P, NB, 64])
                    rows = g.brow.unsqueeze(2).to_broadcast([P, NB, 64])
                    dve.tensor_tensor(b.m8[:, 0, :, :], eight(wg[:, 0, 0, :]), g.bcol, ALU.mult)
                    dve.tensor_tensor(b.m8[:, 1, :, :], eight(tok[:, 0, 2, :]), rows, ALU.mult)
                    m = dve.tensor_tensor(b.m8[:, 2, :, :], eight(tok[:, 0, 1, :]), rows, ALU.mult)
                s.wg_out.mark(m)

            def through(i, c):
                s.u_ready.next(dve)
                s.u_out.mark(dve.tensor_copy(b.u[:, :], g.ps[:, 7, 0:64]))
                if i < GR - 1:
                    at = RWKV_GROUPS[i][0] + c
                    dve.tensor_scalar(b.kept[:, :], b.st[:, :], b.endp[:, at:at + 1], None, ALU.mult)

            def update(i, c):
                c0 = RWKV_GROUPS[i][0]
                s.s_ready.next(dve)
                if i == GR - 1:
                    s.m8_s.mark(dve.tensor_tensor(b.m8[:, 1, :, :], b.ar[:, 16, 1, :].unsqueeze(1).to_broadcast([P, NB, 64]), g.bcol, ALU.mult))
                    s.y_ready.next(dve)
                    m = dve.tensor_tensor(b.st8[:, :, :], g.ps[:, 2, :].rearrange("p (q t) -> p q t", t=64),
                                          b.endp[:, 16:24].unsqueeze(2).to_broadcast([P, NB, 64]), ALU.mult)
                else:
                    s.y_ready.next(dve)
                    dve.drain()
                    m = dve.scalar_tensor_tensor(b.st[:, :], g.ps[:, 7, 64:P], b.endp[:, c0 + c:c0 + c + 1], b.kept[:, :], ALU.mult, ALU.add)
                s.s_out.mark(m)
                dve.drain()

            dve.memset(b.st[:, :], 0.0)
            dve.wait_ge(st_here, 16 * (j + 1))
            masks(0)
            for level in range(7):
                inverse(0, level)
            for i, (c0, n) in enumerate(RWKV_GROUPS):
                if i + 1 < GR:
                    masks(i + 1)
                for c in range(n):
                    through(i, c)
                    if i + 1 < GR:
                        inverse(i + 1, 2 * c)
                    update(i, c)
                    if i + 1 < GR:
                        inverse(i + 1, 2 * c + 1)

        @block.sync
        def _(sp):
            s.s_out.next(sp, 17)
            sp.dma_start(d.rw_p[j], b.st[:, :]).then_inc(stored, 16)
            sp.dma_start(d.rw_s[j], b.st8[:, :, :]).then_inc(stored, 16)
            sp.wait_ge(stored, 48 * j + 32)


def rwkv_finish(g, d, b, s, j, stored):
    nc = g.nc
    col = lambda name: g.col[name][:, j:j + 1]
    ps3 = lambda first: [(g.ps[:, first + c, 0:n], o, n) for c, (o, n) in enumerate(CH)]
    with nc.Block() as block:
        @block.tensor
        def _(pe):
            for p, o, n in ps3(0):
                mm = pe.matmul(p, g.blk, b.y[:, o:o + n], start=True, stop=True)
            s.mean_ready.mark(mm)
            for p, o, n in ps3(3):
                mm = pe.matmul(p, b.lw[:, 1, P * j:P * j + P], b.lora[:, 1, o:o + n], start=True, stop=True)
            s.centered.next(pe)
            for p, o, n in ps3(0):
                mm = pe.matmul(p, g.blk, b.e[:, o:o + n], start=True, stop=True)
            s.var_ready.mark(mm)

        @block.scalar
        def _(act):
            s.var_ready.next(act)
            for p, o, n in ps3(0):
                a = act.activation(b.cum[:, o:o + n], p, ACT.Sqrt, bias=g.col["gneps"], scale=1.0 / HD)
            s.var_root.mark(a)

        @block.vector
        def _(dve):
            s.mean_ready.next(dve)
            for p, o, n in ps3(0):
                dve.scalar_tensor_tensor(b.y[:, o:o + n], p, -1.0 / HD, b.y[:, o:o + n], ALU.mult, ALU.add)
            dve.drain()
            s.centered.mark(dve.tensor_tensor(b.e[:, :], b.y[:, :], b.y[:, :], ALU.mult))
            s.var_root.next(dve)
            dve.reciprocal(b.cum[:, :], b.cum[:, :])
            dve.drain()
            dve.tensor_tensor(b.y[:, :], b.y[:, :], b.cum[:, :], ALU.mult)
            dve.drain()
            dve.tensor_scalar(b.y[:, :], b.y[:, :], col("lnw"), col("lnb"), ALU.mult, ALU.add)
            dve.drain()
            dve.tensor_tensor(b.y[:, :], b.y[:, :], b.bonus[:, :], ALU.add)
            dve.drain()
            for p, o, n in ps3(3):
                m = dve.tensor_tensor(b.y[:, o:o + n], b.y[:, o:o + n], p, ALU.mult)
            s.gated.mark(m)

        @block.sync
        def _(sp):
            s.gated.next(sp)
            sp.dma_start(d.rwkv_out[:, j, :], b.y[:, :]).then_inc(stored, 16)
            sp.wait_ge(stored, 48 * (j + 1))


def gla_mix(g, d):
    nc = g.nc
    with ExitStack() as ctx:
        sb = lambda s, shape: ctx.enter_context(nc.sbuf_tensor("gl_" + s, shape, F32))
        b = names(
            wq=sb("wq", [P, KT, P]), wk=sb("wk", [P, KT, P]), wv=sb("wv", [P, KT, 256]), wgd=sb("wgd", [P, KT, 16]),
            up=sb("up", [16, 512]), gd=sb("gd", [16, TOK]),
            q=sb("q", [P, TOK]), k=sb("k", [P, TOK]), v=sb("v", [P, 9, 256]), cum=sb("cum", [P, TOK]), e=sb("e", [P, TOK]),
            qs=sb("qs", [P, TOK]), ks=sb("ks", [P, TOK]), qe=sb("qe", [P, TOK]), kd=sb("kd", [P, TOK]),
            ref=sb("ref", [P, 2, 24]), dec=sb("dec", [P, 24]),
            at=sb("at", [P, 2, 64]), kt=sb("kt", [P, 2, P]), kt8=sb("kt8", [NS, NB, P]),
            st=sb("st", [P, 4, 256]), st8=sb("st8", [P, NB, 256]), o=sb("o", [P, 2, TOK]),
            gate=sb("gate", [P, 2, TOK]))
        s = signals(nc, ctx, "gl_", "gd_ready gd_out product q_out v_ready v_out logit x_ready soft cum_ready exp_ready exp_read scored turned_out "
                    "outer state o_ready o_out squared mean_ready root r_ready gated")
        here, v_here, st_here, stored = (ctx.enter_context(nc.semaphore("gl_" + n)) for n in ("here", "v_here", "st_here", "stored"))
        with nc.Block() as block:
            @block.sync
            def _(sp):
                sp.dma_start(b.wgd[:, :, :], d.w_gla_gd).then_inc(here, 16)
                sp.dma_start(b.up[:, :], d.gate_up).then_inc(here, 16)

            @block.tensor
            def _(pe):
                pe.wait_ge(here, 32)
                for k in range(KT):
                    for c, (o, n) in enumerate(CH):
                        mm = pe.matmul(g.ps[0:16, c, 0:n], b.wgd[:, k, :], g.act[:, k, o:o + n], start=(k == 0), stop=(k == KT - 1))
                s.gd_ready.mark(mm)

            @block.scalar
            def _(act):
                s.gd_ready.next(act)
                for c, (o, n) in enumerate(CH):
                    act.activation(b.gd[:, o:o + n], g.ps[0:16, c, 0:n], ACT.Copy)
        for h in range(4):
            gla_project(g, d, b, s, h, here, v_here, st_here)
            gla_chunks(g, d, b, s, h, stored)
            gla_finish(g, d, b, s, h, stored)


def gla_project(g, d, b, s, h, here, v_here, st_here):
    nc = g.nc
    ps3 = lambda first: [(g.ps[:, first + c, 0:n], o, n) for c, (o, n) in enumerate(CH)]
    with nc.Block() as block:
        @block.sync
        def _(sp):
            sp.dma_start(b.wk[:, :, :], d.w_gla_qk[4 + h]).then_inc(here, 16)
            sp.dma_start(b.wq[:, :, :], d.w_gla_qk[h]).then_inc(here, 16)
            sp.dma_start(b.wv[:, :, :], d.w_gla_v[h]).then_inc(v_here, 16)
            sp.dma_start(b.st8[:, :, :], d.sgla[h]).then_inc(st_here, 16)
            for x, w in enumerate((b.wk, b.wq)):
                s.product.next(sp)
                sp.dma_start(w[:, :, :], d.w_gla_r[2 * h + x]).then_inc(here, 16)
            sp.wait_ge(st_here, 16 * (h + 1))

        @block.tensor
        def _(pe):
            for p, o, n in ps3(0):
                mm = pe.matmul(p, b.up[:, h * P:h * P + P], b.gd[:, o:o + n], start=True, stop=True)
            s.logit.mark(mm)
            pe.wait_ge(here, 32 + 64 * h + 32)
            for w, first in ((b.wk, 3), (b.wq, 0)):
                if first == 0:
                    s.x_ready.next(pe)
                for k in range(KT):
                    for p, o, n in ps3(first):
                        mm = pe.matmul(p, w[:, k, :], g.act[:, k, o:o + n], start=(k == 0), stop=(k == KT - 1))
                s.product.mark(mm)
            pe.wait_ge(v_here, 16 * (h + 1))
            for t in range(9):
                R = P if t < 8 else NS
                if t >= 2:
                    s.v_out.next(pe)
                for k in range(KT):
                    mm = pe.matmul(g.ps[0:R, 6 + t % 2, 0:256], g.act[:, k, t * P:t * P + R], b.wv[:, k, :], start=(k == 0), stop=(k == KT - 1))
                s.v_ready.mark(mm)
            s.v_out.next(pe, 2)
            s.q_out.next(pe)
            pe.wait_ge(here, 32 + 64 * h + 64)
            for x, w in enumerate((b.wk, b.wq)):
                for k in range(KT):
                    for p, o, n in ps3(3 * x):
                        mm = pe.matmul(p, w[:, k, :], g.act[:, k, o:o + n], start=(k == 0), stop=(k == KT - 1))
                s.r_ready.mark(mm)

        @block.scalar
        def _(act):
            s.x_ready.next(act)
            act.activation(b.e[:, :], b.cum[:, :], ACT.Abs)
            act.drain()
            act.activation(b.e[:, :], b.e[:, :], ACT.Exp, scale=-1.0)
            act.drain()
            s.soft.mark(act.activation(b.e[:, :], b.e[:, :], ACT.Ln, bias=g.ones[:, 0:1]))
            for x in (b.k, b.q):
                s.product.next(act)
                for p, o, n in ps3(3 if x is b.k else 0):
                    a = act.activation(x[:, o:o + n], p, ACT.Copy, scale=1.0 if x is b.k else float(P) ** -0.5)
            s.q_out.mark(a)
            for t in range(9):
                R = P if t < 8 else NS
                s.v_ready.next(act)
                s.v_out.mark(act.activation(b.v[0:R, t, :], g.ps[0:R, 6 + t % 2, 0:256], ACT.Copy))
            for i in range(4):
                s.cum_ready.next(act)
                s.exp_ready.mark(act.activation(b.e[:, :], b.e[:, :], ACT.Exp))
            act.activation(b.dec[:, :], b.ref[:, 1, :], ACT.Exp)
            for x in range(2):
                s.r_ready.next(act)
                for p, o, n in ps3(3 * x):
                    act.activation(b.gate[:, x, o:o + n], p, ACT.Silu)

        @block.vector
        def _(dve):
            s.logit.next(dve)
            for p, o, n in ps3(0):
                m = dve.tensor_scalar(b.cum[:, o:o + n], p, g.col["gb"][:, h:h + 1], None, ALU.add)
            s.x_ready.mark(m)
            dve.drain()
            dve.tensor_scalar(b.kd[:, :], b.cum[:, :], 0.0, None, ALU.min)
            s.soft.next(dve)
            dve.drain()
            dve.tensor_tensor(b.kd[:, :], b.kd[:, :], b.e[:, :], ALU.subtract)
            dve.drain()
            dve.tensor_scalar(b.kd[:, :], b.kd[:, :], 1.0 / 16.0, None, ALU.mult)
            dve.drain()
            dve.tensor_tensor_scan(b.cum[:, :], g.scan, b.kd[:, :], 0.0, ALU.mult, ALU.add)
            dve.drain()
            cp, cs = b.cum[:, 0:NP].rearrange("p (c t) -> p c t", t=64), b.cum[:, NP:TOK].rearrange("p (c t) -> p c t", t=8)
            for i, (a, z) in enumerate(((31, 3), (63, 7))):
                dve.tensor_copy(b.ref[:, i, 0:16].unsqueeze(2), cp[:, :, a:a + 1])
                m = dve.tensor_copy(b.ref[:, i, 16:24].unsqueeze(2), cs[:, :, z:z + 1])
            dve.drain()
            s.q_out.next(dve)

            def exponent(i, sign):
                e = b.e
                if i is None:
                    return dve.tensor_copy(e[:, :], b.cum[:, :])
                r = b.ref[:, i, :]
                for lo, hi, size, ra in ((0, NP, 64, r[:, 0:16]), (NP, TOK, 8, r[:, 16:24])):
                    x = b.cum[:, lo:hi].rearrange("p (c t) -> p c t", t=size)
                    y = e[:, lo:hi].rearrange("p (c t) -> p c t", t=size)
                    ra = ra.unsqueeze(2).to_broadcast([P, (hi - lo) // size, size])
                    m = dve.tensor_tensor(y, x, ra, ALU.subtract) if sign > 0 else dve.tensor_tensor(y, ra, x, ALU.subtract)
                return m

            for i, sign, src, dst in ((0, 1, b.q, b.qs), (0, -1, b.k, b.ks), (None, 1, b.q, b.qe), (1, -1, b.k, b.kd)):
                s.cum_ready.mark(exponent(i, sign))
                s.exp_ready.next(dve)
                dve.tensor_tensor(dst[:, :], src[:, :], b.e[:, :], ALU.mult)
                dve.drain()


def gla_chunks(g, d, b, s, h, stored):
    nc = g.nc
    with nc.Block() as block:
        @block.tensor
        def _(pe):
            def first(t):
                R = P if t < 8 else NS
                for c in range(2 if t < 8 else 1):
                    x = slice(t * P + 64 * c, t * P + 64 * c + 64)
                    pe.matmul(g.ps[64 * c:64 * c + 64, 6 + t % 2, 0:64], b.ks[:, x], b.qs[:, x], start=True, stop=True)
                s.scored.mark(pe.transpose(g.ps[0:R, 6 + t % 2, P:2 * P], b.kd[:, t * P:t * P + R], g.ident))

            first(0)
            for t in range(9):
                s.turned_out.next(pe)
                if t + 1 < 9:
                    first(t + 1)
                if t < 8:
                    if t >= 1:
                        s.state.next(pe)
                    for c in range(2):
                        hr = slice(64 * c, 64 * c + 64)
                        mm = pe.matmul(g.ps[:, c, 0:256], b.kt[hr, t % 2, :], b.v[hr, t, :], start=True, stop=True)
                    s.outer.mark(mm)
                    if t >= 2:
                        s.o_out.next(pe)
                    for c in range(2):
                        hr = slice(64 * c, 64 * c + 64)
                        if c == 1:
                            s.state.next(pe)
                        for x in range(2):
                            p = g.ps[:, 2 + 2 * (t % 2) + c, 64 * x:64 * x + 64]
                            pe.matmul(p, b.v[hr, t, P * x:P * x + P], b.at[hr, t % 2, :], start=True, stop=False)
                            mm = pe.matmul(p, b.st[:, (2 * t + c) % 4, P * x:P * x + P], b.qe[:, t * P + 64 * c:t * P + 64 * c + 64], start=False, stop=True)
                    s.o_ready.mark(mm)
                else:
                    s.o_out.next(pe, 2)
                    s.state.next(pe)
                    for x in range(2):
                        p = g.ps[:, 4, P * x:P * x + 64]
                        pe.matmul(p, b.v[0:NS, 8, P * x:P * x + P], b.at[0:64, 0, :], start=True, stop=False)
                        for q in range(NB):
                            mm = pe.matmul(p[:, 8 * q:8 * q + 8], b.st8[:, q, P * x:P * x + P], b.qe[:, NP + 8 * q:NP + 8 * q + 8],
                                           start=False, stop=(q == NB - 1))
                    s.o_ready.mark(mm)
                    for q in range(NB):
                        mm = pe.matmul(g.ps[:, q // 2, 256 * (q % 2):256 * (q % 2) + 256], b.kt8[:, q, :], b.v[0:NS, 8, :], start=True, stop=True)
                    s.outer.mark(mm)
            s.o_out.next(pe)
            s.state.next(pe)

        @block.scalar
        def _(act):
            for t in range(9):
                s.o_ready.next(act)
                if t < 8:
                    for c in range(2):
                        at = t * P + 64 * c
                        a = act.activation(b.o[:, :, at:at + 64], g.ps[:, 2 + 2 * (t % 2) + c, 0:P].rearrange("p (x t) -> p x t", x=2), ACT.Copy)
                else:
                    a = act.activation(b.o[:, :, NP:TOK], g.ps[:, 4, 0:256].rearrange("p (x t) -> p x t", x=2)[:, :, 0:64], ACT.Copy)
                s.o_out.mark(a)

        @block.vector
        def _(dve):
            dve.memset(b.st[:, 0, :], 0.0)
            for t in range(9):
                R = P if t < 8 else NS
                s.scored.next(dve)
                m = dve.tensor_tensor(b.at[0:R, t % 2, :], g.ps[0:R, 6 + t % 2, 0:64], (g.upto if t < 8 else g.upto8)[0:R, :], ALU.mult)
                if t < 8:
                    m = dve.tensor_copy(b.kt[0:R, t % 2, :], g.ps[0:R, 6 + t % 2, P:2 * P])
                else:
                    m = dve.tensor_tensor(b.kt8[:, :, :], g.ps[0:NS, 6, P:2 * P].unsqueeze(1).to_broadcast([NS, NB, P]),
                                          g.brow[0:NS, :].unsqueeze(2).to_broadcast([NS, NB, P]), ALU.mult)
                s.turned_out.mark(m)
                if t >= 1:
                    s.o_ready.next(dve)
                if t < 8:
                    s.outer.next(dve)
                    for c in range(2):
                        n = 2 * t + c
                        dve.drain()
                        m = dve.scalar_tensor_tensor(b.st[:, (n + 1) % 4, :], b.st[:, n % 4, :], b.dec[:, n:n + 1],
                                                     g.ps[:, c, 0:256], ALU.mult, ALU.add)
                        s.state.mark(m)
                else:
                    s.outer.next(dve)
                    dve.tensor_tensor(b.st8[:, :, :], b.st8[:, :, :], b.dec[:, 16:24].unsqueeze(2).to_broadcast([P, NB, 256]), ALU.mult)
                    dve.drain()
                    s.state.mark(dve.tensor_tensor(b.st8[:, :, :].rearrange("p (a q) t -> p a (q t)", q=2), b.st8[:, :, :].rearrange("p (a q) t -> p a (q t)", q=2),
                                                   g.ps[:, 0:4, :], ALU.add))
            s.o_ready.next(dve)

        @block.sync
        def _(sp):
            s.state.next(sp, 17)
            sp.dma_start(d.gl_p[h], b.st[:, 0, :]).then_inc(stored, 16)
            sp.dma_start(d.gl_s[h], b.st8[:, :, :]).then_inc(stored, 16)
            sp.wait_ge(stored, 64 * h + 32)


def gla_finish(g, d, b, s, h, stored):
    nc = g.nc
    ps3 = lambda first: [(g.ps[:, first + c, 0:n], o, n) for c, (o, n) in enumerate(CH)]
    sq = (b.qe, b.kd)
    with nc.Block() as block:
        @block.sync
        def _(sp):
            for x in range(2):
                s.gated.next(sp)
                sp.dma_start(d.gla_out[:, 2 * h + x, :], b.o[:, x, :]).then_inc(stored, 16)
            sp.wait_ge(stored, 64 * (h + 1))

        @block.tensor
        def _(pe):
            s.squared.next(pe)
            for x in range(2):
                for p, o, n in ps3(0):
                    mm = pe.matmul(p, g.ones, sq[x][:, o:o + n], start=(x == 0), stop=(x == 1))
            s.mean_ready.mark(mm)

        @block.scalar
        def _(act):
            act.activation(sq[0][:, :], b.o[:, 0, :], ACT.Square)
            s.squared.mark(act.activation(sq[1][:, :], b.o[:, 1, :], ACT.Square))
            s.mean_ready.next(act)
            for p, o, n in ps3(0):
                a = act.activation(b.e[:, o:o + n], p, ACT.Sqrt, bias=g.col["eps"], scale=1.0 / 256)
            s.root.mark(a)

        @block.vector
        def _(dve):
            s.root.next(dve)
            dve.reciprocal(b.e[:, :], b.e[:, :])
            dve.drain()
            for x in range(2):
                dve.scalar_tensor_tensor(b.o[:, x, :], b.o[:, x, :], g.col["gn"][:, x:x + 1], b.e[:, :], ALU.mult, ALU.mult)
            dve.drain()
            for x in range(2):
                s.gated.mark(dve.tensor_tensor(b.o[:, x, :], b.o[:, x, :], b.gate[:, x, :], ALU.mult))


def split_buffers(g, ctx, name):
    return [ctx.enter_context(g.nc.sbuf_tensor(name + part, [P, KT, TOK], F32R)) for part in ("_high", "_low")]


def program(nc, d, shapes):
    with ExitStack() as ctx:
        g = allocate(nc, ctx)
        load_inputs(g, d)
        for layer in range(2):
            g.layer = layer
            with ExitStack() as mixer:
                m = allocate_mixer(g, mixer, shapes)
                rmsnorm(m, f"mix{layer}", g.col["mix"][:, KT * layer:KT * layer + KT], (m.act,), d.const)
                if layer == 0:
                    rwkv_mix(m, d)
                    with ExitStack() as nsa:
                        nsa_layer_buffers(m, nsa)
                        nsa_project(m, d)
                        nsa_compress(m, d)
                        sample_buffers(m, nsa)
                        nsa_prompt(m, d)
                        nsa_sample(m, d)
                else:
                    gla_mix(m, d)
                with ExitStack() as out:
                    ah, al = split_buffers(g, out, f"out{layer}")
                    project_out(g, layer, m.act, ah, al, (d.w_out_even, d.w_out_odd)[layer], (d.rwkv_out, d.gla_out)[layer], (4, 0)[layer])
            with ExitStack() as ffn:
                ah, al = split_buffers(g, ffn, f"ffn{layer}")
                rmsnorm(g, f"ffn{layer}", g.col["ffn"][:, KT * layer:KT * layer + KT], (ah, al))
                feed_forward(g, layer, ah, al, d.wg[layer], d.wu[layer], d.wd[layer])
        store_tokens(g, d)


def store_tokens(g, d):
    with g.nc.Block() as block:
        @block.sync
        def _(sp):
            sp.dma_start(d.y, g.resid[:, :, :]).then_inc(g.tokens_moved, 16)
            sp.dma_start(d.win_rows, d.cache_win_rows[:, 8:512, :]).then_inc(g.tokens_moved, 16)
            sp.wait_ge(g.tokens_moved, 64 + 32)


def pack(inp):
    inp = {k: np.asarray(v) for k, v in inp.items()}
    out = {}

    def weight(w, n):
        a, b = w.shape
        return np.ascontiguousarray(w.reshape(a // P, P, b // n, n).transpose(2, 1, 0, 3))

    def column(v):
        return v.reshape(-1, P).T

    x = np.concatenate([inp["x_prompt"].reshape(NP, D), inp["x_sample"].reshape(NS, D)])
    out["x"] = np.ascontiguousarray(x.T.reshape(KT, P, TOK).transpose(1, 0, 2))
    out["const"] = np.concatenate([v.reshape(P, -1) for v in _constants().values()], axis=1)
    w = inp["w_in_even"][0]
    q = w[:, 0:512].reshape(D, 2, 4, HD).transpose(0, 2, 1, 3).reshape(D, 512)
    kv = w[:, 512:1280].reshape(D, 3, 2, P)
    nsa = np.concatenate([q, kv[:, :, 0].reshape(D, 384), kv[:, :, 1].reshape(D, 384), w[:, 1280:1304]], axis=1)
    out["w_nsa"] = np.ascontiguousarray(nsa.reshape(KT, P, NSAW).transpose(1, 0, 2))
    order = np.concatenate([np.arange(1536, 1792)] + [np.arange(P) + 512 * s + P * j for j in range(4) for s in range(3)])
    out["w_rwkv"] = weight(w[:, 1304:][:, order], P)
    out["qk_gain"] = np.concatenate([np.tile(inp["nsa_qnorm"][0], 8), np.tile(inp["nsa_knorm"][0][:, None, :], (1, 2, 1)).reshape(-1)])
    out["cmp_w1"] = np.ascontiguousarray(inp["cmp_w1"][0].reshape(2, 16, P, P).transpose(2, 0, 1, 3))
    out["cmp_w2"] = np.ascontiguousarray(inp["cmp_w2"][0].transpose(1, 0, 2))
    out["cmp_pe"] = np.ascontiguousarray(inp["cmp_pe"][0].reshape(2, 16, P).transpose(2, 0, 1))
    cache = inp["cache_nsa_kv"][0]
    out["cache_cmp"] = np.ascontiguousarray(cache[:, :, 0:2].reshape(80, 64, 2, 2, 2, HD).transpose(0, 2, 5, 3, 4, 1).reshape(80, P, 4, 64))
    out["cache_slc"] = np.ascontiguousarray(np.concatenate([cache[:, :, 2].reshape(80, P, P).transpose(0, 2, 1), cache[:, :, 3].reshape(80, P, P)], axis=2))
    win = inp["cache_nsa_win"][0].reshape(NB, 4, P, 2, P)
    out["cache_win"] = np.ascontiguousarray(np.concatenate([win[:, :, :, 0].transpose(0, 3, 1, 2), win[:, :, :, 1].transpose(0, 2, 1, 3)], axis=3))
    out["cache_win_rows"] = np.ascontiguousarray(inp["cache_nsa_win"][0].reshape(NB, 512, 2 * P))
    out["pages"] = np.ascontiguousarray(inp["page_table"].reshape(1, NB * 8))
    out["shift"] = np.ascontiguousarray(inp["state_rwkv_shift"][0][:, order].reshape(NB, RT, P).transpose(2, 1, 0))
    out["lora"] = np.concatenate([np.concatenate([inp["rwkv_wB"][0], inp["rwkv_aB"][0]]), inp["rwkv_gB"][0]], axis=1)
    out["srwkv"] = np.ascontiguousarray(inp["state_rwkv"][0].reshape(NB, 4, 2, HD, HD).transpose(1, 2, 4, 0, 3).reshape(4, P, NB, HD))
    wo = inp["w_in_odd"][0]
    out["w_gla_qk"] = weight(wo[:, 0:1024], P)
    out["w_gla_v"] = np.ascontiguousarray(wo[:, 1024:2048].reshape(KT, P, 4, 256).transpose(2, 1, 0, 3))
    out["w_gla_gd"] = np.ascontiguousarray(wo[:, 2048:2064].reshape(KT, P, 16).transpose(1, 0, 2))
    out["w_gla_r"] = weight(wo[:, 2064:3088], P)
    out["gate_up"] = inp["gla_gate_up"][0]
    out["sgla"] = np.ascontiguousarray(inp["state_gla"][0].transpose(1, 2, 0, 3))
    out["w_out_even"] = weight(inp["w_out_even"][0], P)
    out["w_out_odd"] = weight(inp["w_out_odd"][0], P)
    out["wg"] = np.stack([weight(inp["ffn_gate"][i], P) for i in range(2)])
    out["wu"] = np.stack([weight(inp["ffn_up"][i], P) for i in range(2)])
    out["wd"] = np.stack([weight(inp["ffn_down"][i], P) for i in range(2)])
    cols = {"mix": inp["norm_mix"], "ffn": inp["norm_ffn"], "mu": inp["rwkv_mu"][0][order], "w0": inp["rwkv_w0"], "a0": inp["rwkv_a0"],
            "kk": inp["rwkv_kk"], "ka": inp["rwkv_ka"], "rk": inp["rwkv_rk"], "lnw": inp["rwkv_ln_w"], "lnb": inp["rwkv_ln_b"],
            "gb": inp["gla_gate_b"], "gn": inp["gla_norm"], "eps": np.full(P, EPS, np.float32), "gneps": np.full(P, GN_EPS, np.float32)}
    out["param"] = np.concatenate([column(cols[n]) for n, _ in PARAMS], axis=1)
    return {k: np.ascontiguousarray(v) for k, v in out.items()}


SCRATCH = {"gate_rows": (NS, 24), "rwkv_out": (P, 4, TOK), "gla_out": (P, KT, TOK)}
OUTS = {"y": (P, KT, TOK), "kv": (TOK, 768), "win_rows": (NB, 504, 2 * P), "last": (P, RT, 9),
        "rw_p": (4, P, HD), "rw_s": (4, P, NB, HD), "gl_p": (4, P, 256), "gl_s": (4, P, NB, 256)}


def kernel(**inputs):
    import concourse.bacc as _bacc
    from concourse.bass_utils import run_bass_kernel_spmd as _run

    nc = _bacc.Bacc("TRN2", target_bir_lowering=False, num_devices=1)
    arrays = pack(inputs)
    d = {n: nc.dram_tensor(f"in_{n}", a.shape, mybir.dt.from_np(a.dtype), kind="ExternalInput").ap() for n, a in arrays.items()}
    d |= {n: nc.dram_tensor(f"out_{n}", s, F32, kind="ExternalOutput").ap() for n, s in OUTS.items()}
    d |= {n: nc.dram_tensor(f"scratch_{n}", s, F32, kind="Internal").ap() for n, s in SCRATCH.items()}
    program(nc, names(**d), {k: v.shape for k, v in _constants().items()})
    r = _run(nc, [{f"in_{n}": a for n, a in arrays.items()}], core_ids=[0]).results[0]
    o = {n: r[f"out_{n}"] for n in OUTS}
    y = o["y"].transpose(2, 1, 0).reshape(TOK, D)
    k, v = o["kv"][:, 0:384].reshape(TOK, 3, 1, 2, HD), o["kv"][:, 384:768].reshape(TOK, 3, 1, 2, HD)
    kv = np.concatenate([k, v], axis=2)
    rows, win = kv[:, 0:2].reshape(TOK, 4, 2, HD), kv[:, 2]
    win_s = np.concatenate([o["win_rows"].reshape(NB, 504, 2, 2, HD), win[NP:].reshape(NB, SS, 2, 2, HD)], axis=1)
    last = o["last"].transpose(2, 1, 0).reshape(9, RT * P)
    order = np.concatenate([np.arange(1536, 1792)] + [np.arange(P) + 512 * s + P * j for j in range(4) for s in range(3)])
    last = last[:, np.argsort(order)]
    rw_p = o["rw_p"].reshape(4, 2, HD, HD).transpose(0, 1, 3, 2).reshape(1, 1, 8, HD, HD)
    rw_s = o["rw_s"].reshape(4, 2, HD, NB, HD).transpose(3, 0, 1, 4, 2).reshape(1, NB, 8, HD, HD)
    out = (y[:NP].reshape(1, NP, D), y[NP:].reshape(NB, SS, D), rows[:NP].reshape(1, 1, NP, 4, 2, HD),
           rows[NP:].reshape(1, NB, SS, 4, 2, HD), win[NP - 512:NP].reshape(1, 1, 512, 2, 2, HD), win_s[None],
           rw_p, rw_s, last[8:9][None], last[0:8][None], o["gl_p"][None, None], o["gl_s"].transpose(2, 0, 1, 3)[None])
    return tuple(np.ascontiguousarray(a) for a in out)
```
